# Optimizing a Trainium2 kernel written in Bass

```python
import jax, jax.numpy as jnp
from jax import lax
import numpy as np

D_MODEL = 1024
BATCH = 1
SEQ = 256
DEPTH = 2

GRID_W = 64
CTX_LEN = 256

RET_HEADS = 4
RET_DK = 128
RET_DV = 128
RET_CHUNK = 128
RET_W = RET_HEADS * RET_DV
MLA_HEADS = 8
MLA_Q_LORA = 384
MLA_KV_LORA = 256
MLA_NOPE = 64
MLA_ROPE = 32
MLA_V = 64
MLA_QK = MLA_NOPE + MLA_ROPE
MLA_W = MLA_HEADS * MLA_V
ATTN_Q_BLOCK = 128
ROPE_THETA = 10000.0
GMLP_GROUPS = 4
GMLP_GROUP_W = 128
GMLP_W = GMLP_GROUPS * GMLP_GROUP_W
GMLP_CHUNK = 128

N_BRANCH = 3

N_EXPERTS = 64
TOP_K = 6
D_EXPERT = 256
D_SHARED = 256
ROUTED_SCALE = 2.5
MOE_BLOCK = 128

EPS = 1e-6

OFF_RET_Q = 0
OFF_RET_K = OFF_RET_Q + RET_HEADS * RET_DK
OFF_RET_V = OFF_RET_K + RET_HEADS * RET_DK
OFF_RET_G = OFF_RET_V + RET_W
OFF_MLA_CQ = OFF_RET_G + RET_W
OFF_MLA_CKV = OFF_MLA_CQ + MLA_Q_LORA
OFF_MLA_KR = OFF_MLA_CKV + MLA_KV_LORA
OFF_GMLP_UV = OFF_MLA_KR + MLA_ROPE
OFF_MERGE = OFF_GMLP_UV + 2 * GMLP_W
N_IN = OFF_MERGE + N_BRANCH * D_MODEL

kernel_name = 'hybrid_retention_mla_gmlp_moe_dit'

def _rmsnorm(x, g):
    x32 = x.astype(jnp.float32)
    y = x32 * lax.rsqrt(jnp.mean(x32 * x32, axis=-1, keepdims=True) + EPS)
    return (y * g.astype(jnp.float32)).astype(x.dtype)

def _layernorm(x, g, b):
    x32 = x.astype(jnp.float32)
    mu = jnp.mean(x32, axis=-1, keepdims=True)
    var = jnp.mean(jnp.square(x32 - mu), axis=-1, keepdims=True)
    y = (x32 - mu) * lax.rsqrt(var + EPS) * g.astype(jnp.float32) + b.astype(jnp.float32)
    return y.astype(x.dtype)

def _heads(t, n):
    B, L, _ = t.shape
    return t.reshape(B, L, n, -1).transpose(0, 2, 1, 3)

def _merge_heads(t):
    B, n, L, d = t.shape
    return t.transpose(0, 2, 1, 3).reshape(B, L, n * d)

def _flip(t):
    return jnp.flip(t, axis=2)

def _axial_rope_tables(L):
    rows = L // GRID_W
    half = MLA_ROPE // 2
    n_freq = half // 2
    inv = ROPE_THETA ** (-2.0 * jnp.arange(n_freq, dtype=jnp.float32) / half)
    ang_r = jnp.arange(rows, dtype=jnp.float32)[:, None, None] * inv
    ang_c = jnp.arange(GRID_W, dtype=jnp.float32)[None, :, None] * inv
    ang_r = jnp.broadcast_to(ang_r, (rows, GRID_W, n_freq)).reshape(L, n_freq)
    ang_c = jnp.broadcast_to(ang_c, (rows, GRID_W, n_freq)).reshape(L, n_freq)
    return (jnp.cos(ang_r), jnp.sin(ang_r), jnp.cos(ang_c), jnp.sin(ang_c))

def _rope_half(x, cos, sin):
    x1, x2 = jnp.split(x, 2, axis=-1)
    return jnp.concatenate([x1 * cos - x2 * sin, x1 * sin + x2 * cos], axis=-1)

def _apply_axial_rope(x, tables):
    cos_r, sin_r, cos_c, sin_c = tables
    xr, xc = jnp.split(x.astype(jnp.float32), 2, axis=-1)
    out = jnp.concatenate([_rope_half(xr, cos_r, sin_r), _rope_half(xc, cos_c, sin_c)], axis=-1)
    return out.astype(x.dtype)

def _retention_dir(q, k, v, log_g, s0, strict):
    B, H, L, dk = q.shape
    dv = v.shape[-1]
    n = L // RET_CHUNK
    qc = q.astype(jnp.float32).reshape(B, H, n, RET_CHUNK, dk)
    kc = k.astype(jnp.float32).reshape(B, H, n, RET_CHUNK, dk)
    vc = v.astype(jnp.float32).reshape(B, H, n, RET_CHUNK, dv)
    pos = jnp.arange(RET_CHUNK, dtype=jnp.float32)
    diff = pos[:, None] - pos[None, :]
    keep = diff > 0 if strict else diff >= 0
    dmat = jnp.where(keep, jnp.exp(log_g[:, None, None] * jnp.maximum(diff, 0.0)), 0.0)
    att = jnp.einsum('bhnid,bhnjd->bhnij', qc, kc) * dmat[None, :, None]
    intra = jnp.einsum('bhnij,bhnjv->bhniv', att, vc)
    k_dec = jnp.exp(log_g[:, None] * (RET_CHUNK - 1 - pos))
    q_dec = jnp.exp(log_g[:, None] * (pos + 1.0))
    chunk_kv = jnp.einsum('bhnjd,hj,bhnjv->nbhdv', kc, k_dec, vc)
    c_dec = jnp.exp(log_g * RET_CHUNK)[None, :, None, None]

    def step(s, kv):
        return s * c_dec + kv, s

    s_fin, s_prev = lax.scan(step, s0, chunk_kv)
    inter = jnp.einsum('bhnid,hi,nbhdv->bhniv', qc, q_dec, s_prev)
    return (intra + inter).reshape(B, H, L, dv), s_fin

def _retention_state(k, v, log_g):
    L = k.shape[2]
    dec = jnp.exp(log_g[:, None] * (L - 1 - jnp.arange(L, dtype=jnp.float32)))
    return jnp.einsum('bhjd,hj,bhjv->bhdv', k.astype(jnp.float32), dec, v.astype(jnp.float32))

def _retention_bidir(q, k, v, lg_f, lg_b, s0_f, s0_b):
    o_f, s_f = _retention_dir(q, k, v, lg_f, s0_f, False)
    o_b, s_b = _retention_dir(_flip(q), _flip(k), _flip(v), lg_b, s0_b, True)
    return o_f + _flip(o_b), s_f, s_b

def _retention_out(o, g, gn_g, gn_b, w_br):
    mu = jnp.mean(o, axis=-1, keepdims=True)
    var = jnp.mean(jnp.square(o - mu), axis=-1, keepdims=True)
    on = _merge_heads((o - mu) * lax.rsqrt(var + EPS))
    y = jax.nn.silu(g.astype(jnp.float32)) * (on * gn_g.astype(jnp.float32) + gn_b.astype(jnp.float32))
    return y.astype(g.dtype) @ w_br

def _mla_kv(ckv, kr, kva_g, w_ukv, kn_g, kr_g, tables):
    B, L, _ = ckv.shape
    kv = _heads(_rmsnorm(ckv, kva_g) @ w_ukv, MLA_HEADS)
    k_nope = _rmsnorm(kv[..., :MLA_NOPE], kn_g)
    v = kv[..., MLA_NOPE:]
    k_rope = _rmsnorm(kr, kr_g)[:, None]
    if tables is not None:
        k_rope = _apply_axial_rope(k_rope, tables)
    k = jnp.concatenate([k_nope, jnp.broadcast_to(k_rope, (B, MLA_HEADS, L, MLA_ROPE))], axis=-1)
    return k, v

def _mla_q(cq, qa_g, w_uq, qn_g, tables):
    q = _rmsnorm(_heads(_rmsnorm(cq, qa_g) @ w_uq, MLA_HEADS), qn_g)
    if tables is not None:
        q = jnp.concatenate([q[..., :MLA_NOPE], _apply_axial_rope(q[..., MLA_NOPE:], tables)], axis=-1)
    return q

def _attend(q, k, v):
    s = jnp.einsum('bhqd,bhkd->bhqk', q, k, preferred_element_type=jnp.float32) * (MLA_QK ** -0.5)
    p = jax.nn.softmax(s, axis=-1).astype(v.dtype)
    return jnp.einsum('bhqk,bhkv->bhqv', p, v)

def _attend_blocks(q, k, v):
    B, H, L, d = q.shape
    nb = L // ATTN_Q_BLOCK
    qb = q.reshape(B, H, nb, ATTN_Q_BLOCK, d).transpose(2, 0, 1, 3, 4)
    ob = lax.map(lambda t: _attend(t, k, v), qb)
    return ob.transpose(1, 2, 0, 3, 4).reshape(B, H, L, -1)

def _gmlp_branch(uv, ln_g, ln_b, ws, bs, w_br):
    z = jax.nn.gelu(uv)
    u, v = jnp.split(z, 2, axis=-1)
    B, L, _ = v.shape
    n = L // GMLP_CHUNK
    vn = _layernorm(v, ln_g, ln_b).reshape(B, n, GMLP_CHUNK, GMLP_GROUPS, GMLP_GROUP_W)
    sv = jnp.einsum('gij,bnjgc->bnigc', ws, vn) + bs.T[None, None, :, :, None]
    return (u * sv.reshape(B, L, GMLP_W)) @ w_br

def _gated_merge(gate_logits, y_a, y_b, y_c, w_out):
    g = jax.nn.sigmoid(gate_logits.astype(jnp.float32))
    y = (g[..., :D_MODEL] * y_a + g[..., D_MODEL:2 * D_MODEL] * y_b + g[..., 2 * D_MODEL:] * y_c)
    return y.astype(y_a.dtype) @ w_out

def _mixer(h, hc, tables, w_in, dec_f, dec_b, gn_g, gn_b, w_br_ret,
           qa_g, w_uq, kva_g, w_ukv, qn_g, kn_g, kr_g, w_br_mla,
           ln_g, ln_b, ws, bs, w_br_gmlp, w_out, ctx_out):
    B = h.shape[0]
    p = h @ w_in
    pc = hc @ w_in if ctx_out else None

    def lat(off, size):
        return p[..., off:off + size]

    def con(off, size):
        if ctx_out:
            return pc[..., off:off + size]
        return hc @ w_in[:, off:off + size]

    lg_f = jax.nn.log_sigmoid(dec_f.astype(jnp.float32))
    lg_b = jax.nn.log_sigmoid(dec_b.astype(jnp.float32))
    qk_w = RET_HEADS * RET_DK
    k_scale = RET_DK ** -0.5

    rk_c = _heads(con(OFF_RET_K, qk_w), RET_HEADS) * k_scale
    rv_c = _heads(con(OFF_RET_V, RET_W), RET_HEADS)
    if ctx_out:
        zero = jnp.zeros((B, RET_HEADS, RET_DK, RET_DV), jnp.float32)
        o_c, s_f, s_b = _retention_bidir(_heads(con(OFF_RET_Q, qk_w), RET_HEADS), rk_c, rv_c,
                                         lg_f, lg_b, zero, zero)
        yr_c = _retention_out(o_c, con(OFF_RET_G, RET_W), gn_g, gn_b, w_br_ret)
    else:
        s_f = _retention_state(rk_c, rv_c, lg_f)
        s_b = _retention_state(_flip(rk_c), _flip(rv_c), lg_b)
    o, _, _ = _retention_bidir(_heads(lat(OFF_RET_Q, qk_w), RET_HEADS),
                               _heads(lat(OFF_RET_K, qk_w), RET_HEADS) * k_scale,
                               _heads(lat(OFF_RET_V, RET_W), RET_HEADS),
                               lg_f, lg_b, s_f, s_b)
    yr = _retention_out(o, lat(OFF_RET_G, RET_W), gn_g, gn_b, w_br_ret)

    k_c, v_c = _mla_kv(con(OFF_MLA_CKV, MLA_KV_LORA), con(OFF_MLA_KR, MLA_ROPE),
                       kva_g, w_ukv, kn_g, kr_g, None)
    k_l, v_l = _mla_kv(lat(OFF_MLA_CKV, MLA_KV_LORA), lat(OFF_MLA_KR, MLA_ROPE),
                       kva_g, w_ukv, kn_g, kr_g, tables)
    q_l = _mla_q(lat(OFF_MLA_CQ, MLA_Q_LORA), qa_g, w_uq, qn_g, tables)
    o_m = _attend_blocks(q_l, jnp.concatenate([k_c, k_l], axis=2), jnp.concatenate([v_c, v_l], axis=2))
    ym = _merge_heads(o_m) @ w_br_mla

    yg = _gmlp_branch(lat(OFF_GMLP_UV, 2 * GMLP_W), ln_g, ln_b, ws, bs, w_br_gmlp)

    y = _gated_merge(lat(OFF_MERGE, N_BRANCH * D_MODEL), yr, ym, yg, w_out)
    if not ctx_out:
        return y, None
    q_c = _mla_q(con(OFF_MLA_CQ, MLA_Q_LORA), qa_g, w_uq, qn_g, None)
    ym_c = _merge_heads(_attend(q_c, k_c, v_c)) @ w_br_mla
    yg_c = _gmlp_branch(con(OFF_GMLP_UV, 2 * GMLP_W), ln_g, ln_b, ws, bs, w_br_gmlp)
    y_c = _gated_merge(con(OFF_MERGE, N_BRANCH * D_MODEL), yr_c, ym_c, yg_c, w_out)
    return y, y_c

def _routed_experts(t, idx, w, wg, wu, wd):
    N, D = t.shape
    A = N * TOP_K
    n_blocks = -(-(A + N_EXPERTS * (MOE_BLOCK - 1)) // MOE_BLOCK)
    n_rows = n_blocks * MOE_BLOCK
    flat_e = idx.reshape(-1)
    order = jnp.argsort(flat_e)
    e_sorted = flat_e[order]
    counts = jnp.zeros((N_EXPERTS,), jnp.int32).at[flat_e].add(1)
    padded = (counts + MOE_BLOCK - 1) // MOE_BLOCK * MOE_BLOCK
    pad_end = jnp.cumsum(padded)
    pad_start = pad_end - padded
    start = jnp.cumsum(counts) - counts
    dest = pad_start[e_sorted] + jnp.arange(A, dtype=jnp.int32) - start[e_sorted]
    row_tok = jnp.zeros((n_rows,), jnp.int32).at[dest].set((order // TOP_K).astype(jnp.int32))
    row_w = jnp.zeros((n_rows,), jnp.float32).at[dest].set(w.reshape(-1)[order])
    blk_e = jnp.minimum(jnp.searchsorted(pad_end, jnp.arange(n_blocks, dtype=jnp.int32) * MOE_BLOCK,
                                         side='right'), N_EXPERTS - 1)

    def step(acc, blk):
        tok_b, w_b, e = blk
        xb = t[tok_b]
        hb = jax.nn.silu(xb @ wg[e]) * (xb @ wu[e])
        yb = (hb @ wd[e]).astype(jnp.float32) * w_b[:, None]
        return acc.at[tok_b].add(yb), None

    acc, _ = lax.scan(step, jnp.zeros((N, D), jnp.float32),
                      (row_tok.reshape(n_blocks, MOE_BLOCK), row_w.reshape(n_blocks, MOE_BLOCK), blk_e))
    return acc.astype(t.dtype)

def _moe(t, router, bias, wg, wu, wd, sg, su, sd):
    scores = jax.nn.sigmoid((t @ router).astype(jnp.float32))
    _, idx = lax.top_k(scores + bias.astype(jnp.float32), TOP_K)
    w = jnp.take_along_axis(scores, idx, axis=-1)
    w = w / jnp.sum(w, axis=-1, keepdims=True) * ROUTED_SCALE
    shared = (jax.nn.silu(t @ sg) * (t @ su)) @ sd
    return _routed_experts(t, idx, w, wg, wu, wd) + shared

def setup_inputs(seed: int = 0) -> dict:
    key = jax.random.key(seed)
    kit = iter(jax.random.split(key, 40))
    f32 = jnp.float32
    D = D_MODEL

    def nrm(shape, scale):
        return jax.random.normal(next(kit), shape, f32) * scale

    def gain(shape):
        return 1.0 + 0.05 * jax.random.normal(next(kit), shape, f32)

    gam = 1.0 - 2.0 ** (-5.0 - jnp.arange(RET_HEADS, dtype=f32))
    decay_logit = jnp.log(gam) - jnp.log1p(-gam)
    x = nrm((BATCH, SEQ, D), 1.0)
    c = nrm((BATCH, D), 1.0)
    ctx = nrm((BATCH, CTX_LEN, D), 1.0)
    c_ctx = nrm((D,), 1.0)
    ada_w = nrm((DEPTH, D, 6 * D), 0.5 * D ** -0.5)
    ada_b = nrm((DEPTH, 6 * D), 0.02)
    norm1_g = gain((DEPTH, D))
    norm2_g = gain((DEPTH, D))
    w_in = nrm((DEPTH, D, N_IN), D ** -0.5)
    ret_decay_fwd = decay_logit + nrm((DEPTH, RET_HEADS), 0.1)
    ret_decay_bwd = decay_logit + nrm((DEPTH, RET_HEADS), 0.1)
    ret_gn_g = gain((DEPTH, RET_W))
    ret_gn_b = nrm((DEPTH, RET_W), 0.02)
    w_br_ret = nrm((DEPTH, RET_W, D), RET_W ** -0.5)
    mla_qa_g = gain((DEPTH, MLA_Q_LORA))
    mla_w_uq = nrm((DEPTH, MLA_Q_LORA, MLA_HEADS * MLA_QK), MLA_Q_LORA ** -0.5)
    mla_kva_g = gain((DEPTH, MLA_KV_LORA))
    mla_w_ukv = nrm((DEPTH, MLA_KV_LORA, MLA_HEADS * (MLA_NOPE + MLA_V)), MLA_KV_LORA ** -0.5)
    mla_qn_g = gain((DEPTH, MLA_QK))
    mla_kn_g = gain((DEPTH, MLA_NOPE))
    mla_kr_g = gain((DEPTH, MLA_ROPE))
    w_br_mla = nrm((DEPTH, MLA_W, D), MLA_W ** -0.5)
    gmlp_ln_g = gain((DEPTH, GMLP_W))
    gmlp_ln_b = nrm((DEPTH, GMLP_W), 0.02)
    gmlp_ws = nrm((DEPTH, GMLP_GROUPS, GMLP_CHUNK, GMLP_CHUNK), GMLP_CHUNK ** -0.5)
    gmlp_bs = gain((DEPTH, GMLP_GROUPS, GMLP_CHUNK))
    w_br_gmlp = nrm((DEPTH, GMLP_W, D), GMLP_W ** -0.5)
    w_out = nrm((DEPTH, D, D), D ** -0.5)
    moe_router = nrm((DEPTH, D, N_EXPERTS), D ** -0.5)
    moe_bias = nrm((DEPTH, N_EXPERTS), 0.01)
    moe_w_gate = nrm((DEPTH, N_EXPERTS, D, D_EXPERT), D ** -0.5)
    moe_w_up = nrm((DEPTH, N_EXPERTS, D, D_EXPERT), D ** -0.5)
    moe_w_down = nrm((DEPTH, N_EXPERTS, D_EXPERT, D), D_EXPERT ** -0.5)
    sh_w_gate = nrm((DEPTH, D, D_SHARED), D ** -0.5)
    sh_w_up = nrm((DEPTH, D, D_SHARED), D ** -0.5)
    sh_w_down = nrm((DEPTH, D_SHARED, D), D_SHARED ** -0.5)
    return {'x': x, 'c': c, 'ctx': ctx, 'c_ctx': c_ctx, 'ada_w': ada_w, 'ada_b': ada_b,
            'norm1_g': norm1_g, 'norm2_g': norm2_g, 'w_in': w_in,
            'ret_decay_fwd': ret_decay_fwd, 'ret_decay_bwd': ret_decay_bwd,
            'ret_gn_g': ret_gn_g, 'ret_gn_b': ret_gn_b, 'w_br_ret': w_br_ret,
            'mla_qa_g': mla_qa_g, 'mla_w_uq': mla_w_uq, 'mla_kva_g': mla_kva_g, 'mla_w_ukv': mla_w_ukv,
            'mla_qn_g': mla_qn_g, 'mla_kn_g': mla_kn_g, 'mla_kr_g': mla_kr_g, 'w_br_mla': w_br_mla,
            'gmlp_ln_g': gmlp_ln_g, 'gmlp_ln_b': gmlp_ln_b, 'gmlp_ws': gmlp_ws, 'gmlp_bs': gmlp_bs,
            'w_br_gmlp': w_br_gmlp, 'w_out': w_out,
            'moe_router': moe_router, 'moe_bias': moe_bias, 'moe_w_gate': moe_w_gate,
            'moe_w_up': moe_w_up, 'moe_w_down': moe_w_down,
            'sh_w_gate': sh_w_gate, 'sh_w_up': sh_w_up, 'sh_w_down': sh_w_down}

def reference(x, c, ctx, c_ctx, ada_w, ada_b, norm1_g, norm2_g, w_in,
              ret_decay_fwd, ret_decay_bwd, ret_gn_g, ret_gn_b, w_br_ret,
              mla_qa_g, mla_w_uq, mla_kva_g, mla_w_ukv, mla_qn_g, mla_kn_g, mla_kr_g, w_br_mla,
              gmlp_ln_g, gmlp_ln_b, gmlp_ws, gmlp_bs, w_br_gmlp, w_out,
              moe_router, moe_bias, moe_w_gate, moe_w_up, moe_w_down,
              sh_w_gate, sh_w_up, sh_w_down):
    B, L, D = x.shape
    tables = _axial_rope_tables(L)
    s_lat = jax.nn.silu(c)
    s_ctx = jax.nn.silu(c_ctx)
    cs = ctx
    for l in range(DEPTH):
        ctx_out = l < DEPTH - 1
        mod = (s_lat @ ada_w[l] + ada_b[l])[:, None, :]
        mod_c = s_ctx @ ada_w[l] + ada_b[l]
        shift_a, scale_a, gate_a, shift_f, scale_f, gate_f = jnp.split(mod, 6, axis=-1)
        shift_ac, scale_ac, gate_ac, shift_fc, scale_fc, gate_fc = jnp.split(mod_c, 6, axis=-1)

        h = _rmsnorm(x, norm1_g[l]) * (1.0 + scale_a) + shift_a
        hc = _rmsnorm(cs, norm1_g[l]) * (1.0 + scale_ac) + shift_ac
        y, y_c = _mixer(h, hc, tables, w_in[l], ret_decay_fwd[l], ret_decay_bwd[l],
                        ret_gn_g[l], ret_gn_b[l], w_br_ret[l],
                        mla_qa_g[l], mla_w_uq[l], mla_kva_g[l], mla_w_ukv[l],
                        mla_qn_g[l], mla_kn_g[l], mla_kr_g[l], w_br_mla[l],
                        gmlp_ln_g[l], gmlp_ln_b[l], gmlp_ws[l], gmlp_bs[l], w_br_gmlp[l],
                        w_out[l], ctx_out)
        x = x + gate_a * y
        h2 = _rmsnorm(x, norm2_g[l]) * (1.0 + scale_f) + shift_f
        moe_args = (moe_router[l], moe_bias[l], moe_w_gate[l], moe_w_up[l], moe_w_down[l],
                    sh_w_gate[l], sh_w_up[l], sh_w_down[l])
        if ctx_out:
            cs = cs + gate_ac * y_c
            h2c = _rmsnorm(cs, norm2_g[l]) * (1.0 + scale_fc) + shift_fc
            n_lat = B * L
            f = _moe(jnp.concatenate([h2.reshape(n_lat, D), h2c.reshape(-1, D)], axis=0), *moe_args)
            x = x + gate_f * f[:n_lat].reshape(B, L, D)
            cs = cs + gate_fc * f[n_lat:].reshape(cs.shape)
        else:
            x = x + gate_f * _moe(h2.reshape(B * L, D), *moe_args).reshape(B, L, D)
    return x


_drawn_inputs = setup_inputs


def setup_inputs(seed=0):
    import zlib

    import numpy as np

    out = dict(_drawn_inputs(seed))
    spreads = {}
    factors = {'mla_qa_g': 3.533,
     'mla_kva_g': 3.994,
     'mla_qn_g': 3.367,
     'mla_kn_g': 3.02,
     'mla_kr_g': 5.849}
    for name, (base, spread) in spreads.items():
        noise = np.random.default_rng([zlib.crc32(name.encode()), seed]).standard_normal(out[name].shape)
        drawn = base * np.exp(spread * noise) if base else spread * noise
        out[name] = __import__('jax').numpy.asarray(drawn.astype(out[name].dtype))
    for name, factor in factors.items():
        out[name] = (out[name] * factor).astype(out[name].dtype)
    return out
```

```python
from contextlib import ExitStack

import numpy as np

import concourse.bass as bass
from concourse import mybir

F32 = mybir.dt.float32
I32 = mybir.dt.int32
ALU = mybir.AluOpType
ACT = mybir.ActivationFunctionType
AX_X = mybir.AxisListType.X

P = 128
D = 1024
KT = D // P
SEQ = 256
CTX = 256
T = SEQ + CTX
TT = T // P
DEPTH = 2
EPS = 1e-6

HEADS_R = 4
RW = HEADS_R * P
HEADS_M = 8
QL, KVL, NOPE, ROPE, VD = 384, 256, 64, 32, 64
QK = NOPE + ROPE
CW = QL + KVL + ROPE
GW = 512
OFF_Q, OFF_K, OFF_V, OFF_G = 0, RW, 2 * RW, 3 * RW
OFF_C = 4 * RW
OFF_U = OFF_C + CW
OFF_GV = OFF_U + GW
OFF_MERGE = OFF_GV + GW
N_EXP, TOPK, FF = 64, 6, 256
ROUTED_SCALE = 2.5

NS = 9
SLOT = 2048
BODY = 3
CAP = [128, 64]
BIG = 8192.0

VEC_ROWS = {"c": 8, "cctx": 8, "ada_b": 48, "n1": 8, "n2": 8, "gng": 4, "gnb": 4, "qag": 3, "kvag": 2}
ROW_BC = {"qn": QK, "kn": NOPE, "kr": ROPE, "lng": GW, "lnb": GW, "bs": GW, "bias": N_EXP, "dec": 8}
CONST_COLS = {"ident": P, "iota1": P, "diff": 384, "tri": P, "tok": 8, "cos": 2 * ROPE, "sin": 2 * ROPE}


def offsets(sizes):
    at, out = 0, {}
    for name, n in sizes.items():
        out[name] = at
        at += n
    return out, at


N_SMALL = len(VEC_ROWS) + len(ROW_BC) + 1
VEC_AT, N_VEC = offsets(VEC_ROWS)
ROW_AT, N_ROW = offsets(ROW_BC)
CONST_AT, N_CONST = offsets(CONST_COLS)


def shape_constants():
    out = np.zeros((P, N_CONST), np.float32)

    def put(name, a):
        out[:, CONST_AT[name]:CONST_AT[name] + CONST_COLS[name]] = a

    p = np.arange(P)
    put("ident", np.eye(P))
    put("iota1", np.broadcast_to(np.arange(P) + 1, (P, P)))
    put("diff", np.arange(384)[None, :] - P - p[:, None])
    put("tri", (p[:, None] < p[None, :]))
    tok = np.arange(TT)[None, :] * P + p[:, None] - BIG
    put("tok", np.concatenate([tok, tok - CTX], 1))
    t = np.arange(SEQ)
    nf = ROPE // 4
    inv = (np.float32(10000.0) ** (np.float32(-2.0) * np.arange(nf, dtype=np.float32) / np.float32(ROPE // 2)))
    row = (t // 64).astype(np.float32)[:, None] * inv.astype(np.float32)
    col = (t % 64).astype(np.float32)[:, None] * inv.astype(np.float32)
    cos = np.concatenate([np.cos(row), np.cos(row), np.cos(col), np.cos(col)], 1)
    sin = np.concatenate([-np.sin(row), np.sin(row), -np.sin(col), np.sin(col)], 1)
    put("cos", cos.reshape(2, P, ROPE).transpose(1, 0, 2).reshape(P, 2 * ROPE))
    put("sin", sin.reshape(2, P, ROPE).transpose(1, 0, 2).reshape(P, 2 * ROPE))
    return out


def main_tiles(l):
    return list(range(TT)) if l < DEPTH - 1 else list(range(CTX // P, TT))


def streams(l):
    return [0, 1] if l < DEPTH - 1 else [1]


def weight_pieces(l):
    out = [("ada", j) for j in range(24)]
    out += [("cA",), ("cB",), ("cC",)]
    out += [("rq", j) for j in range(2)] + [("rk", j) for j in range(2)]
    out += [("rv", j) for j in range(2)] + [("rg", j) for j in range(2)]
    out += [("uqA",), ("uqB",), ("ukv",), ("ws",)]
    out += [("u", j) for j in range(2)] + [("gv", j) for j in range(2)]
    for mp in range(4):
        for br in range(3):
            out += [("gate", mp, br), ("br", mp, br)]
    out += [("wo", j) for j in range(4)]
    out += [("router",), ("sg",), ("su",), ("sd",)]
    return out


def ret_units(l):
    return [(h, s) for h in range(HEADS_R) for s in streams(l)]


def att_units(l):
    return [(t, h) for t in main_tiles(l) for h in range(HEADS_M)]


def psum_jobs():
    out = []
    for tt in range(TT):
        out += [(("x", tt, 0), "act"), (("x", tt, 1), "dve")]
    for l in range(DEPTH):
        mt = main_tiles(l)
        out += [(("vec", l), "dve"), (("ada", l), "dve"), (("ms1", l), "dve")]
        out += [(("c", l, 0, t), "dve") for t in mt]
        out += [(("c", l, j, t), "dve") for j in (1, 2) for t in range(TT)]
        out += [(("q", l, h), "act") for h in range(4)] + [(("k", l, h), "act") for h in range(4)]
        out += [(("v", l, j, t), "dve") for j in range(2) for t in range(TT)]
        out += [(("g", l, h), "act") for h in range(4)]
        ru = ret_units(l)
        for n in range(len(ru) + 2):
            if n < len(ru):
                out += [(("s", l, n, pr), "dve") for pr in range(1 + ru[n][1])]
            if 0 <= n - 1 < len(ru):
                out += [(("o", l, n - 1), "dve")]
            if n >= 2:
                out += [(("ot", l, n - 2), "dve")]
        for t in range(TT + 1):
            if t < TT:
                if t in mt:
                    out += [(("ct", l, t, 0), "act")]
                out += [(("ct", l, t, 1), "act")]
                if t in mt:
                    out += [(("qp", l, t, hf), "dve") for hf in range(2)]
                out += [(("kvp", l, t, hf), "dve") for hf in range(2)]
            if t >= 1:
                if t - 1 in mt:
                    out += [(("qt", l, t - 1, hf), "act") for hf in range(2)]
                out += [(("kt", l, t - 1, hf), "act") for hf in range(2)]
        au = att_units(l)
        for n in range(len(au) + 2):
            if n < len(au):
                out += [(("S", l, n), "act")]
            if 0 <= n - 1 < len(au):
                out += [(("PT", l, n - 1), "dve")]
            if n >= 2:
                out += [(("pv", l, n - 2), "dve")]
                if au[n - 2][1] == HEADS_M - 1:
                    out += [(("omt", l, au[n - 2][0]), "act")]
        out += [(("ws", l), "act")]
        out += [(("u", l, g), "act") for g in range(4)]
        out += [(("gv", l, j, t), "act") for j in range(2) for t in mt]
        out += [(("sv", l, t), "dve") for t in mt]
        for m in range(8):
            mp, mi = divmod(m, 2)
            if mi == 0:
                for br in range(3):
                    for i in range(2):
                        out += [(("gate", l, m + i, br), "act"), (("y", l, m + i, br), "dve")]
        out += [(("out", l, m), "dve") for m in range(8)]
        out += [(("ms2", l), "dve")]
        for t in mt:
            out += [(("h2", l, t, 0), "act"), (("h2", l, t, 1), "dve")]
        out += [(("rt", l), "act")]
        for m in range(2):
            out += [(("sg", l, m), "act")]
        for m in range(2):
            out += [(("su", l, m), "dve")]
        out += [(("sd", l, m), "dve") for m in range(8)]
        out += [(("pos", l), "dve"), (("cnt", l), "dve")]
        for t in mt:
            out += [(("comb", l, t, 0), "dve"), (("comb", l, t, 1), "dve")]
    for t in range(2):
        out += [(("fin", t, 0), "act"), (("fin", t, 1), "dve")]
    return out


def backbone(nc, dram, out):
    jobs = psum_jobs()
    job_at = {k: n for n, (k, _) in enumerate(jobs)}
    assert len(job_at) == len(jobs)
    emptied_before = {"act": [0], "dve": [0]}
    for _, e in jobs:
        for k in emptied_before:
            emptied_before[k].append(emptied_before[k][-1] + (k == e))

    pieces, piece_at, moe_at = [], {}, []
    for l in range(DEPTH):
        for w in weight_pieces(l):
            piece_at[(l,) + w] = len(pieces)
            pieces.append((l,) + w)
        moe_at.append(len(pieces))
        pieces += [(l, kind, e) for e in range(N_EXP) for kind in ("expert_gate", "expert_up", "expert_down")]

    h2_dram = nc.dram_tensor("h2_rows", (T, D), F32, kind="Internal").ap()
    y_dram = nc.dram_tensor("expert_rows", (TOPK * T, D), F32, kind="Internal").ap()

    with ExitStack() as ctx:
        def sb(name, shape, dt=F32):
            return ctx.enter_context(nc.sbuf_tensor(name, shape, dt))

        def sem(name):
            return ctx.enter_context(nc.semaphore(name))

        ring = sb("ring", [P, NS, SLOT])
        xT = sb("xT", [P, KT, T])
        hT = sb("hT", [P, KT, T])
        const = sb("const", [P, N_CONST])
        ones = sb("ones", [P, P])
        vec_rows = sb("vec_rows", [P, P])
        vec = sb("vec", [P, N_VEC])
        row_bc = sb("row_bc", [P, N_ROW])
        silu_c = sb("silu_c", [P, KT, 2])
        mod = sb("mod", [P, 48, 2])
        gain1 = sb("gain1", [P, KT, 2])
        gain2 = sb("gain2", [P, KT, 2])
        half_gate = sb("half_gate", [P, KT, 2])
        lg = sb("lg", [P, 64])
        stat = sb("stat", [P, 256])
        eps_col = sb("eps_col", [P, 3])
        idx = sb("idx", [P, 3, 2], I32)
        wrow = sb("wrow", [P, 3])
        maxcnt = sb("maxcnt", [P, 2], I32)
        AREA = 22016
        area = sb("area", [P, AREA])
        bank = [ctx.enter_context(nc.psum_tensor(f"bank{i}", [P, 512], F32)) for i in range(8)]

        def region(at, *dims):
            n = int(np.prod(dims))
            assert at + n <= AREA, (at, n)
            v = area[:, at:at + n]
            if len(dims) == 2:
                return v.rearrange("p (a b) -> p a b", a=dims[0])
            if len(dims) == 3:
                return v.rearrange("p (a b c) -> p a b c", a=dims[0], b=dims[1])
            return v

        def const_cols(name):
            return const[:, CONST_AT[name]:CONST_AT[name] + CONST_COLS[name]]

        def vcol(name, i):
            at = VEC_AT[name] + i
            return vec[:, at:at + 1]

        def rows(name):
            return row_bc[:, ROW_AT[name]:ROW_AT[name] + ROW_BC[name]]

        ident = const_cols("ident")
        y_ret = region(0, 4, T)
        y_mla = region(2048, 4, T)
        BASE = 4096
        decay = region(BASE, 2, 4, 384)
        rqT = region(BASE + 3072, 4, T)
        rkT = region(BASE + 5120, 4, T)
        rv = region(BASE + 7168, TT, RW)
        att = region(BASE + 9216, 2, 4, 256)
        on = region(BASE + 11264, 2, 256)
        tmp_ret = region(BASE + 11776, 2, 256)
        decay_b = region(BASE + 9216, 4, 384)
        lat_c = region(BASE + 12288, TT, CW)
        qT = region(BASE, HEADS_M, T)
        kT = region(BASE + 4096, HEADS_M, T)
        mv = region(BASE + 8192, TT, HEADS_M * VD)
        q_tok = region(BASE + 10240, HEADS_M, QK)
        k_tok = region(BASE + 11008, HEADS_M, QK)
        sq_tok = region(BASE + 14976, 2, 512)
        cqT = region(BASE + 16000, 3, P)
        ckT = region(BASE + 16384, 2, P)
        rope_t = region(BASE + 16640, HEADS_M, ROPE)
        rope_u = region(BASE + 16896, HEADS_M, ROPE)
        probs = region(BASE + 12288, 2, 512)
        probsT = region(BASE + 13312, 2, 512)
        o_tok = region(BASE + 14336, 512)
        y_gmlp = region(BASE, 4, T)
        rstd = region(BASE + 11264, T)
        gv = region(BASE + 2048, TT, GW)
        wsT = region(BASE + 10240, 4, P)
        sv_tmp = region(BASE + 10752, 2, 512)
        merged = region(BASE + 4096, KT, T)
        gate_t = region(BASE + 11776, 2, 512)
        prod_t = region(BASE + 12800, 512)
        ws_t = region(BASE + 13312, 512)
        x_in = region(0, TT, D)
        sq_x = region(BASE + 8192, 2, T)
        x_rows = region(0, 3, D)
        x_rowsT = region(3072, 3, KT * P)
        y_rows = region(6144, 3, D)
        pick = region(9216, 3, TT * P)
        act_g = region(10752, 3, FF)
        hid = region(11520, 3, FF)
        hidT = region(12288, 3, 2 * P)
        pos1 = region(13056, TT, N_EXP + 2)
        table = area[:, 13320:13320 + TT * (N_EXP + 2) * 3].rearrange("p (t e c) -> p t e c", t=TT, c=3)
        R0 = 14112
        score = region(R0, TT, N_EXP)
        sel = region(R0 + 256, TT, N_EXP)
        mask = region(R0 + 512, TT, N_EXP)
        eq = region(R0 + 768, TT, N_EXP)
        cum = region(R0 + 1024, TT, N_EXP)
        top8 = region(R0 + 1280, TT, 8)
        need = region(R0 + 1312, TT)
        wsum = region(R0 + 1316, TT)
        kslot = region(R0 + 1344, TT, N_EXP)
        one64 = region(R0 + 1600, N_EXP)
        h2_tok = region(R0 + 1664, 2, D)
        shT = region(R0 + 3712, 2, T)
        sil_s = region(R0 + 4736, 2, T)
        late_w = region(R0, 3, SLOT)
        y_parts = region(0, 2, TOPK * D)
        fin = region(0, 2, D)

        piece_loaded = [sem(f"piece_loaded{s}") for s in range(NS)]
        ada_used = sem("ada_used")
        bank_full = sem("bank_full")
        emptied = {"act": sem("emptied_by_act"), "dve": sem("emptied_by_dve")}
        const_in = sem("const_in")
        x_loaded = sem("x_loaded")
        small_loaded = sem("small_loaded")
        small_used = sem("small_used")
        ones_ready = sem("ones_ready")
        pe_passed = sem("pe_passed")
        pool_passed = sem("pool_passed")
        root_asked = sem("root_asked")
        roots = sem("roots")
        late_iota = [sem(f"late_iota{l}") for l in range(DEPTH)]
        act_step = sem("act_step")
        dve_step = sem("dve_step")
        silu_ready = sem("silu_ready")
        mod_ready = sem("mod_ready")
        sq_ready = sem("sq_ready")
        gained = sem("gained")
        h_ready = sem("h_ready")
        sq_used = sem("sq_used")
        y_gmlp_ready = sem("y_gmlp_ready")
        decay_arg = sem("decay_arg")
        decay_ready = sem("decay_ready")
        lg_exp = sem("lg_exp")
        lg_arg = sem("lg_arg")
        c_squared = sem("c_squared")
        c_normed = sem("c_normed")
        qk_squared = sem("qk_squared")
        v_copied = sem("v_copied")
        on_ready = sem("on_ready")
        qk_tok_ready = sem("qk_tok_ready")
        neg_max = sem("neg_max")
        gv_normed = sem("gv_normed")
        merged_ready = sem("merged_ready")
        h2_stored = [sem(f"h2_stored{j}") for j in range(2)]
        moe_ready = sem("moe_ready")
        mask_ready = sem("mask_ready")
        sh_ready = sem("sh_ready")
        pick_ready = sem("pick_ready")
        list_full = sem("list_full")
        list_read = sem("list_read")
        rows_in = [sem(f"rows_in{j}") for j in range(3)]
        rows_turned = sem("rows_turned")
        turned_act = sem("turned_act")
        turned_dve = sem("turned_dve")
        gu_full = sem("gu_full")
        silu_done = sem("silu_done")
        hid_ready = sem("hid_ready")
        hidT_full = sem("hidT_full")
        hidT_ready = sem("hidT_ready")
        down_full = sem("down_full")
        y_act = sem("y_act")
        y_dve = sem("y_dve")
        rows_out = [sem(f"rows_out{j}") for j in range(3)]
        y_in = [sem(f"y_in{j}") for j in range(2)]
        y_summed = sem("y_summed")
        late_loaded = [sem(f"late_loaded{l}") for l in range(DEPTH)]
        late_in = [sem(f"late_in{l}") for l in range(DEPTH)]
        late_out = [sem(f"late_out{l}") for l in range(DEPTH)]
        late_pe = [sem(f"late_pe{l}") for l in range(DEPTH)]
        late_dve = [sem(f"late_dve{l}") for l in range(DEPTH)]
        late_act = [sem(f"late_act{l}") for l in range(DEPTH)]
        out_ready = sem("out_ready")
        stored = sem("stored")

        block = ctx.enter_context(nc.Block())

        def await_loaded(eng, p):
            eng.wait_ge(piece_loaded[p % NS], 16 * (p // NS + 1))

        def await_full(eng, key):
            eng.wait_ge(bank_full, job_at[key] + 1)
            return bank[job_at[key] % 8]

        def await_emptied(eng, key):
            n = job_at[key]
            e = jobs[n][1]
            eng.wait_ge(emptied[e], emptied_before[e][n + 1])

        def open_bank(pe, key):
            n = job_at[key]
            if n >= 8:
                await_emptied(pe, jobs[n - 8][0])
            return bank[n % 8]

        def norm_at(key):
            return 2 * key[1] + (key[0] == "ms2")

        def c0(l):
            return 0 if l < DEPTH - 1 else CTX

        def tokens(l):
            return P * len(main_tiles(l))

        def before(l, per_layer):
            return sum(per_layer(i) for i in range(l))

        def h2_base(l, buf):
            return before(l, lambda i: (len(main_tiles(i)) + 1 - buf) // 2)

        def span(l, s, t0=0):
            return slice(CTX * s - t0, CTX * s + CTX - t0)

        experts = BODY * (N_EXP // BODY)
        LISTS, PICKS = N_EXP + 1, N_EXP + 2
        lists_of = [len(range(j, LISTS, 3)) for j in range(3)]
        experts_of = [len(range(j, N_EXP, 3)) for j in range(3)]

        def slot_of(p):
            return ring[:, p % NS, :]

        def piece_view(p, a, b):
            return ring[:, p % NS, 0:a * b].rearrange("p (a b) -> p a b", a=a)

        def src_and_dst(p):
            l, kind, *r = pieces[p]
            w_in = dram["w_in"][l].rearrange("(k p) n -> p k n", p=P)

            def cols(at, n):
                return w_in[:, :, at:at + n], piece_view(p, KT, n)

            if kind == "ada":
                return dram["ada_w"][l].rearrange("(k p) n -> p k n", p=P)[:, :, 256 * r[0]:256 * r[0] + 256], piece_view(p, KT, 256)
            if kind == "cA":
                return cols(OFF_C, 256)
            if kind == "cB":
                return cols(OFF_C + 256, 256)
            if kind == "cC":
                return cols(OFF_C + 512, CW - 512)
            if kind in ("rq", "rk", "rv", "rg", "u", "gv"):
                at = {"rq": OFF_Q, "rk": OFF_K, "rv": OFF_V, "rg": OFF_G, "u": OFF_U, "gv": OFF_GV}[kind]
                return cols(at + 256 * r[0], 256)
            if kind == "uqA":
                return dram["mla_w_uq"][l, 0:256].rearrange("(k p) n -> p k n", p=P), piece_view(p, 2, HEADS_M * QK)
            if kind == "uqB":
                return dram["mla_w_uq"][l, 256:384], slot_of(p)[:, 0:HEADS_M * QK]
            if kind == "ukv":
                return dram["mla_w_ukv"][l].rearrange("(k p) n -> p k n", p=P), piece_view(p, 2, D)
            if kind == "ws":
                return dram["gmlp_ws"][l].rearrange("g i j -> i g j"), piece_view(p, 4, P)
            if kind == "gate":
                return cols(OFF_MERGE + D * r[1] + 256 * r[0], 256)
            if kind == "br":
                w = dram[("w_br_ret", "w_br_mla", "w_br_gmlp")[r[1]]][l]
                return w.rearrange("(k p) n -> p k n", p=P)[:, :, 256 * r[0]:256 * r[0] + 256], piece_view(p, 4, 256)
            if kind == "wo":
                return dram["w_out"][l].rearrange("(k p) n -> p k n", p=P)[:, :, 256 * r[0]:256 * r[0] + 256], piece_view(p, KT, 256)
            if kind == "router":
                return dram["moe_router"][l].rearrange("(k p) n -> p k n", p=P), piece_view(p, KT, N_EXP)
            if kind in ("sg", "su"):
                return dram["sh_w_gate" if kind == "sg" else "sh_w_up"][l].rearrange("(k p) n -> p k n", p=P), piece_view(p, KT, FF)
            assert kind == "sd"
            return dram["sh_w_down"][l].rearrange("(k p) n -> p k n", p=P), piece_view(p, 2, D)

        def last_job(l, kind, r):
            last = TT - 1
            if kind == "ada":
                return ("ada", l)
            if kind in ("cA", "cB", "cC"):
                return ("c", l, ("cA", "cB", "cC").index(kind), last)
            if kind in ("rq", "rk", "rg"):
                return (kind[1], l, 2 * r[0] + 1)
            if kind in ("rv", "gv"):
                return ("v" if kind == "rv" else "gv", l, r[0], last)
            if kind in ("uqA", "uqB", "ukv"):
                return ("kvp" if kind == "ukv" else "qp", l, last, 1)
            if kind in ("ws", "router"):
                return ({"ws": "ws", "router": "rt"}[kind], l)
            if kind == "u":
                return ("u", l, 2 * r[0] + 1)
            if kind in ("gate", "br"):
                return ("gate" if kind == "gate" else "y", l, 2 * r[0] + 1, r[1])
            if kind == "wo":
                return ("out", l, 2 * r[0] + 1)
            return (kind, l, 7 if kind == "sd" else 1)

        def expert_src(l, kind, e):
            name = ("moe_w_gate", "moe_w_up", "moe_w_down")[kind]
            w = dram[name][l, e] if isinstance(e, int) else dram[name][l, bass.ds(e, 1)].rearrange("o a b -> (o a) b")
            return w.rearrange("(p k) n -> p (k n)", p=P)

        @block.sync
        def _(sp):
            def await_free(p):
                l, kind, *r = pieces[p]
                if kind == "ada" and r[0] < 23:
                    sp.wait_ge(ada_used, 23 * l + r[0] + 1)
                elif kind in ("expert_gate", "expert_up"):
                    sp.wait_ge(gu_full, N_EXP * l + r[0] + 1)
                elif kind == "expert_down":
                    sp.wait_ge(down_full, N_EXP * l + r[0] + 1)
                else:
                    sp.wait_ge(bank_full, job_at[last_job(l, kind, r)] + 1)

            def load_expert(l, e, j, i):
                for kind in range(3):
                    p = moe_at[l] + 3 * j + kind
                    sp.wait_ge(down_full if kind == 2 else gu_full, N_EXP * l + e - BODY + 1)
                    sp.dma_start(slot_of(p), expert_src(l, kind, e)).then_inc(piece_loaded[p % NS], 16)

            for l in range(DEPTH):
                for p in range(piece_at[(l, "ada", 0)], moe_at[l] + 3 * BODY):
                    if p >= NS:
                        await_free(p - NS)
                    if p < moe_at[l]:
                        src, dst = src_and_dst(p)
                    else:
                        e, kind = divmod(p - moe_at[l], 3)
                        src, dst = expert_src(l, kind, e), slot_of(p)
                    sp.dma_start(dst, src).then_inc(piece_loaded[p % NS], 16)
                with sp.Fori(1, N_EXP // BODY) as i:
                    for j in range(BODY):
                        load_expert(l, i * BODY + j, j, i)
                load_expert(l, experts, 0, N_EXP // BODY)

                sp.wait_ge(moe_ready, l + 1)
                await_emptied(sp, ("sd", l, 7))
                sp.wait_ge(h2_stored[0], 16 * h2_base(l + 1, 0))
                sp.wait_ge(h2_stored[1], 16 * h2_base(l + 1, 1))
                most = sp.value_load(maxcnt[0:1, l:l + 1], min_val=0, max_val=T)
                with sp.If(most > CAP[l]):
                    for b in range(1, tokens(l) // CAP[l]):
                        with sp.Fori(0, N_EXP) as e:
                            q = (b - 1) * N_EXP + e
                            sp.wait_ge(late_dve[l], 6 * q + 1)
                            for kind in range(3):
                                sp.dma_start(late_w[:, kind, :], expert_src(l, kind, e)).then_inc(late_loaded[l], 16)

        @block.tensor
        def _(pe):
            mm = nc.tensor.matmul

            def turn(dst, src, n=P):
                return nc.tensor.transpose(dst, src, ident[0:n, 0:n])

            pe.wait_ge(const_in, 16)
            pe.wait_ge(x_loaded, 32)
            pe.wait_ge(ones_ready, 1)
            for tt in range(TT):
                for hf in range(2):
                    b = open_bank(pe, ("x", tt, hf))
                    for k in range(4):
                        last = turn(b[:, P * k:P * k + P], x_in[:, tt, P * (4 * hf + k):P * (4 * hf + k) + P])
                    last.then_inc(bank_full, 1)

            def feature_job(key, lhs, rhs, c, n, used=0):
                b = open_bank(pe, key)
                K = lhs.shape[1]
                for k in range(K):
                    last = mm(b[:, 0:n], lhs[:, k, :], rhs[:, k, c:c + n], start=(k == 0), stop=(k == K - 1))
                last.then_inc(bank_full, 1)
                return last

            def token_job(key, lhs, tt, rhs, n):
                b = open_bank(pe, key)
                K = rhs.shape[1]
                for k in range(K):
                    last = mm(b[:, 0:n], lhs[:, k, P * tt:P * tt + P], rhs[:, k, :], start=(k == 0), stop=(k == K - 1))
                last.then_inc(bank_full, 1)

            def mean_square(key, c, n):
                b = open_bank(pe, key)
                for k in range(KT):
                    pe.wait_ge(sq_ready, KT * norm_at(key) + k + 1)
                    last = mm(b[:, 0:n], ones[:, :], sq_x[:, k % 2, 0:n], start=(k == 0), stop=(k == KT - 1))
                    if k < KT - 1:
                        last.then_inc(sq_used, 1)
                last.then_inc(bank_full, 1)

            for l in range(DEPTH):
                mt, t0 = main_tiles(l), c0(l)
                nt = T - t0
                pe.wait_ge(small_loaded, 16 * N_SMALL * (l + 1))
                b = open_bank(pe, ("vec", l))
                turn(b[:, 0:N_VEC], vec_rows[0:N_VEC, :], N_VEC).then_inc(bank_full, 1)
                pe.wait_ge(silu_ready, l + 1)
                b = open_bank(pe, ("ada", l))
                for j in range(24):
                    p = piece_at[(l, "ada", j)]
                    await_loaded(pe, p)
                    w = piece_view(p, KT, 256)
                    for i in range(2):
                        for k in range(KT):
                            last = mm(b[:, 4 * j + 2 * i:4 * j + 2 * i + 2], w[:, k, P * i:P * i + P], silu_c[:, k, :],
                                      start=(k == 0), stop=(k == KT - 1))
                    if j < 23:
                        last.then_inc(ada_used, 1)
                last.then_inc(bank_full, 1)
                mean_square(("ms1", l), 0, T)
                pe.wait_ge(h_ready, 2 * l + 1)
                for j, name in enumerate(("cA", "cB", "cC")):
                    p = piece_at[(l, name)]
                    await_loaded(pe, p)
                    n = 256 if j < 2 else CW - 512
                    w = piece_view(p, KT, n)
                    for t in (mt if j == 0 else range(TT)):
                        token_job(("c", l, j, t), hT, t, w, n)
                for name, full in (("q", False), ("k", True)):
                    for j in range(2):
                        p = piece_at[(l, "r" + name, j)]
                        await_loaded(pe, p)
                        w = piece_view(p, KT, 256)
                        for i in range(2):
                            feature_job((name, l, 2 * j + i), w[:, :, P * i:P * i + P], hT, 0 if full else t0, T if full else nt)
                for j in range(2):
                    p = piece_at[(l, "rv", j)]
                    await_loaded(pe, p)
                    for t in range(TT):
                        token_job(("v", l, j, t), hT, t, piece_view(p, KT, 256), 256)
                for j in range(2):
                    p = piece_at[(l, "rg", j)]
                    await_loaded(pe, p)
                    w = piece_view(p, KT, 256)
                    for i in range(2):
                        feature_job(("g", l, 2 * j + i), w[:, :, P * i:P * i + P], hT, t0, nt)
                ru = ret_units(l)
                for n in range(len(ru) + 2):
                    if n < len(ru):
                        h, s = ru[n]
                        if n == 0:
                            await_emptied(pe, ("q", l, 3))
                            await_emptied(pe, ("k", l, 3))
                        for pr in range(1 + s):
                            b = open_bank(pe, ("s", l, n, pr))
                            for i in range(2):
                                j = 2 * pr + i
                                last = mm(b[:, 256 * i:256 * i + 256], rkT[:, h, P * j:P * j + P],
                                          rqT[:, h, 256 * s:256 * s + 256], start=True, stop=True)
                            last.then_inc(bank_full, 1)
                    if 0 <= n - 1 < len(ru):
                        h, s = ru[n - 1]
                        b = open_bank(pe, ("o", l, n - 1))
                        await_emptied(pe, ("s", l, n - 1, s))
                        if n == 1:
                            await_emptied(pe, ("v", l, 1, TT - 1))
                        for i in range(2):
                            nj = 2 + 2 * s
                            for j in range(nj):
                                last = mm(b[:, P * i:P * i + P], att[:, (n - 1) % 2, j, P * i:P * i + P],
                                          rv[:, j, P * h:P * h + P], start=(j == 0), stop=(j == nj - 1))
                        last.then_inc(bank_full, 1)
                    if n >= 2:
                        b = open_bank(pe, ("ot", l, n - 2))
                        pe.wait_ge(on_ready, before(l, lambda i: len(ret_units(i))) + n - 1)
                        for i in range(2):
                            last = turn(b[:, P * i:P * i + P], on[:, (n - 2) % 2, P * i:P * i + P])
                        last.then_inc(bank_full, 1)
                pa, pb_, pk = piece_at[(l, "uqA")], piece_at[(l, "uqB")], piece_at[(l, "ukv")]
                for p in (pa, pb_, pk):
                    await_loaded(pe, p)
                wa, wb, wk = piece_view(pa, 2, 768), slot_of(pb_), piece_view(pk, 2, D)
                for t in range(TT + 1):
                    if t < TT:
                        pe.wait_ge(c_normed, TT * l + t + 1)
                        if t in mt:
                            b = open_bank(pe, ("ct", l, t, 0))
                            for k in range(3):
                                last = turn(b[:, P * k:P * k + P], lat_c[:, t, P * k:P * k + P])
                            last.then_inc(bank_full, 1)
                        b = open_bank(pe, ("ct", l, t, 1))
                        for k in range(2):
                            last = turn(b[:, P * k:P * k + P], lat_c[:, t, QL + P * k:QL + P * k + P])
                        last.then_inc(bank_full, 1)
                        if t in mt:
                            await_emptied(pe, ("ct", l, t, 0))
                            for hf in range(2):
                                b = open_bank(pe, ("qp", l, t, hf))
                                for k in range(3):
                                    w = wa[:, k, 384 * hf:384 * hf + 384] if k < 2 else wb[:, 384 * hf:384 * hf + 384]
                                    last = mm(b[:, 0:384], cqT[:, k, :], w, start=(k == 0), stop=(k == 2))
                                last.then_inc(bank_full, 1)
                        await_emptied(pe, ("ct", l, t, 1))
                        for hf in range(2):
                            b = open_bank(pe, ("kvp", l, t, hf))
                            for k in range(2):
                                last = mm(b[:, :], ckT[:, k, :], wk[:, k, 512 * hf:512 * hf + 512], start=(k == 0), stop=(k == 1))
                            last.then_inc(bank_full, 1)
                    if t >= 1:
                        pe.wait_ge(qk_tok_ready, TT * l + t)
                        for name, src in (("qt", q_tok), ("kt", k_tok)):
                            if name == "qt" and t - 1 not in mt:
                                continue
                            for hf in range(2):
                                b = open_bank(pe, (name, l, t - 1, hf))
                                for i in range(4):
                                    last = turn(b[0:QK, P * i:P * i + P], src[:, 4 * hf + i, :])
                                last.then_inc(bank_full, 1)
                au = att_units(l)
                for n in range(len(au) + 2):
                    if n < len(au):
                        t, h = au[n]
                        nk = T if t >= 2 else CTX
                        if n == 0:
                            await_emptied(pe, ("kt", l, TT - 1, 1))
                        b = open_bank(pe, ("S", l, n))
                        mm(b[:, 0:nk], qT[0:QK, h, P * t:P * t + P], kT[0:QK, h, 0:nk], start=True, stop=True).then_inc(bank_full, 1)
                    if 0 <= n - 1 < len(au):
                        t, h = au[n - 1]
                        nk = T if t >= 2 else CTX
                        b = open_bank(pe, ("PT", l, n - 1))
                        await_emptied(pe, ("S", l, n - 1))
                        for j in range(nk // P):
                            last = turn(b[:, P * j:P * j + P], probs[:, (n - 1) % 2, P * j:P * j + P])
                        last.then_inc(bank_full, 1)
                    if n >= 2:
                        t, h = au[n - 2]
                        nk = T if t >= 2 else CTX
                        b = open_bank(pe, ("pv", l, n - 2))
                        await_emptied(pe, ("PT", l, n - 2))
                        for j in range(nk // P):
                            last = mm(b[:, 0:VD], probsT[:, (n - 2) % 2, P * j:P * j + P], mv[:, j, VD * h:VD * h + VD],
                                      start=(j == 0), stop=(j == nk // P - 1))
                        last.then_inc(bank_full, 1)
                        if h == HEADS_M - 1:
                            b = open_bank(pe, ("omt", l, t))
                            await_emptied(pe, ("pv", l, n - 2))
                            for k in range(4):
                                last = turn(b[:, P * k:P * k + P], o_tok[:, P * k:P * k + P])
                            last.then_inc(bank_full, 1)
                p = piece_at[(l, "ws")]
                await_loaded(pe, p)
                b = open_bank(pe, ("ws", l))
                for g in range(4):
                    last = turn(b[:, P * g:P * g + P], piece_view(p, 4, P)[:, g, :])
                last.then_inc(bank_full, 1)
                for j in range(2):
                    p = piece_at[(l, "u", j)]
                    await_loaded(pe, p)
                    w = piece_view(p, KT, 256)
                    for i in range(2):
                        feature_job(("u", l, 2 * j + i), w[:, :, P * i:P * i + P], hT, t0, nt)
                for j in range(2):
                    p = piece_at[(l, "gv", j)]
                    await_loaded(pe, p)
                    for t in mt:
                        token_job(("gv", l, j, t), hT, t, piece_view(p, KT, 256), 256)
                await_emptied(pe, ("ws", l))
                for i, t in enumerate(mt):
                    b = open_bank(pe, ("sv", l, t))
                    pe.wait_ge(gv_normed, before(l, lambda i: len(main_tiles(i))) + i + 1)
                    for g in range(4):
                        last = mm(b[:, P * g:P * g + P], gv[:, t, P * g:P * g + P], wsT[:, g, :], start=True, stop=True)
                    last.then_inc(bank_full, 1)
                ys = (y_ret, y_mla, y_gmlp)
                await_emptied(pe, ("ot", l, len(ru) - 1))
                await_emptied(pe, ("omt", l, TT - 1))
                for mp in range(4):
                    for br in range(3):
                        pg, pw = piece_at[(l, "gate", mp, br)], piece_at[(l, "br", mp, br)]
                        await_loaded(pe, pg)
                        await_loaded(pe, pw)
                        if br == 2 and mp == 0:
                            pe.wait_ge(y_gmlp_ready, before(l, lambda i: len(main_tiles(i))) + len(mt))
                        for i in range(2):
                            feature_job(("gate", l, 2 * mp + i, br), piece_view(pg, KT, 256)[:, :, P * i:P * i + P], hT, t0, nt)
                            feature_job(("y", l, 2 * mp + i, br), piece_view(pw, 4, 256)[:, :, P * i:P * i + P], ys[br], t0, nt)
                pe.wait_ge(merged_ready, 8 * (l + 1))
                for j in range(4):
                    p = piece_at[(l, "wo", j)]
                    await_loaded(pe, p)
                    for i in range(2):
                        feature_job(("out", l, 2 * j + i), piece_view(p, KT, 256)[:, :, P * i:P * i + P], merged, 0, nt)
                mean_square(("ms2", l), t0, nt)
                pe.wait_ge(h_ready, 2 * l + 2)
                for t in mt:
                    for hf in range(2):
                        b = open_bank(pe, ("h2", l, t, hf))
                        for k in range(4):
                            last = turn(b[:, P * k:P * k + P], hT[:, 4 * hf + k, P * t:P * t + P])
                        last.then_inc(bank_full, 1)
                p = piece_at[(l, "router")]
                await_loaded(pe, p)
                b = open_bank(pe, ("rt", l))
                for i, t in enumerate(mt):
                    for k in range(KT):
                        last = mm(b[:, N_EXP * i:N_EXP * i + N_EXP], hT[:, k, P * t:P * t + P], piece_view(p, KT, N_EXP)[:, k, :],
                                  start=(k == 0), stop=(k == KT - 1))
                last.then_inc(bank_full, 1)
                for name in ("sg", "su"):
                    p = piece_at[(l, name)]
                    await_loaded(pe, p)
                    for m in range(2):
                        feature_job((name, l, m), piece_view(p, KT, FF)[:, :, P * m:P * m + P], hT, t0, nt)
                p = piece_at[(l, "sd")]
                await_loaded(pe, p)
                pe.wait_ge(sh_ready, 2 * (l + 1))
                for m in range(8):
                    feature_job(("sd", l, m), piece_view(p, 2, D)[:, :, P * m:P * m + P], shT[:, :, t0:T], 0, nt)
                pe.wait_ge(mask_ready, l + 1)
                b = open_bank(pe, ("pos", l))
                for i in range(len(mt)):
                    for j in range(i + 1):
                        last = mm(b[:, N_EXP * i:N_EXP * i + N_EXP], const_cols("tri") if j == i else ones[:, :], mask[:, j, :],
                                  start=(j == 0), stop=(j == i))
                last.then_inc(bank_full, 1)
                b = open_bank(pe, ("cnt", l))
                for j in range(len(mt)):
                    last = mm(b[:, 0:N_EXP], ones[:, :], mask[:, j, :], start=(j == 0), stop=(j == len(mt) - 1))
                last.then_inc(bank_full, 1)
                await_emptied(pe, ("cnt", l))
                await_emptied(pe, ("rt", l))
                await_emptied(pe, ("sg", l, 1))
                pe.wait_ge(moe_ready, l + 1)

                cap, nm = CAP[l], len(mt)

                def make_list(e, j):
                    pe.wait_ge(pick_ready, l * PICKS + e + 1)
                    pe.wait_ge(list_read, l * LISTS + e)
                    for i in range(nm):
                        last = mm(bank[7][0:cap, 256:259], pick[:, j, P * i:P * i + cap], entry(i, e), start=(i == 0), stop=(i == nm - 1))
                    last.then_inc(list_full, 1)

                def turn_rows(j, i):
                    pe.wait_ge(rows_in[j], 16 * (l * lists_of[j] + 1) + 16 * i)
                    pe.sem_inc(pe_passed, 1)
                    for k in range(KT):
                        last = turn(bank[k // 4][:, cap * (k % 4):cap * (k % 4) + cap], x_rows[0:cap, j, k::KT], cap)
                    last.then_inc(rows_turned, 1)

                def gate_up(e, j, i):
                    gp, up = moe_at[l] + 3 * j, moe_at[l] + 3 * j + 1
                    pe.wait_ge(turned_act, l * N_EXP + e + 1)
                    pe.wait_ge(turned_dve, l * N_EXP + e + 1)
                    pe.wait_ge(piece_loaded[gp % NS], 16 * (gp // NS + 1) + 16 * i)
                    pe.wait_ge(piece_loaded[up % NS], 16 * (up // NS + 1) + 16 * i)
                    wg, wu = piece_view(gp, KT, FF), piece_view(up, KT, FF)
                    for k in range(KT):
                        x = x_rowsT[:, j, cap * k:cap * k + cap]
                        if cap == P:
                            mm(bank[4 + j][:, 0:FF], x, wg[:, k, :], start=(k == 0), stop=(k == KT - 1), skip_group_check=True)
                            last = mm(bank[4 + j][:, FF:2 * FF], x, wu[:, k, :], start=False, stop=(k == KT - 1), skip_group_check=True)
                        else:
                            mm(bank[4 + j][0:cap, 0:FF], x, wg[:, k, :], start=(k == 0), stop=(k == KT - 1))
                            last = mm(bank[4 + j][cap:2 * cap, 0:FF], x, wu[:, k, :], start=(k == 0), stop=(k == KT - 1))
                    last.then_inc(gu_full, 1)

                def down(e, j, i):
                    dp = moe_at[l] + 3 * j + 2
                    pe.wait_ge(hid_ready, l * N_EXP + e + 1)
                    pe.sem_inc(pe_passed, 1)
                    for k in range(2):
                        last = turn(bank[7][:, cap * k:cap * k + cap], hid[0:cap, j, k::2], cap)
                    last.then_inc(hidT_full, 1)
                    pe.wait_ge(piece_loaded[dp % NS], 16 * (dp // NS + 1) + 16 * i)
                    pe.wait_ge(hidT_ready, l * N_EXP + e + 1)
                    pe.wait_ge(y_act, l * N_EXP + e)
                    pe.wait_ge(y_dve, l * N_EXP + e)
                    wd = piece_view(dp, 2, D)
                    for k in range(2):
                        for hf in range(2):
                            o = cap if (cap < P and hf) else 0
                            last = mm(bank[2 + hf][o:o + cap, :], hidT[:, j, cap * k:cap * k + cap], wd[:, k, 512 * hf:512 * hf + 512],
                                      start=(k == 0), stop=(k == 1))
                    last.then_inc(down_full, 1)

                def entry(i, e):
                    if isinstance(e, int):
                        return table[:, i, e, :]
                    return table[:, i, bass.ds(e, 1), :].rearrange("p o c -> p (o c)")

                for e in range(2):
                    pe.wait_ge(pick_ready, l * PICKS + e + 1)
                    pe.wait_ge(list_read, l * LISTS + e)
                    for i in range(nm):
                        last = mm(bank[7][0:cap, 256:259], pick[:, e, P * i:P * i + cap], entry(i, e), start=(i == 0), stop=(i == nm - 1))
                    last.then_inc(list_full, 1)
                turn_rows(0, 0)

                def three_experts(i):
                    for j in range(BODY):
                        e = i * BODY + j
                        gate_up(e, j, i)
                        make_list(e + 2, (j + 2) % 3)
                        turn_rows((j + 1) % 3, i + (j + 1) // 3)
                        pe.wait_ge(list_read, l * LISTS + e + 3)
                        down(e, j, i)

                three_experts(0)
                with pe.Fori(1, N_EXP // BODY) as i:
                    three_experts(i)
                gate_up(experts, 0, N_EXP // BODY)
                down(experts, 0, N_EXP // BODY)
                pe.wait_ge(y_act, (l + 1) * N_EXP)
                pe.wait_ge(y_dve, (l + 1) * N_EXP)

                most = pe.value_load(maxcnt[0:1, l:l + 1], min_val=0, max_val=T)
                with pe.If(most > cap):
                    for b in range(1, tokens(l) // cap):
                        with pe.Fori(0, N_EXP) as e:
                            q = (b - 1) * N_EXP + e
                            pe.wait_ge(late_dve[l], 6 * q + 1)
                            for i in range(nm):
                                last = mm(bank[7][0:cap, 256:259], pick[:, 0, P * i:P * i + cap], entry(i, e), start=(i == 0), stop=(i == nm - 1))
                            last.then_inc(late_pe[l], 1)
                            pe.wait_ge(late_in[l], 16 * q + 16)
                            pe.sem_inc(pe_passed, 1)
                            for k in range(KT):
                                last = turn(bank[k // 4][:, cap * (k % 4):cap * (k % 4) + cap], x_rows[0:cap, 0, k::KT], cap)
                            last.then_inc(late_pe[l], 1)
                            pe.wait_ge(late_dve[l], 6 * q + 3)
                            pe.wait_ge(late_loaded[l], 48 * q + 48)
                            for w in range(2):
                                for k in range(KT):
                                    last = mm(bank[4 + w][0:cap, 0:FF], x_rowsT[:, 0, cap * k:cap * k + cap],
                                              late_w[:, w, FF * k:FF * k + FF], start=(k == 0), stop=(k == KT - 1))
                            last.then_inc(late_pe[l], 1)
                            pe.wait_ge(late_dve[l], 6 * q + 4)
                            pe.sem_inc(pe_passed, 1)
                            for k in range(2):
                                last = turn(bank[6][:, cap * k:cap * k + cap], hid[0:cap, 0, k::2], cap)
                            last.then_inc(late_pe[l], 1)
                            pe.wait_ge(late_dve[l], 6 * q + 5)
                            for k in range(2):
                                for hf in range(2):
                                    last = mm(bank[2 + hf][0:cap, :], hidT[:, 0, cap * k:cap * k + cap],
                                              late_w[:, 2, D * k + 512 * hf:D * k + 512 * hf + 512], start=(k == 0), stop=(k == 1))
                            last.then_inc(late_pe[l], 1)
                            pe.wait_ge(late_dve[l], 6 * q + 6)
                for i, t in enumerate(mt):
                    pe.wait_ge(y_summed, before(l, lambda i: len(main_tiles(i))) + i + 1)
                    for hf in range(2):
                        b = open_bank(pe, ("comb", l, t, hf))
                        for k in range(4):
                            last = turn(b[:, P * k:P * k + P], y_parts[:, i % 2, P * (4 * hf + k):P * (4 * hf + k) + P])
                        last.then_inc(bank_full, 1)
            await_emptied(pe, ("comb", DEPTH - 1, TT - 1, 1))
            for t in range(2):
                for hf in range(2):
                    b = open_bank(pe, ("fin", t, hf))
                    for k in range(4):
                        last = turn(b[:, P * k:P * k + P], xT[:, 4 * hf + k, CTX + P * t:CTX + P * t + P])
                    last.then_inc(bank_full, 1)

        @block.scalar
        def _(act):
            af = nc.scalar.activation
            steps = [0]

            def link(ins):
                steps[0] += 1
                ins.then_inc(act_step, 1)
                act.wait_ge(act_step, steps[0])

            def copy_out(key, dst, src=None, func=ACT.Copy, **kw):
                b = await_full(act, key)
                return af(dst, b[:, :] if src is None else src(b), func, **kw).then_inc(emptied["act"], 1)

            taken = [0]

            def root(dst, src, scale=1.0, eps=0):
                taken[0] += 1
                act.wait_ge(root_asked, taken[0])
                af(dst, src, ACT.Sqrt, scale=scale, bias=eps_col[:, eps:eps + 1]).then_inc(roots, 1)

            def squares(key, t0, nt):
                n = norm_at(key)
                for k in range(KT):
                    if k >= 2:
                        act.wait_ge(sq_used, 7 * n + k - 1)
                    elif n:
                        await_full(act, ("ms2", 0) if key == ("ms1", 1) else ("ms1", key[1]))
                    af(sq_x[:, k % 2, 0:nt], xT[:, k, t0:T], ACT.Square).then_inc(sq_ready, 1)
                root(rstd[:, 0:nt], await_full(act, key)[:, 0:nt], 1.0 / D)

            def shifts(l, which, t0):
                for k in range(KT):
                    act.wait_ge(gained, KT * (2 * l + which) + k + 1)
                    for s in streams(l) if which else (0, 1):
                        last = af(hT[:, k, span(l, s)], hT[:, k, span(l, s)], ACT.Identity, bias=mod[:, 24 * which + k, s:s + 1])
                last.then_inc(h_ready, 1)

            for tt in range(TT):
                copy_out(("x", tt, 0), xT[:, 0:4, P * tt:P * tt + P], lambda b: b[:, :].rearrange("p (k n) -> p k n", k=4))
            for l in range(DEPTH):
                mt, t0 = main_tiles(l), c0(l)
                nt = T - t0
                await_emptied(act, ("vec", l))
                for s, name in enumerate(("cctx", "c")):
                    last = af(silu_c[:, :, s], vec[:, VEC_AT[name]:VEC_AT[name] + KT], ACT.Silu)
                last.then_inc(silu_ready, 1)
                act.wait_ge(lg_arg, 2 * l + 1)
                af(lg[:, 8:16], lg[:, 0:8], ACT.Exp, scale=-1.0).then_inc(lg_exp, 1)
                if l:
                    await_emptied(act, ("comb", l - 1, TT - 1, 1))
                else:
                    await_emptied(act, ("x", TT - 1, 0))
                    await_emptied(act, ("x", TT - 1, 1))
                squares(("ms1", l), 0, T)
                act.wait_ge(lg_arg, 2 * l + 2)
                act.wait_ge(decay_arg, l + 1)
                for h in range(HEADS_R):
                    af(decay[:, 0, h, :], decay[:, 0, h, :], ACT.Exp)
                    af(decay[:, 1, h, :], const_cols("diff"), ACT.Exp, scale=lg[:, 16 + h:17 + h], bias=lg[:, 24 + h:25 + h])
                    last = af(decay_b[:, h, :], const_cols("diff"), ACT.Exp, scale=lg[:, 36 + h:37 + h], bias=lg[:, 28 + h:29 + h])
                last.then_inc(decay_ready, 1)
                shifts(l, 0, 0)
                await_emptied(act, ("c", l, 2, TT - 1))
                for t in range(TT):
                    for j, (at, n) in enumerate(((0, QL), (QL, KVL), (QL + KVL, ROPE))):
                        if j or t in mt:
                            link(af(sq_tok[:, 0, 0:n], lat_c[:, t, at:at + n], ACT.Square, accum_out=stat[:, 4 * j + t:4 * j + t + 1]))
                for j, n in enumerate((QL, KVL, ROPE)):
                    last = af(stat[:, 12 + 4 * j:16 + 4 * j], stat[:, 4 * j:4 * j + 4], ACT.Sqrt, scale=1.0 / n, bias=eps_col[:, 0:1])
                last.then_inc(c_squared, 1)
                for h in range(4):
                    copy_out(("q", l, h), rqT[:, h, t0:T], lambda b: b[:, 0:nt])
                for h in range(4):
                    copy_out(("k", l, h), rkT[:, h, :])
                for h in range(4):
                    copy_out(("g", l, h), y_ret[:, h, t0:T], lambda b: b[:, 0:nt], ACT.Silu)
                for u in range(len(ret_units(l))):
                    root(stat[:, 40:42], stat[:, 37:40:2])
                for t in range(TT + 1):
                    if t < TT:
                        if t in mt:
                            b = await_full(act, ("ct", l, t, 0))
                            for k in range(3):
                                last = af(cqT[:, k, :], b[:, P * k:P * k + P], ACT.Identity, scale=vcol("qag", k))
                            last.then_inc(emptied["act"], 1)
                        b = await_full(act, ("ct", l, t, 1))
                        for k in range(2):
                            last = af(ckT[:, k, :], b[:, P * k:P * k + P], ACT.Identity, scale=vcol("kvag", k))
                        last.then_inc(emptied["act"], 1)
                        if t in mt:
                            for hf in range(2):
                                b = await_full(act, ("qp", l, t, hf))
                                if t:
                                    await_emptied(act, ("kvp", l, t - 1, hf))
                                af(sq_tok[:, hf, 0:384], b[:, 0:384], ACT.Square).then_inc(qk_squared, 1)
                            root(stat[:, 48:56], stat[:, 48:56], eps=1)
                        for hf in range(2):
                            b = await_full(act, ("kvp", l, t, hf))
                            kv4 = b[:, :].rearrange("p (h d) -> p h d", h=4)
                            if t in mt:
                                await_emptied(act, ("qp", l, t, hf))
                            elif t:
                                await_emptied(act, ("kvp", l, t - 1, hf))
                            af(sq_tok[:, hf, 0:256].rearrange("p (h d) -> p h d", h=4), kv4[:, :, 0:NOPE], ACT.Square)
                            af(mv[:, t, 256 * hf:256 * hf + 256].rearrange("p (h d) -> p h d", h=4), kv4[:, :, NOPE:P],
                               ACT.Copy).then_inc(qk_squared, 1)
                        root(stat[:, 64:72], stat[:, 64:72], eps=2)
                    if t >= 1:
                        for name, dst in (("qt", qT), ("kt", kT)):
                            if name == "qt" and t - 1 not in mt:
                                continue
                            for hf in range(2):
                                b = await_full(act, (name, l, t - 1, hf))
                                af(dst[0:QK, 4 * hf:4 * hf + 4, P * (t - 1):P * t],
                                   b[0:QK, :].rearrange("p (h n) -> p h n", h=4), ACT.Copy).then_inc(emptied["act"], 1)
                au = att_units(l)
                for n in range(len(au) + 2):
                    if n < len(au):
                        t, h = au[n]
                        nk = T if t >= 2 else CTX
                        b = await_full(act, ("S", l, n))
                        act.wait_ge(neg_max, before(l, lambda i: len(att_units(i))) + n + 1)
                        if n >= 2:
                            await_full(act, ("PT", l, n - 2))
                        if n >= 4:
                            await_emptied(act, ("pv", l, n - 4))
                        af(probs[:, n % 2, 0:nk], b[:, 0:nk], ACT.Exp, bias=stat[:, 80 + n % 4:81 + n % 4], scale=QK ** -0.5,
                           accum_out=stat[:, 84 + n % 4:85 + n % 4]).then_inc(emptied["act"], 1)
                    if n >= 2 and au[n - 2][1] == HEADS_M - 1:
                        t = au[n - 2][0]
                        copy_out(("omt", l, t), y_mla[:, :, P * t:P * t + P], lambda b: b[:, :].rearrange("p (k n) -> p k n", k=4))
                copy_out(("ws", l), wsT[:, :, :].rearrange("p g i -> p (g i)"))
                for g in range(4):
                    copy_out(("u", l, g), y_gmlp[:, g, t0:T], lambda b: b[:, 0:nt], ACT.Gelu_apprx_tanh)
                for j in range(2):
                    for t in mt:
                        copy_out(("gv", l, j, t), gv[:, t, 256 * j:256 * j + 256], lambda b: b[:, 0:256], ACT.Gelu_apprx_tanh)
                root(stat[:, 112 + mt[0]:116], stat[:, 105 + 2 * mt[0]:112:2])
                n = 0
                for mp in range(4):
                    for br in range(3):
                        for i in range(2):
                            if n >= 2:
                                m_, b_, i_ = (n - 2) // 6, (n - 2) // 2 % 3, (n - 2) % 2
                                await_emptied(act, ("y", l, 2 * m_ + i_, b_))
                            copy_out(("gate", l, 2 * mp + i, br), gate_t[:, n % 2, 0:nt], lambda b: b[:, 0:nt], ACT.Tanh, scale=0.5)
                            n += 1
                await_emptied(act, ("out", l, 7))
                squares(("ms2", l), t0, nt)
                shifts(l, 1, t0)
                for i, t in enumerate(mt):
                    if i >= 2:
                        act.wait_ge(h2_stored[i % 2], 16 * (h2_base(l, i % 2) + i // 2))
                    copy_out(("h2", l, t, 0), h2_tok[:, i % 2, 0:512])
                    await_emptied(act, ("h2", l, t, 0))
                    await_emptied(act, ("h2", l, t, 1))
                    act.dma_start(h2_dram[P * i:P * i + P, :], h2_tok[:, i % 2, :]).then_inc(h2_stored[i % 2], 16)
                copy_out(("rt", l), score[:, 0:len(mt), :].rearrange("p t e -> p (t e)"), lambda b: b[:, 0:N_EXP * len(mt)], ACT.Tanh, scale=0.5)
                for m in range(2):
                    copy_out(("sg", l, m), sil_s[:, m, t0:T], lambda b: b[:, 0:nt], ACT.Silu)

                cap = CAP[l]
                act.wait_ge(moe_ready, l + 1)

                def turned(e, j):
                    act.wait_ge(rows_turned, l * N_EXP + e + 1)
                    af(x_rowsT[:, j, 0:4 * cap], bank[0][:, 0:4 * cap], ACT.Copy).then_inc(turned_act, 1)

                def silu(e, j):
                    act.wait_ge(gu_full, l * N_EXP + e + 1)
                    af(act_g[0:cap, j, :], bank[4 + j][0:cap, 0:FF], ACT.Silu).then_inc(silu_done, 1)

                def rows_down(e, j, i):
                    act.wait_ge(down_full, l * N_EXP + e + 1)
                    act.wait_ge(rows_out[j], 16 * (l * experts_of[j]) + 16 * i)
                    af(y_rows[0:cap, j, 0:512], bank[2][0:cap, :], ACT.Copy).then_inc(y_act, 1)

                turned(0, 0)

                def three_experts(i):
                    for j in range(BODY):
                        e = i * BODY + j
                        silu(e, j)
                        turned(e + 1, (j + 1) % 3)
                        rows_down(e, j, i)

                three_experts(0)
                with act.Fori(1, N_EXP // BODY) as i:
                    three_experts(i)
                silu(experts, 0)
                rows_down(experts, 0, N_EXP // BODY)
                most = act.value_load(maxcnt[0:1, l:l + 1], min_val=0, max_val=T)
                with act.If(most > cap):
                    for b in range(1, tokens(l) // cap):
                        with act.Fori(0, N_EXP) as e:
                            q = (b - 1) * N_EXP + e
                            act.wait_ge(late_pe[l], 5 * q + 3)
                            af(act_g[0:cap, 0, :], bank[4][0:cap, 0:FF], ACT.Silu).then_inc(late_act[l], 1)
            for t in range(2):
                copy_out(("fin", t, 0), fin[:, t, 0:512])
            await_emptied(act, ("fin", 1, 0))
            await_emptied(act, ("fin", 1, 1))
            act.dma_start(out.rearrange("o (t p) d -> p (o t) d", p=P), fin[:, :, :]).then_inc(stored, 16)
            act.wait_ge(stored, 16)

        @block.vector
        def _(dve):
            v = nc.vector
            steps = [0]

            def link(ins):
                steps[0] += 1
                ins.then_inc(dve_step, 1)
                dve.wait_ge(dve_step, steps[0])

            def copy_out(key, dst, src=None):
                b = await_full(dve, key)
                return v.tensor_copy(dst, b[:, :] if src is None else src(b)).then_inc(emptied["dve"], 1)

            def norm(l, which):
                key = (("ms1", "ms2")[which], l)
                b = await_full(dve, key)
                t0 = c0(l) if which else 0
                nt = T - t0
                ask_root()
                link(v.reciprocal(rstd[:, 0:nt], rstd[:, 0:nt]))
                dve.nop().then_inc(emptied["dve"], 1)
                g = (gain1, gain2)[which]
                for k in range(KT):
                    for s in streams(l) if which else (0, 1):
                        last = v.scalar_tensor_tensor(out=hT[:, k, span(l, s)], in0=xT[:, k, span(l, s)], scalar=g[:, k, s:s + 1],
                                                      in1=rstd[:, span(l, s, t0)], op0=ALU.mult, op1=ALU.mult)
                    last.then_inc(gained, 1)

            def rope(x, t, heads):
                def table_of(name):
                    at = CONST_AT[name] + ROPE * (t - 2)
                    return const[:, at:at + ROPE]

                cos_b = table_of("cos").unsqueeze(1).to_broadcast([P, heads, ROPE])
                y, z = rope_t[:, 0:heads, :], rope_u[:, 0:heads, :]
                v.tensor_tensor(y, x, cos_b, ALU.mult)
                for hf in range(2):
                    for i in range(2):
                        a, b = 16 * hf + 8 * i, 16 * hf + 8 * (1 - i)
                        last = v.tensor_tensor(z[:, :, a:a + 8], x[:, :, b:b + 8],
                                               table_of("sin")[:, a:a + 8].unsqueeze(1).to_broadcast([P, heads, 8]), ALU.mult)
                link(last)
                return v.tensor_tensor(x, y, z, ALU.add)

            asked = [0]

            def ask_root():
                asked[0] += 1
                dve.nop().then_inc(root_asked, 1)
                dve.wait_ge(roots, asked[0])

            v.memset(ones[:, :], 1.0)
            for i, w in enumerate((1, QK, NOPE)):
                v.memset(eps_col[:, i:i + 1], w * EPS)
            link(v.memset(stat[:, :], 0.0))
            dve.nop().then_inc(ones_ready, 1)
            for tt in range(TT):
                copy_out(("x", tt, 1), xT[:, 4:8, P * tt:P * tt + P], lambda b: b[:, :].rearrange("p (k n) -> p k n", k=4))
            for l in range(DEPTH):
                mt, t0 = main_tiles(l), c0(l)
                nt = T - t0
                nm = len(mt)
                copy_out(("vec", l), vec[:, :], lambda b: b[:, 0:N_VEC])
                await_emptied(dve, ("vec", l))
                dec = rows("dec")
                link(v.scalar_tensor_tensor(out=lg[:, 0:8], in0=dec, scalar=-1.0, in1=dec, op0=ALU.mult, op1=ALU.max))
                dve.nop().then_inc(lg_arg, 1)
                dve.wait_ge(lg_exp, l + 1)
                e_, s_, s2, q_ = lg[:, 8:16], lg[:, 40:48], lg[:, 48:56], lg[:, 56:64]
                link(v.tensor_scalar(s_, e_, 2.0, None, ALU.add))
                link(v.reciprocal(s2, s_))
                link(v.tensor_tensor(s_, s2, e_, ALU.mult))
                link(v.tensor_tensor(s2, s_, s_, ALU.mult))
                link(v.tensor_scalar(q_, s2, 1.0 / 19, None, ALU.mult))
                for odd in (17, 15, 13, 11, 9, 7, 5, 3):
                    link(v.scalar_tensor_tensor(out=q_, in0=q_, scalar=1.0 / odd, in1=s2, op0=ALU.add, op1=ALU.mult))
                link(v.scalar_tensor_tensor(out=q_, in0=q_, scalar=1.0, in1=s_, op0=ALU.add, op1=ALU.mult))
                link(v.tensor_scalar(s2, dec, 0.0, None, ALU.min))
                link(v.scalar_tensor_tensor(out=lg[:, 16:24], in0=q_, scalar=-2.0, in1=s2, op0=ALU.mult, op1=ALU.add))
                link(v.tensor_scalar(lg[:, 24:32], lg[:, 16:24], float(CTX), None, ALU.mult))
                link(v.tensor_scalar(lg[:, 32:40], lg[:, 16:24], -1.0, None, ALU.mult))
                dve.nop().then_inc(lg_arg, 1)
                if l:
                    await_full(dve, ("comb", l - 1, TT - 1, 1))
                diff = const_cols("diff")
                for h in range(HEADS_R):
                    v.tensor_scalar(decay[:, 0, h, :], diff, 0.0, lg[:, 16 + h:17 + h], ALU.max, ALU.mult)
                    link(v.tensor_scalar(decay_b[:, h, :], diff, 0.0, lg[:, 36 + h:37 + h], ALU.min, ALU.mult))
                    last = v.tensor_tensor(decay[:, 0, h, :], decay[:, 0, h, :], decay_b[:, h, :], ALU.add)
                last.then_inc(decay_arg, 1)
                b = await_full(dve, ("ada", l))
                ada_b = vec[:, VEC_AT["ada_b"]:VEC_AT["ada_b"] + 48].unsqueeze(2).to_broadcast([P, 48, 2])
                link(v.tensor_tensor(mod[:, :, :], b[:, 0:96].rearrange("p (m s) -> p m s", s=2), ada_b, ALU.add))
                dve.nop().then_inc(emptied["dve"], 1)
                for g, name, at in ((gain1, "n1", 8), (gain2, "n2", 32)):
                    n_g = vec[:, VEC_AT[name]:VEC_AT[name] + KT].unsqueeze(2).to_broadcast([P, KT, 2])
                    link(v.scalar_tensor_tensor(out=g[:, :, :], in0=mod[:, at:at + KT, :], scalar=1.0, in1=n_g, op0=ALU.add, op1=ALU.mult))
                link(v.tensor_scalar(half_gate[:, :, :], mod[:, 16:24, :], 0.5, None, ALU.mult))
                v.tensor_scalar(rows("qn"), rows("qn"), QK ** 0.5, None, ALU.mult)
                link(v.tensor_scalar(rows("kn"), rows("kn"), NOPE ** 0.5, None, ALU.mult))
                norm(l, 0)
                for t in mt:
                    copy_out(("c", l, 0, t), lat_c[:, t, 0:256], lambda b: b[:, 0:256])
                for j, n in ((1, 256), (2, CW - 512)):
                    for t in range(TT):
                        copy_out(("c", l, j, t), lat_c[:, t, 256 * j:256 * j + n], lambda b: b[:, 0:n])
                dve.wait_ge(decay_ready, l + 1)
                link(v.tensor_tensor(decay[:, 1, :, :], decay[:, 1, :, :], decay_b[:, :, :], ALU.add))
                dve.wait_ge(c_squared, l + 1)
                link(v.reciprocal(stat[:, 12:24], stat[:, 12:24]))
                for t in range(TT):
                    if t in mt:
                        v.tensor_scalar(lat_c[:, t, 0:QL], lat_c[:, t, 0:QL], stat[:, 12 + t:13 + t], None, ALU.mult)
                    v.tensor_scalar(lat_c[:, t, QL:QL + KVL], lat_c[:, t, QL:QL + KVL], stat[:, 16 + t:17 + t], None, ALU.mult)
                    kr = lat_c[:, t, QL + KVL:CW]
                    link(v.scalar_tensor_tensor(out=kr, in0=kr, scalar=stat[:, 20 + t:21 + t], in1=rows("kr"), op0=ALU.mult, op1=ALU.mult))
                    if t >= 2:
                        link(rope(lat_c[:, t:t + 1, QL + KVL:CW], t, 1))
                    dve.nop().then_inc(c_normed, 1)
                for j in range(2):
                    for t in range(TT):
                        copy_out(("v", l, j, t), rv[:, t, 256 * j:256 * j + 256], lambda b: b[:, 0:256])
                ru = ret_units(l)
                await_emptied(dve, ("g", l, 3))
                for n in range(len(ru) + 2):
                    if n < len(ru):
                        h, s = ru[n]
                        if n >= 2:
                            await_full(dve, ("o", l, n - 2))
                        for pr in range(1 + s):
                            b = await_full(dve, ("s", l, n, pr))
                            for i in range(2):
                                cross = s == 1 and pr == 0
                                w = decay[:, int(cross), h, P - P * i:P - P * i + 256]
                                last = v.scalar_tensor_tensor(out=att[:, n % 2, 2 * pr + i, :], in0=b[:, 256 * i:256 * i + 256],
                                                              scalar=P ** -0.5, in1=w, op0=ALU.mult, op1=ALU.mult)
                            last.then_inc(emptied["dve"], 1)
                    if 0 <= n - 1 < len(ru):
                        u = n - 1
                        if u >= 2:
                            await_full(dve, ("ot", l, u - 2))
                        b = await_full(dve, ("o", l, u))
                        for i in range(2):
                            last = v.bn_stats(stat[:, 24 + 6 * i:30 + 6 * i], b[:, P * i:P * i + P])
                        link(last)
                        for i in range(2):
                            last = v.bn_aggr(stat[:, 36 + 2 * i:38 + 2 * i], stat[:, 24 + 6 * i:30 + 6 * i])
                        link(last)
                        ask_root()
                        link(v.reciprocal(stat[:, 40:42], stat[:, 40:42]))
                        for i in range(2):
                            last = v.tensor_scalar(on[:, u % 2, P * i:P * i + P], b[:, P * i:P * i + P], stat[:, 36 + 2 * i:37 + 2 * i],
                                                   stat[:, 40 + i:41 + i], ALU.subtract, ALU.mult)
                        link(last)
                        dve.nop().then_inc(on_ready, 1)
                        dve.nop().then_inc(emptied["dve"], 1)
                    if n >= 2:
                        h, s = ru[n - 2]
                        b = await_full(dve, ("ot", l, n - 2))
                        link(v.tensor_scalar(tmp_ret[:, n % 2, :], b[:, 0:256], vcol("gng", h), vcol("gnb", h), ALU.mult, ALU.add))
                        v.tensor_tensor(y_ret[:, h, span(l, s)], y_ret[:, h, span(l, s)], tmp_ret[:, n % 2, :],
                                        ALU.mult).then_inc(emptied["dve"], 1)
                sq_n = before(l, lambda i: 2 * TT + 2 * len(main_tiles(i)))
                for t in range(TT):
                    parts = [("qp", q_tok, 384, QK, 48)] * (t in mt) + [("kvp", k_tok, 256, NOPE, 64)]
                    for name, dst, width, w, at in parts:
                        for hf in range(2):
                            sq_n += 1
                            dve.wait_ge(qk_squared, sq_n)
                            sq = sq_tok[:, hf, 0:width].rearrange("p (h d) -> p h d", h=4)
                            last = v.tensor_reduce(stat[:, at + 4 * hf:at + 4 * hf + 4], sq, AX_X, ALU.add)
                        link(last)
                        ask_root()
                        link(v.reciprocal(stat[:, at:at + 8], stat[:, at:at + 8]))
                        if t:
                            await_full(dve, ("kt", l, t - 1, 1))
                        for hf in range(2):
                            b = await_full(dve, (name, l, t, hf))
                            r = stat[:, at + 4 * hf:at + 4 * hf + 4]
                            src = b[:, 0:4 * (QK if name == "qp" else P)].rearrange("p (h d) -> p h d", h=4)[:, :, 0:w]
                            last = v.tensor_tensor(dst[:, 4 * hf:4 * hf + 4, 0:w], src, r.unsqueeze(2).to_broadcast([P, 4, w]), ALU.mult)
                            last.then_inc(emptied["dve"], 1)
                        await_emptied(dve, (name, l, t, 1))
                        g = rows("qn" if name == "qp" else "kn")
                        link(v.tensor_tensor(dst[:, :, 0:w], dst[:, :, 0:w], g.unsqueeze(1).to_broadcast([P, HEADS_M, w]), ALU.mult))
                        if name == "qp" and t >= 2:
                            link(rope(dst[:, :, NOPE:QK], t, HEADS_M))
                    link(v.tensor_copy(k_tok[:, :, NOPE:QK], lat_c[:, t:t + 1, QL + KVL:CW].to_broadcast([P, HEADS_M, ROPE])))
                    dve.nop().then_inc(qk_tok_ready, 1)
                au = att_units(l)
                for n in range(len(au) + 2):
                    if n < len(au):
                        t, h = au[n]
                        nk = T if t >= 2 else CTX
                        b = await_full(dve, ("S", l, n))
                        mx = stat[:, 80 + n % 4:81 + n % 4]
                        link(v.tensor_reduce(mx, b[:, 0:nk], AX_X, ALU.max))
                        link(v.tensor_scalar(mx, mx, -QK ** -0.5, None, ALU.mult))
                        dve.nop().then_inc(neg_max, 1)
                    if 0 <= n - 1 < len(au):
                        t, h = au[n - 1]
                        nk = T if t >= 2 else CTX
                        if n >= 3:
                            await_full(dve, ("pv", l, n - 3))
                        copy_out(("PT", l, n - 1), probsT[:, (n - 1) % 2, 0:nk], lambda b: b[:, 0:nk])
                    if n >= 2:
                        t, h = au[n - 2]
                        rec = stat[:, 88 + n % 4:89 + n % 4]
                        await_emptied(dve, ("S", l, n - 2))
                        link(v.reciprocal(rec, stat[:, 84 + (n - 2) % 4:85 + (n - 2) % 4]))
                        b = await_full(dve, ("pv", l, n - 2))
                        if h == 0 and t > mt[0]:
                            await_full(dve, ("omt", l, t - 1))
                        v.tensor_scalar(o_tok[:, VD * h:VD * h + VD], b[:, 0:VD], rec, None, ALU.mult).then_inc(emptied["dve"], 1)
                for t in mt:
                    await_emptied(dve, ("gv", l, 1, t))
                    link(v.bn_stats(stat[:, 96:102], gv[:, t, :]))
                    link(v.bn_aggr(stat[:, 104 + 2 * t:106 + 2 * t], stat[:, 96:102]))
                ask_root()
                link(v.reciprocal(stat[:, 112 + mt[0]:116], stat[:, 112 + mt[0]:116]))
                for t in mt:
                    link(v.tensor_scalar(gv[:, t, :], gv[:, t, :], stat[:, 104 + 2 * t:105 + 2 * t], stat[:, 112 + t:113 + t], ALU.subtract, ALU.mult))
                    link(v.tensor_tensor(gv[:, t, :], gv[:, t, :], rows("lng"), ALU.mult))
                    v.tensor_tensor(gv[:, t, :], gv[:, t, :], rows("lnb"), ALU.add).then_inc(gv_normed, 1)
                for i, t in enumerate(mt):
                    b = await_full(dve, ("sv", l, t))
                    link(v.tensor_tensor(sv_tmp[:, i % 2, :], b[:, :], rows("bs"), ALU.add))
                    dve.nop().then_inc(emptied["dve"], 1)
                    yg = y_gmlp[:, :, P * t:P * t + P]
                    v.tensor_tensor(yg, yg, sv_tmp[:, i % 2, :].rearrange("p (g n) -> p g n", g=4), ALU.mult).then_inc(y_gmlp_ready, 1)
                n = 0
                for mp in range(4):
                    for br in range(3):
                        for i in range(2):
                            m = 2 * mp + i
                            b = await_full(dve, ("y", l, m, br))
                            await_emptied(dve, ("gate", l, m, br))
                            dst = merged[:, m, 0:nt] if br == 0 else prod_t[:, 0:nt]
                            ins = v.scalar_tensor_tensor(out=dst, in0=gate_t[:, n % 2, 0:nt], scalar=1.0, in1=b[:, 0:nt], op0=ALU.add, op1=ALU.mult)
                            ins.then_inc(emptied["dve"], 1)
                            n += 1
                            if br:
                                await_emptied(dve, ("y", l, m, br))
                                ins = v.tensor_tensor(merged[:, m, 0:nt], merged[:, m, 0:nt], prod_t[:, 0:nt], ALU.add)
                                link(ins)
                            if br == 2:
                                dve.nop().then_inc(merged_ready, 1)

                def residual(key, gate, m, cols, src0):
                    b = await_full(dve, key)
                    for s in streams(l):
                        last = v.scalar_tensor_tensor(out=xT[:, m, span(l, s)], in0=b[:, span(l, s, t0)], scalar=gate[:, s:s + 1],
                                                      in1=xT[:, m, span(l, s)], op0=ALU.mult, op1=ALU.add)
                    last.then_inc(emptied["dve"], 1)

                for m in range(8):
                    residual(("out", l, m), half_gate[:, m, :], m, nt, t0)
                norm(l, 1)
                for i, t in enumerate(mt):
                    if i >= 2:
                        dve.wait_ge(h2_stored[i % 2], 16 * (h2_base(l, i % 2) + i // 2))
                    copy_out(("h2", l, t, 1), h2_tok[:, i % 2, 512:1024])
                for m in range(2):
                    b = await_full(dve, ("su", l, m))
                    await_emptied(dve, ("sg", l, m))
                    link(v.tensor_tensor(shT[:, m, t0:T], sil_s[:, m, t0:T], b[:, 0:nt], ALU.mult))
                    dve.nop().then_inc(emptied["dve"], 1)
                    dve.nop().then_inc(sh_ready, 1)
                await_emptied(dve, ("rt", l))
                sc, se, ma, eqm, cu = (x[:, 0:nm, :] for x in (score, sel, mask, eq, cum))
                link(v.tensor_scalar(sc, sc, 0.5, 0.5, ALU.mult, ALU.add))
                link(v.tensor_tensor(se, sc, rows("bias").unsqueeze(1).to_broadcast([P, nm, N_EXP]), ALU.add))
                for i in range(nm):
                    last = v.max(top8[:, i, :], sel[:, i, :])
                link(last)
                sixth = top8[:, 0:nm, TOPK - 1:TOPK].to_broadcast([P, nm, N_EXP])
                v.tensor_tensor(ma, se, sixth, ALU.is_gt)
                link(v.tensor_tensor(eqm, se, sixth, ALU.is_equal))
                v.memset(one64[:, :], 1.0)
                link(v.tensor_reduce(need[:, 0:nm], ma, AX_X, ALU.add))
                link(v.tensor_scalar(need[:, 0:nm], need[:, 0:nm], -1.0, float(TOPK), ALU.mult, ALU.add))
                for i in range(nm):
                    last = v.tensor_tensor_scan(cum[:, i, :], one64[:, :], eq[:, i, :], 0.0, ALU.mult, ALU.add)
                link(last)
                link(v.tensor_tensor(cu, cu, need[:, 0:nm].unsqueeze(2).to_broadcast([P, nm, N_EXP]), ALU.is_le))
                link(v.tensor_tensor(eqm, eqm, cu, ALU.mult))
                link(v.tensor_tensor(ma, ma, eqm, ALU.add))
                dve.nop().then_inc(mask_ready, 1)
                link(v.memset(table[:, :, :, :], 0.0))
                for i in range(nm):
                    last = v.tensor_tensor_scan(cum[:, i, :], one64[:, :], mask[:, i, :], 0.0, ALU.mult, ALU.add)
                link(last)
                link(v.tensor_tensor(kslot[:, 0:nm, :], cu, ma, ALU.subtract))
                tok = const[:, CONST_AT["tok"] + 4 * l + mt[0]:CONST_AT["tok"] + 4 * l + TT].unsqueeze(2).to_broadcast([P, nm, N_EXP])
                v.scalar_tensor_tensor(out=table[:, 0:nm, 0:N_EXP, 1], in0=kslot[:, 0:nm, :], scalar=float(tokens(l)), in1=tok, op0=ALU.mult, op1=ALU.add)
                v.tensor_copy(table[:, 0:nm, 0:N_EXP, 0], tok)
                link(v.tensor_tensor(se, sc, ma, ALU.mult))
                link(v.tensor_reduce(wsum[:, 0:nm], se, AX_X, ALU.add))
                link(v.reciprocal(wsum[:, 0:nm], wsum[:, 0:nm]))
                link(v.scalar_tensor_tensor(out=table[:, 0:nm, 0:N_EXP, 2], in0=se, scalar=ROUTED_SCALE,
                                            in1=wsum[:, 0:nm].unsqueeze(2).to_broadcast([P, nm, N_EXP]), op0=ALU.mult, op1=ALU.mult))
                v.memset(pos1[:, :, :], 0.0)
                link(v.memset(x_rows[:, :, :], 0.0))
                dve.nop().then_inc(small_used, 1)
                for m in range(8):
                    residual(("sd", l, m), mod[:, 40 + m, :], m, nt, t0)
                b = await_full(dve, ("pos", l))
                link(v.scalar_tensor_tensor(out=pos1[:, 0:nm, 0:N_EXP], in0=b[:, 0:nm * N_EXP].rearrange("p (t e) -> p t e", t=nm),
                                            scalar=1.0, in1=ma, op0=ALU.add, op1=ALU.mult))
                dve.nop().then_inc(emptied["dve"], 1)
                b = await_full(dve, ("cnt", l))
                link(v.tensor_reduce(need[:, 0:1], b[:, 0:N_EXP], AX_X, ALU.max))
                dve.nop().then_inc(emptied["dve"], 1)
                link(v.tensor_copy(maxcnt[:, l:l + 1], need[:, 0:1]))
                dve.nop().then_inc(moe_ready, 1)

                cap = CAP[l]

                def picks(e, j, iota):
                    for i in range(nm):
                        pp = pos1[:, i, e:e + 1] if isinstance(e, int) else pos1[:, i, bass.ds(e, 1)]
                        last = v.tensor_scalar(pick[:, j, P * i:P * i + cap], iota, pp, None, ALU.is_equal)
                    return last

                def read_list(j):
                    v.tensor_scalar(idx[0:cap, j, :], bank[7][0:cap, 256:258], BIG, None, ALU.add)
                    return v.tensor_copy(wrow[0:cap, j:j + 1], bank[7][0:cap, 258:259])

                def pick_for(e, j):
                    dve.wait_ge(list_full, l * LISTS + e - 2)
                    picks(e, j, const_cols("iota1")[:, 0:cap]).then_inc(pick_ready, 1)

                def list_of(e, j, i):
                    dve.wait_ge(list_full, l * LISTS + e + 1)
                    dve.wait_ge(rows_out[j], 16 * (l * experts_of[j]) + 16 * i)
                    read_list(j).then_inc(list_read, 1)

                def turned(e, j):
                    dve.wait_ge(rows_turned, l * N_EXP + e + 1)
                    v.tensor_copy(x_rowsT[:, j, 4 * cap:8 * cap], bank[1][:, 0:4 * cap]).then_inc(turned_dve, 1)

                def hidden(e, j):
                    dve.wait_ge(silu_done, l * N_EXP + e + 1)
                    dve.wait_ge(list_read, l * LISTS + e + 1)
                    up = bank[4 + j][:, FF:2 * FF] if cap == P else bank[4 + j][cap:2 * cap, 0:FF]
                    v.scalar_tensor_tensor(out=hid[0:cap, j, :], in0=act_g[0:cap, j, :], scalar=wrow[0:cap, j:j + 1], in1=up,
                                           op0=ALU.mult, op1=ALU.mult).then_inc(hid_ready, 1)

                def hidden_turned(e, j):
                    dve.wait_ge(hidT_full, l * N_EXP + e + 1)
                    v.tensor_copy(hidT[:, j, 0:2 * cap], bank[7][:, 0:2 * cap]).then_inc(hidT_ready, 1)

                def rows_down(e, j, i):
                    dve.wait_ge(down_full, l * N_EXP + e + 1)
                    o = 0 if cap == P else cap
                    v.tensor_copy(y_rows[0:cap, j, 512:1024], bank[3][o:o + cap, :]).then_inc(y_dve, 1)

                for e in range(3):
                    picks(e, e, const_cols("iota1")[:, 0:cap]).then_inc(pick_ready, 1)
                for e in range(2):
                    list_of(e, e, 0)
                turned(0, 0)

                def three_experts(i):
                    for j in range(BODY):
                        e = i * BODY + j
                        hidden(e, j)
                        list_of(e + 2, (j + 2) % 3, i + (j + 2) // 3)
                        pick_for(e + 3, j)
                        turned(e + 1, (j + 1) % 3)
                        hidden_turned(e, j)
                        rows_down(e, j, i)

                three_experts(0)
                with dve.Fori(1, N_EXP // BODY) as i:
                    three_experts(i)
                hidden(experts, 0)
                hidden_turned(experts, 0)
                rows_down(experts, 0, N_EXP // BODY)

                most = dve.value_load(maxcnt[0:1, l:l + 1], min_val=0, max_val=T)
                with dve.If(most > cap):
                    for j in range(3):
                        dve.wait_ge(rows_out[j], 16 * ((l + 1) * experts_of[j]))
                    for b in range(1, tokens(l) // cap):
                        v.tensor_scalar(hid[:, 1, 0:cap], const_cols("iota1")[:, 0:cap], float(b * cap), None, ALU.add).then_inc(late_iota[l], 1)
                        dve.wait_ge(late_iota[l], b)
                        with dve.Fori(0, N_EXP) as e:
                            q = (b - 1) * N_EXP + e
                            picks(e, 0, hid[:, 1, 0:cap]).then_inc(late_dve[l], 1)
                            dve.wait_ge(late_pe[l], 5 * q + 1)
                            read_list(0).then_inc(late_dve[l], 1)
                            dve.wait_ge(late_pe[l], 5 * q + 2)
                            v.tensor_copy(x_rowsT[:, 0, 0:4 * cap], bank[0][:, 0:4 * cap])
                            v.tensor_copy(x_rowsT[:, 0, 4 * cap:8 * cap], bank[1][:, 0:4 * cap]).then_inc(late_dve[l], 1)
                            dve.wait_ge(late_act[l], q + 1)
                            dve.wait_ge(late_dve[l], 6 * q + 2)
                            v.scalar_tensor_tensor(out=hid[0:cap, 0, :], in0=act_g[0:cap, 0, :], scalar=wrow[0:cap, 0:1],
                                                   in1=bank[5][0:cap, 0:FF], op0=ALU.mult, op1=ALU.mult).then_inc(late_dve[l], 1)
                            dve.wait_ge(late_pe[l], 5 * q + 4)
                            v.tensor_copy(hidT[:, 0, 0:2 * cap], bank[6][:, 0:2 * cap]).then_inc(late_dve[l], 1)
                            dve.wait_ge(late_pe[l], 5 * q + 5)
                            v.tensor_copy(y_rows[0:cap, 0, 0:512], bank[2][0:cap, :])
                            v.tensor_copy(y_rows[0:cap, 0, 512:1024], bank[3][0:cap, :]).then_inc(late_dve[l], 1)
                            dve.wait_ge(late_out[l], 16 * q + 16)

                for i, t in enumerate(mt):
                    dve.wait_ge(y_in[i % 2], 16 * (h2_base(l, i % 2) + i // 2 + 1))
                    for k in range(1, TOPK):
                        link(v.tensor_tensor(y_parts[:, i % 2, 0:D], y_parts[:, i % 2, 0:D], y_parts[:, i % 2, D * k:D * k + D], ALU.add))
                    dve.nop().then_inc(y_summed, 1)
                    for hf in range(2):
                        b = await_full(dve, ("comb", l, t, hf))
                        s = 0 if t < 2 else 1
                        for k in range(4):
                            m = 4 * hf + k
                            xs = xT[:, m, P * t:P * t + P]
                            last = v.scalar_tensor_tensor(out=xs, in0=b[:, P * k:P * k + P], scalar=mod[:, 40 + m, s:s + 1], in1=xs,
                                                          op0=ALU.mult, op1=ALU.add)
                        last.then_inc(emptied["dve"], 1)
            for t in range(2):
                copy_out(("fin", t, 1), fin[:, t, 512:1024])

        @block.gpsimd
        def _(pool):
            pool.dma_start(const[:, :], dram["const"]).then_inc(const_in, 16)
            for s, name in enumerate(("ctx", "x")):
                pool.dma_start(x_in[:, 2 * s:2 * s + 2, :], dram[name].rearrange("o (t p) d -> p (o t) d", p=P)).then_inc(x_loaded, 16)
            for l in range(DEPTH):
                if l:
                    pool.wait_ge(small_used, l)
                vecs = {"c": dram["c"].rearrange("o (k p) -> (o k) p", p=P), "cctx": dram["c_ctx"].rearrange("(k p) -> k p", p=P)}
                for name, src in (("ada_b", "ada_b"), ("n1", "norm1_g"), ("n2", "norm2_g"), ("gng", "ret_gn_g"), ("gnb", "ret_gn_b"),
                                  ("qag", "mla_qa_g"), ("kvag", "mla_kva_g")):
                    vecs[name] = dram[src][l].rearrange("(k p) -> k p", p=P)
                for name, n in VEC_ROWS.items():
                    pool.dma_start(vec_rows[VEC_AT[name]:VEC_AT[name] + n, :], vecs[name]).then_inc(small_loaded, 16)
                for name, src in (("qn", "mla_qn_g"), ("kn", "mla_kn_g"), ("kr", "mla_kr_g"), ("lng", "gmlp_ln_g"), ("lnb", "gmlp_ln_b"),
                                  ("bias", "moe_bias")):
                    pool.dma_start(rows(name), dram[src][l].partition_broadcast(P)).then_inc(small_loaded, 16)
                pool.dma_start(rows("bs"), dram["gmlp_bs"][l].rearrange("g i -> (g i)").partition_broadcast(P)).then_inc(small_loaded, 16)
                pool.dma_start(rows("dec")[:, 0:4], dram["ret_decay_fwd"][l].partition_broadcast(P)).then_inc(small_loaded, 16)
                pool.dma_start(rows("dec")[:, 4:8], dram["ret_decay_bwd"][l].partition_broadcast(P)).then_inc(small_loaded, 16)

                cap = CAP[l]

                def gather(j, done, step):
                    pool.sem_inc(pool_passed, 1)
                    pool.indirect_dma_start(out=x_rows[0:cap, j, :], out_offset=None, in_=h2_dram[0:tokens(l), :],
                                            in_offset=bass.IndirectOffsetOnAxis(ap=idx[0:cap, j, 0:1], axis=0),
                                            bounds_check=tokens(l) - 1, oob_is_err=False).then_inc(done, step)

                def scatter(j, done, step):
                    pool.sem_inc(pool_passed, 1)
                    pool.indirect_dma_start(out=y_dram[0:TOPK * tokens(l), :],
                                            out_offset=bass.IndirectOffsetOnAxis(ap=idx[0:cap, j, 1:2], axis=0),
                                            in_=y_rows[0:cap, j, :], in_offset=None,
                                            bounds_check=TOPK * tokens(l) - 1, oob_is_err=False).then_inc(done, step)

                pool.wait_ge(moe_ready, l + 1)
                for j in range(2):
                    pool.wait_ge(h2_stored[j], 16 * h2_base(l + 1, j))
                for e in range(2):
                    pool.wait_ge(list_read, l * LISTS + e + 1)
                    gather(e, rows_in[e], 16)
                with pool.Fori(0, N_EXP // BODY) as i:
                    for j in range(BODY):
                        e = i * BODY + j
                        j2 = (j + 2) % 3
                        pool.wait_ge(list_read, l * LISTS + e + 3)
                        gather(j2, rows_in[j2], 16)
                        pool.wait_ge(y_act, l * N_EXP + e + 1)
                        pool.wait_ge(y_dve, l * N_EXP + e + 1)
                        scatter(j, rows_out[j], 16)
                pool.wait_ge(y_act, (l + 1) * N_EXP)
                pool.wait_ge(y_dve, (l + 1) * N_EXP)
                scatter(0, rows_out[0], 16)
                for j in range(3):
                    pool.wait_ge(rows_out[j], 16 * ((l + 1) * experts_of[j]))
                    pool.wait_ge(rows_in[j], 16 * (l + 1) * lists_of[j])

                most = pool.value_load(maxcnt[0:1, l:l + 1], min_val=0, max_val=T)
                with pool.If(most > cap):
                    for b in range(1, tokens(l) // cap):
                        with pool.Fori(0, N_EXP) as e:
                            q = (b - 1) * N_EXP + e
                            pool.wait_ge(late_dve[l], 6 * q + 2)
                            gather(0, late_in[l], 16)
                            pool.wait_ge(late_dve[l], 6 * q + 6)
                            scatter(0, late_out[l], 16)
                            pool.wait_ge(late_out[l], 16 * q + 16)
                    
                parts = y_dram[0:TOPK * tokens(l), :].rearrange("(k n) d -> n k d", k=TOPK)
                for i, t in enumerate(main_tiles(l)):
                    if i >= 2:
                        await_full(pool, ("comb", l, main_tiles(l)[i - 2], 1))
                    pool.dma_start(y_parts[:, i % 2, :].rearrange("p (k d) -> p k d", k=TOPK), parts[P * i:P * i + P]).then_inc(y_in[i % 2], 16)


_INS = ["x", "c", "ctx", "c_ctx", "ada_w", "ada_b", "norm1_g", "norm2_g", "w_in", "ret_decay_fwd", "ret_decay_bwd",
        "ret_gn_g", "ret_gn_b", "w_br_ret", "mla_qa_g", "mla_w_uq", "mla_kva_g", "mla_w_ukv", "mla_qn_g", "mla_kn_g",
        "mla_kr_g", "w_br_mla", "gmlp_ln_g", "gmlp_ln_b", "gmlp_ws", "gmlp_bs", "w_br_gmlp", "w_out", "moe_router",
        "moe_bias", "moe_w_gate", "moe_w_up", "moe_w_down", "sh_w_gate", "sh_w_up", "sh_w_down"]


def kernel(**inputs):
    import concourse.bacc as _bacc
    from concourse.bass_utils import run_bass_kernel_spmd as _run

    nc = _bacc.Bacc("TRN2", target_bir_lowering=False, num_devices=1)
    arrays, dram = {}, {}
    for name in _INS + ["const"]:
        a = np.ascontiguousarray(shape_constants() if name == "const" else inputs[name])
        arrays[f"in_{name}"] = a
        dram[name] = nc.dram_tensor(f"in_{name}", a.shape, mybir.dt.from_np(a.dtype), kind="ExternalInput").ap()
    out = nc.dram_tensor("out_x", (1, SEQ, D), F32, kind="ExternalOutput").ap()
    backbone(nc, dram, out)
    r = _run(nc, [arrays], core_ids=[0])
    return r.results[0]["out_x"]
```

```python
from contextlib import ExitStack

import numpy as np

import concourse.bass as bass
from concourse import mybir

F32 = mybir.dt.float32
I32 = mybir.dt.int32
ALU = mybir.AluOpType
ACT = mybir.ActivationFunctionType
AX_X = mybir.AxisListType.X

P = 128
D = 1024
KT = D // P
SEQ = 256
CTX = 256
T = SEQ + CTX
TT = T // P
DEPTH = 2
EPS = 1e-6

HEADS_R = 4
RW = HEADS_R * P
HEADS_M = 8
QL, KVL, NOPE, ROPE, VD = 384, 256, 64, 32, 64
QK = NOPE + ROPE
CW = QL + KVL + ROPE
GW = 512
OFF_Q, OFF_K, OFF_V, OFF_G = 0, RW, 2 * RW, 3 * RW
OFF_C = 4 * RW
OFF_U = OFF_C + CW
OFF_GV = OFF_U + GW
OFF_MERGE = OFF_GV + GW
N_EXP, TOPK, FF = 64, 6, 256
ROUTED_SCALE = 2.5

NS = 9
SLOT = 2048
BODY = 3
CAP = [128, 64]
BIG = 8192.0
PE_ROWS = 4
FIRST = 0

VEC_ROWS = {"ada_b": 48, "n1": 8, "n2": 8, "gng": 4, "gnb": 4, "qag": 3, "kvag": 2, "c": 8, "cctx": 8}
ROW_BC = {"qn": QK, "kn": NOPE, "kr": ROPE, "lng": GW, "lnb": GW, "bs": GW, "bias": N_EXP, "dec": 8}
CONST_COLS = {"ident": P, "iota1": P, "diff": 384, "tri": P, "tok": 8, "cos": 2 * ROPE, "sin": 2 * ROPE, "sel": 2}


def offsets(sizes):
    at, out = 0, {}
    for name, n in sizes.items():
        out[name] = at
        at += n
    return out, at


N_VEC_LOADS, N_ROW_LOADS = DEPTH * (len(VEC_ROWS) - 2) + 2, len(ROW_BC) + 1
VEC_AT, N_VEC = offsets(VEC_ROWS)
VEC_OF = [N_VEC] + [VEC_AT["c"]] * (DEPTH - 1)
ROW_AT, N_ROW = offsets(ROW_BC)
CONST_AT, N_CONST = offsets(CONST_COLS)


def shape_constants():
    out = np.zeros((P, N_CONST), np.float32)

    def put(name, a):
        out[:, CONST_AT[name]:CONST_AT[name] + CONST_COLS[name]] = a

    p = np.arange(P)
    put("ident", np.eye(P))
    put("iota1", np.broadcast_to(np.arange(P) + 1, (P, P)))
    put("diff", np.arange(384)[None, :] - P - p[:, None])
    put("tri", (p[:, None] < p[None, :]))
    put("sel", (p[:, None] % 32 == np.arange(2)[None, :]))
    tok = np.arange(TT)[None, :] * P + p[:, None] - BIG
    put("tok", np.concatenate([tok, tok - CTX], 1))
    t = np.arange(SEQ)
    nf = ROPE // 4
    inv = (np.float32(10000.0) ** (np.float32(-2.0) * np.arange(nf, dtype=np.float32) / np.float32(ROPE // 2)))
    row = (t // 64).astype(np.float32)[:, None] * inv.astype(np.float32)
    col = (t % 64).astype(np.float32)[:, None] * inv.astype(np.float32)
    cos = np.concatenate([np.cos(row), np.cos(row), np.cos(col), np.cos(col)], 1)
    sin = np.concatenate([-np.sin(row), np.sin(row), -np.sin(col), np.sin(col)], 1)
    put("cos", cos.reshape(2, P, ROPE).transpose(1, 0, 2).reshape(P, 2 * ROPE))
    put("sin", sin.reshape(2, P, ROPE).transpose(1, 0, 2).reshape(P, 2 * ROPE))
    return out


def main_tiles(l):
    return list(range(TT)) if l < DEPTH - 1 else list(range(CTX // P, TT))


def streams(l):
    return [0, 1] if l < DEPTH - 1 else [1]


def ret_units(l):
    return [(h, s) for h in range(HEADS_R) for s in streams(l)]


def att_units(l):
    return [(t, h) for t in main_tiles(l) for h in range(HEADS_M)]


def spread(chain, bulk):
    out, done = [], 0
    for i, step in enumerate(chain):
        out.append(step)
        upto = (i + 1) * len(bulk) // len(chain)
        out += bulk[done:upto]
        done = upto
    return out


def ada_steps(l, qs):
    return [(kind, l, q) for q in qs for kind in ("adaw", "adat")]


def weave(a, b):
    return spread(a, b) if len(a) >= len(b) else spread(b, a)


def layer_steps(l):
    mt = main_tiles(l)
    out = []
    latents = [[("c", j, t) for j in range(3) if j or t in mt] + [("cnorm", t)] for t in range(TT)]
    heads = [[("turn_c", t)] + [("turn_qk", t - 1)] * (t > 0) + [("project", t)] for t in range(TT)]
    if l == 0:
        ada = ada_steps(0, list(range(4)))
        out += [("vec",)] + ada[:2] + [("x", 0), ("x", 1)] + ada[2:4] + [("x", 2), ("x", 3), ("ms1", 0)] + ada[4:6]
        out += [("ms1", 1)] + ada[6:] + [("norm", 0), ("norm", 1)]
    else:
        out += [("comb", l - 1, 0), ("comb", l - 1, 1), ("ms1", 0), ("norm", 0)]
        out += [("comb", l - 1, 2), ("comb", l - 1, 3), ("ms1", 1), ("norm", 1)]
    out += latents[0] + latents[1] + heads[0] + latents[2] + heads[1] + latents[3]
    bulk = [("ws",)] + [("u", g) for g in range(4)] + [("gv", j, t) for j in range(2) for t in mt]
    n = len(bulk)
    out += bulk[:n // 3] + heads[2] + bulk[n // 3:2 * n // 3] + heads[3] + bulk[2 * n // 3:] + [("turn_qk", TT - 1)]
    out += [("gnorm",)]
    att = [("att", n) for n in range(len(att_units(l)) + 2)]
    bulk = [("merge", m, 2) for m in range(8)]
    if l == 0:
        bulk = weave(ada_steps(0, list(range(4, 12))), bulk)
    out += att[:4] + [("sv", t) for t in mt] + spread(att[4:], bulk)
    out += [("decay", 0)] + [("q", h) for h in range(4)] + [("decay", 1)] + [("k", h) for h in range(4)]
    out += [("v", j, t) for j in range(2) for t in range(TT)] + [("g", h) for h in range(4)]
    bulk = [("merge", m, 1) for m in range(8)]
    if l + 1 < DEPTH:
        bulk = weave(ada_steps(l + 1, list(range(12))), bulk)
    out += spread([("ret", n) for n in range(len(ret_units(l)) + 2)], bulk)
    out += [("merge", m, 0) for m in range(8)]
    out += [("out", m) for m in range(8)] + [("ms2",), ("norm", 2), ("rt",)] + [("h2", t) for t in mt]
    out += [("sg", m) for m in range(2)] + [("pos",), ("cnt",)] + [("su", m) for m in range(2)]
    out += [("list", e) for e in range(2)] + [("sd", m) for m in range(8)]
    return out


def last_steps():
    return [("comb", DEPTH - 1, t) for t in main_tiles(DEPTH - 1)] + [("fin", t) for t in range(2)]


def step_jobs(l, kind, *a):
    mt = main_tiles(l)
    if kind == "vec":
        return [(("vec", i), "dve") for i in range(DEPTH)]
    if kind == "x":
        return [(("x", a[0], 0), "act"), (("x", a[0], 1), "dve")]
    if kind == "adaw":
        return [(("adaw",) + a, "act")]
    if kind == "adat":
        return [(("adat",) + a, "dve")]
    if kind == "turn_c":
        return [(("ct", l, a[0], i), "act") for i in range(2) if i or a[0] in mt]
    if kind == "project":
        return [((name, l, a[0], hf), "dve") for name in ("qp", "kvp") for hf in range(2) if name == "kvp" or a[0] in mt]
    if kind == "turn_qk":
        return [((name, l, a[0], hf), "act") for name in ("qt", "kt") for hf in range(2) if name == "kt" or a[0] in mt]
    if kind == "ret":
        n, ru = a[0], ret_units(l)
        out = [(("s", l, n, pr), "dve") for pr in range(1 + ru[n][1])] if n < len(ru) else []
        if 0 <= n - 1 < len(ru):
            out += [(("o", l, n - 1), "dve")]
        if n >= 2:
            out += [(("ot", l, n - 2), "dve")]
        return out
    if kind == "att":
        n, au = a[0], att_units(l)
        out = [(("S", l, n), "act")] if n < len(au) else []
        if 0 <= n - 1 < len(au):
            out += [(("PT", l, n - 1), "dve")]
        if n >= 2:
            out += [(("pv", l, n - 2), "dve")]
            if au[n - 2][1] == HEADS_M - 1:
                out += [(("omt", l, au[n - 2][0]), "act")]
        return out
    if kind == "merge":
        return [(("gate", l) + a, "act"), (("y", l) + a, "dve")]
    if kind in ("h2", "fin"):
        return [((kind, l, a[0], hf), "act") for hf in range(2)]
    if kind == "comb":
        return [((kind,) + a + (hf,), "dve") for hf in range(2)]
    if kind in ("decay", "cnorm", "gnorm", "norm"):
        return []
    return [((kind, l) + a, "act" if kind in ("q", "k", "g", "ws", "u", "gv", "rt", "sg", "ms1", "ms2") else "dve")]


def step_pieces(l, kind, *a):
    if kind == "adaw":
        return [(a[0], "ada", 2 * a[1] + i) for i in range(2)]
    if kind == "c":
        return [(l, ("cA", "cB", "cC")[a[0]])]
    if kind == "project":
        return [(l, "uqA"), (l, "uqB"), (l, "ukv")]
    if kind in ("q", "k", "g"):
        return [(l, "r" + kind, a[0] // 2)]
    if kind == "v":
        return [(l, "rv", a[0])]
    if kind == "u":
        return [(l, "u", a[0] // 2)]
    if kind == "gv":
        return [(l, "gv", a[0])]
    if kind == "merge":
        return [(l, "gate", a[0] // 2, a[1]), (l, "br", a[0] // 2, a[1])]
    if kind == "out":
        return [(l, "wo", a[0] // 2)]
    return {"ws": [(l, "ws")], "rt": [(l, "router")], "sg": [(l, "sg")], "su": [(l, "su")], "sd": [(l, "sd")]}.get(kind, [])


def backbone(nc, dram, out):
    jobs, pieces, first_use, last_use, moe_at, start_at = [], [], {}, {}, [], []
    for l in range(DEPTH):
        start_at.append(len(pieces))
        for step in layer_steps(l):
            for piece in step_pieces(l, *step):
                if piece not in first_use:
                    first_use[piece] = len(jobs)
                    pieces.append(piece)
            jobs += step_jobs(l, *step)
            for piece in step_pieces(l, *step):
                last_use[piece] = len(jobs) - 1
        moe_at.append(len(pieces))
        pieces += [(l, kind, e) for e in range(N_EXP) for kind in ("expert_gate", "expert_up", "expert_down")]
    for step in last_steps():
        jobs += step_jobs(DEPTH, *step)
    job_at = {k: n for n, (k, _) in enumerate(jobs)}
    piece_at = {k: n for n, k in enumerate(pieces)}
    assert len(job_at) == len(jobs) and len(piece_at) == len(pieces)
    for p in range(len(pieces) - NS):
        if pieces[p] in last_use and pieces[p + NS] in first_use:
            assert first_use[pieces[p + NS]] > last_use[pieces[p]], (pieces[p], pieces[p + NS])
    emptied_before = {"act": [0], "dve": [0]}
    for _, e in jobs:
        for k in emptied_before:
            emptied_before[k].append(emptied_before[k][-1] + (k == e))

    h2_dram = nc.dram_tensor("h2_rows", (T, D), F32, kind="Internal").ap()
    y_dram = nc.dram_tensor("expert_rows", (TOPK * T, D), F32, kind="Internal").ap()

    with ExitStack() as ctx:
        def sb(name, shape, dt=F32):
            return ctx.enter_context(nc.sbuf_tensor(name, shape, dt))

        def sem(name):
            return ctx.enter_context(nc.semaphore(name))

        ring = sb("ring", [P, NS, SLOT])
        xT = sb("xT", [P, KT, T])
        hT = sb("hT", [P, KT, T])
        const = sb("const", [P, N_CONST])
        ones = sb("ones", [P, P])
        vec = sb("vec", [P, DEPTH, N_VEC])
        row_bc = sb("row_bc", [P, N_ROW])
        silu_c = sb("silu_c", [P, KT, 32])
        ada_row = sb("ada_row", [P, 512])
        mod = sb("mod", [P, DEPTH, 48, 2])
        gain1 = sb("gain1", [P, DEPTH, KT, 2])
        gain2 = sb("gain2", [P, DEPTH, KT, 2])
        half_gate = sb("half_gate", [P, DEPTH, KT, 2])
        lg = sb("lg", [P, 64])
        stat = sb("stat", [P, 128])
        eps_col = sb("eps_col", [P, 3])
        idx = sb("idx", [P, 3, 3], I32)
        wrow = sb("wrow", [P, 3])
        maxcnt = sb("maxcnt", [P, 2], I32)
        counts = sb("counts", [P, N_EXP + 2], I32)
        AREA = 22016
        area = sb("area", [P, AREA])
        bank = [ctx.enter_context(nc.psum_tensor(f"bank{i}", [P, 512], F32)) for i in range(8)]

        def region(at, *dims):
            n = int(np.prod(dims))
            assert at + n <= AREA, (at, n)
            v = area[:, at:at + n]
            if len(dims) == 2:
                return v.rearrange("p (a b) -> p a b", a=dims[0])
            if len(dims) == 3:
                return v.rearrange("p (a b c) -> p a b c", a=dims[0], b=dims[1])
            return v

        def const_cols(name):
            return const[:, CONST_AT[name]:CONST_AT[name] + CONST_COLS[name]]

        def vcol(l, name, i):
            at = VEC_AT[name] + i
            return vec[:, l, at:at + 1]

        def rows(name):
            return row_bc[:, ROW_AT[name]:ROW_AT[name] + ROW_BC[name]]

        ident = const_cols("ident")
        y_mla = region(12800, 4, T)
        merged = region(14848, KT, T)
        gate_t = region(18944, 2, 512)
        y_gmlp = region(19968, 4, T)
        qT = region(0, HEADS_M, T)
        kT = region(4096, HEADS_M, T)
        mv = region(8192, TT, HEADS_M * VD)
        probs = region(10240, 2, 512)
        probsT = region(11264, 2, 512)
        o_tok = region(12288, 512)
        lat_c = region(10240, TT, CW)
        q_tok = region(12928, HEADS_M, QK)
        k_tok = region(13696, HEADS_M, QK)
        sq_tok = region(14464, 2, 512)
        ckT = region(15488, 2, P)
        cqT = region(15744, 3, P)
        rope_t = region(16128, HEADS_M, ROPE)
        rope_u = region(16384, HEADS_M, ROPE)
        gv = region(16640, TT, GW)
        wsT = region(18688, 4, P)
        sv_tmp = region(19200, 512)
        decay = region(0, 2, 4, 384)
        rqT = region(3072, 4, T)
        rkT = region(5120, 4, T)
        rv = region(7168, TT, RW)
        att = region(9216, 2, 4, 256)
        decay_b = region(9216, 4, 384)
        on = region(11264, 2, 256)
        tmp_ret = region(11776, 2, 256)
        prod_t = region(12288, 512)
        y_ret = region(19968, 4, T)
        x_in = region(0, TT, D)
        vec_rows = region(4096, DEPTH, P)
        c_sq = [region(19456, 512), region(12928, 512)]
        sq_1 = region(9216, 2, CTX)
        sq_2 = region(8192, 2, T)
        rstd = region(9728, T)
        x_rows = region(0, 3, D)
        x_rowsT = region(3072, 3, KT * P)
        y_rows = region(6144, 3, D)
        pick = region(9216, 3, TT * P)
        act_g = region(10752, 3, FF)
        hid = region(11520, 3, FF)
        hidT = region(12288, 3, 2 * P)
        pos1 = region(13056, TT, N_EXP + 2)
        table = area[:, 13320:13320 + TT * (N_EXP + 2) * 3].rearrange("p (t e c) -> p t e c", t=TT, c=3)
        R0 = 14112
        score = region(R0, TT, N_EXP)
        sel = region(R0 + 256, TT, N_EXP)
        mask = region(R0 + 512, TT, N_EXP)
        eq = region(R0 + 768, TT, N_EXP)
        cum = region(R0 + 1024, TT, N_EXP)
        top8 = region(R0 + 1280, TT, 8)
        need = region(R0 + 1312, TT)
        wsum = region(R0 + 1316, TT)
        kslot = region(R0 + 1344, TT, N_EXP)
        one64 = region(R0 + 1600, N_EXP)
        h2_tok = region(R0 + 1664, 2, D)
        shT = region(R0 + 3712, 2, T)
        sil_s = region(R0 + 4736, 2, T)
        late_w = region(R0, 3, SLOT)
        y_parts = [region(0, TOPK * D), region(15872, TOPK * D)]
        fin = region(0, 2, D)

        piece_loaded = [sem(f"piece_loaded{s}") for s in range(NS)]
        bank_full = sem("bank_full")
        emptied = {"act": sem("emptied_by_act"), "dve": sem("emptied_by_dve")}
        const_in = sem("const_in")
        x_loaded = sem("x_loaded")
        vec_loaded = sem("vec_loaded")
        rows_loaded = sem("rows_loaded")
        small_used = sem("small_used")
        ones_ready = sem("ones_ready")
        pe_passed = sem("pe_passed")
        pool_passed = sem("pool_passed")
        dve_passed = sem("dve_passed")
        root_asked = sem("root_asked")
        roots = sem("roots")
        late_iota = [sem(f"late_iota{l}") for l in range(DEPTH)]
        act_step = sem("act_step")
        dve_step = sem("dve_step")
        silu_ready = sem("silu_ready")
        sq_ready = sem("sq_ready")
        gained = sem("gained")
        h_ready = sem("h_ready")
        sq_used = sem("sq_used")
        y_gmlp_ready = sem("y_gmlp_ready")
        decay_arg = sem("decay_arg")
        decay_ready = sem("decay_ready")
        lg_exp = sem("lg_exp")
        lg_arg = sem("lg_arg")
        c_squared = sem("c_squared")
        c_normed = sem("c_normed")
        qk_squared = sem("qk_squared")
        on_ready = sem("on_ready")
        qk_tok_ready = sem("qk_tok_ready")
        neg_max = sem("neg_max")
        gv_normed = sem("gv_normed")
        merged_ready = sem("merged_ready")
        h2_stored = [sem(f"h2_stored{j}") for j in range(2)]
        moe_ready = sem("moe_ready")
        mask_ready = sem("mask_ready")
        sh_ready = sem("sh_ready")
        pick_ready = sem("pick_ready")
        list_full = sem("list_full")
        list_read = sem("list_read")
        rows_in = [sem(f"rows_in{j}") for j in range(3)]
        rows_turned = sem("rows_turned")
        turned_act = sem("turned_act")
        turned_dve = sem("turned_dve")
        gu_full = sem("gu_full")
        silu_done = sem("silu_done")
        hid_ready = sem("hid_ready")
        hidT_full = sem("hidT_full")
        hidT_ready = sem("hidT_ready")
        down_full = sem("down_full")
        y_act = sem("y_act")
        y_dve = sem("y_dve")
        rows_out = [sem(f"rows_out{j}") for j in range(3)]
        y_in = [[sem(f"y_in{j}_{k}") for k in range(TOPK)] for j in range(2)]
        y_summed = sem("y_summed")
        late_loaded = [sem(f"late_loaded{l}") for l in range(DEPTH)]
        late_in = [sem(f"late_in{l}") for l in range(DEPTH)]
        late_out = [sem(f"late_out{l}") for l in range(DEPTH)]
        late_pe = [sem(f"late_pe{l}") for l in range(DEPTH)]
        late_dve = [sem(f"late_dve{l}") for l in range(DEPTH)]
        late_act = [sem(f"late_act{l}") for l in range(DEPTH)]
        stored = sem("stored")

        block = ctx.enter_context(nc.Block())

        def await_loaded(eng, p):
            eng.wait_ge(piece_loaded[p % NS], 16 * (p // NS + 1))

        def await_full(eng, key):
            eng.wait_ge(bank_full, job_at[key] + 1)
            return bank[job_at[key] % 8]

        def await_emptied(eng, key):
            n = job_at[key]
            e = jobs[n][1]
            eng.wait_ge(emptied[e], emptied_before[e][n + 1])

        def open_bank(pe, key):
            n = job_at[key]
            if n >= 8:
                await_emptied(pe, jobs[n - 8][0])
            return bank[n % 8]

        def norm_at(key):
            return 3 * key[1] + (2 if key[0] == "ms2" else key[2])

        def norm_before(key):
            if key[0] == "ms2":
                return ("ms1", key[1], 1)
            return ("ms1", key[1], 0) if key[2] else ("ms2", key[1] - 1)

        def norm_streams(key):
            return streams(key[1]) if key[0] == "ms2" else [key[2]]

        def norm_cols(key):
            s = norm_streams(key)
            return CTX * s[0], CTX * s[-1] + CTX

        def c0(l):
            return 0 if l < DEPTH - 1 else CTX

        def tokens(l):
            return P * len(main_tiles(l))

        def before(l, per_layer):
            return sum(per_layer(i) for i in range(l))

        def h2_base(l, buf):
            return before(l, lambda i: (len(main_tiles(i)) + 1 - buf) // 2)

        def span(l, s, t0=0):
            return slice(CTX * s - t0, CTX * s + CTX - t0)

        experts = BODY * (N_EXP // BODY)
        LISTS, PICKS = N_EXP + 1, N_EXP + 2
        lists_of = [len(range(j, LISTS, 3)) for j in range(3)]
        experts_of = [len(range(j, N_EXP, 3)) for j in range(3)]

        def few(eng, e, cap):
            at = slice(e, e + 1) if isinstance(e, int) else bass.ds(e, 1)
            return eng.value_load(counts[0:1, at], min_val=0, max_val=T) <= cap // 2

        def by_size(eng, passed, l, e, halves, whole):
            if CAP[l] < P:
                return halves()
            eng.sem_inc(passed, 1)
            with eng.If(few(eng, e, P)):
                halves()
            with eng.Else():
                whole()

        def slot_of(p):
            return ring[:, p % NS, :]

        def piece_view(p, a, b):
            return ring[:, p % NS, 0:a * b].rearrange("p (a b) -> p a b", a=a)

        def src_and_dst(p):
            l, kind, *r = pieces[p]
            w_in = dram["w_in"][l].rearrange("(k p) n -> p k n", p=P)

            def cols(at, n):
                return w_in[:, :, at:at + n], piece_view(p, KT, n)

            if kind == "ada":
                return dram["ada_w"][l].rearrange("(k p) n -> p k n", p=P)[:, :, 256 * r[0]:256 * r[0] + 256], piece_view(p, KT, 256)
            if kind == "cA":
                return cols(OFF_C, 256)
            if kind == "cB":
                return cols(OFF_C + 256, 256)
            if kind == "cC":
                return cols(OFF_C + 512, CW - 512)
            if kind in ("rq", "rk", "rv", "rg", "u", "gv"):
                at = {"rq": OFF_Q, "rk": OFF_K, "rv": OFF_V, "rg": OFF_G, "u": OFF_U, "gv": OFF_GV}[kind]
                return cols(at + 256 * r[0], 256)
            if kind == "uqA":
                return dram["mla_w_uq"][l, 0:256].rearrange("(k p) n -> p k n", p=P), piece_view(p, 2, HEADS_M * QK)
            if kind == "uqB":
                return dram["mla_w_uq"][l, 256:384], slot_of(p)[:, 0:HEADS_M * QK]
            if kind == "ukv":
                return dram["mla_w_ukv"][l].rearrange("(k p) n -> p k n", p=P), piece_view(p, 2, D)
            if kind == "ws":
                return dram["gmlp_ws"][l].rearrange("g i j -> i g j"), piece_view(p, 4, P)
            if kind == "gate":
                return cols(OFF_MERGE + D * r[1] + 256 * r[0], 256)
            if kind == "br":
                w = dram[("w_br_ret", "w_br_mla", "w_br_gmlp")[r[1]]][l]
                return w.rearrange("(k p) n -> p k n", p=P)[:, :, 256 * r[0]:256 * r[0] + 256], piece_view(p, 4, 256)
            if kind == "wo":
                return dram["w_out"][l].rearrange("(k p) n -> p k n", p=P)[:, :, 256 * r[0]:256 * r[0] + 256], piece_view(p, KT, 256)
            if kind == "router":
                return dram["moe_router"][l].rearrange("(k p) n -> p k n", p=P), piece_view(p, KT, N_EXP)
            if kind in ("sg", "su"):
                return dram["sh_w_gate" if kind == "sg" else "sh_w_up"][l].rearrange("(k p) n -> p k n", p=P), piece_view(p, KT, FF)
            assert kind == "sd"
            return dram["sh_w_down"][l].rearrange("(k p) n -> p k n", p=P), piece_view(p, 2, D)

        def expert_src(l, kind, e):
            name = ("moe_w_gate", "moe_w_up", "moe_w_down")[kind]
            w = dram[name][l, e] if isinstance(e, int) else dram[name][l, bass.ds(e, 1)].rearrange("o a b -> (o a) b")
            return w.rearrange("(p k) n -> p (k n)", p=P)

        @block.sync
        def _(sp):
            sp.wait_ge(vec_loaded, 16 * N_VEC_LOADS)

            def await_free(p):
                l, kind, *r = pieces[p]
                if kind in ("expert_gate", "expert_up"):
                    sp.wait_ge(gu_full, N_EXP * l + r[0] + 1)
                elif kind == "expert_down":
                    sp.wait_ge(down_full, N_EXP * l + r[0] + 1)
                else:
                    sp.wait_ge(bank_full, last_use[pieces[p]] + 1)

            def load_expert(l, e, j, i):
                for kind in range(3):
                    p = moe_at[l] + 3 * j + kind
                    sp.wait_ge(down_full if kind == 2 else gu_full, N_EXP * l + e - BODY + 1)
                    sp.dma_start(slot_of(p), expert_src(l, kind, e)).then_inc(piece_loaded[p % NS], 16)

            for l in range(DEPTH):
                for p in range(start_at[l], moe_at[l] + 3 * BODY):
                    if p >= NS:
                        await_free(p - NS)
                    if p < moe_at[l]:
                        src, dst = src_and_dst(p)
                    else:
                        e, kind = divmod(p - moe_at[l], 3)
                        src, dst = expert_src(l, kind, e), slot_of(p)
                    sp.dma_start(dst, src).then_inc(piece_loaded[p % NS], 16)
                with sp.Fori(1, N_EXP // BODY) as i:
                    for j in range(BODY):
                        load_expert(l, i * BODY + j, j, i)
                load_expert(l, experts, 0, N_EXP // BODY)

                sp.wait_ge(moe_ready, l + 1)
                await_emptied(sp, ("sd", l, 7))
                sp.wait_ge(h2_stored[0], 16 * h2_base(l + 1, 0))
                sp.wait_ge(h2_stored[1], 16 * h2_base(l + 1, 1))
                most = sp.value_load(maxcnt[0:1, l:l + 1], min_val=0, max_val=T)
                for b in range(1, tokens(l) // CAP[l]):
                    with sp.If(most > b * CAP[l]):
                        with sp.Fori(0, N_EXP) as e:
                            q = (b - 1) * N_EXP + e
                            sp.wait_ge(late_dve[l], 6 * q + 1)
                            for kind in range(3):
                                sp.dma_start(late_w[:, kind, :], expert_src(l, kind, e)).then_inc(late_loaded[l], 16)

        @block.tensor
        def _(pe):
            mm = nc.tensor.matmul

            def turn(dst, src, n=P):
                return nc.tensor.transpose(dst, src, ident[0:n, 0:n])

            def feature_job(key, lhs, rhs, c, n):
                b = open_bank(pe, key)
                K = lhs.shape[1]
                for k in range(K):
                    last = mm(b[:, 0:n], lhs[:, k, :], rhs[:, k, c:c + n], start=(k == 0), stop=(k == K - 1))
                last.then_inc(bank_full, 1)

            def token_job(key, lhs, tt, rhs, n):
                b = open_bank(pe, key)
                K = rhs.shape[1]
                for k in range(K):
                    last = mm(b[:, 0:n], lhs[:, k, P * tt:P * tt + P], rhs[:, k, :], start=(k == 0), stop=(k == K - 1))
                last.then_inc(bank_full, 1)

            def entry(i, e):
                if isinstance(e, int):
                    return table[:, i, e, :]
                return table[:, i, bass.ds(e, 1), :].rearrange("p o c -> p (o c)")

            def mean_square(key, ks):
                lo, hi = norm_cols(key)
                for k in ks:
                    b = open_bank(pe, key)
                    pe.wait_ge(sq_ready, KT * norm_at(key) + k + 1)
                    last = mm(b[:, 0:hi - lo], ones[:, :], (sq_2 if key[0] == "ms2" else sq_1)[:, k % 2, 0:hi - lo], start=(k == 0), stop=(k == KT - 1))
                    last.then_inc(*((bank_full, 1) if k == KT - 1 else (sq_used, 1)))

            def step_comb(l, t):
                i = t - main_tiles(l)[0]
                b = [open_bank(pe, ("comb", l, t, hf)) for hf in range(2)]
                for k in range(PE_ROWS + 1):
                    if k < PE_ROWS:
                        pe.wait_ge(y_in[i % 2][k], 16 * (h2_base(l, i % 2) + i // 2 + 1))
                    else:
                        pe.wait_ge(y_summed, before(l, lambda i: len(main_tiles(i))) + i + 1)
                    for m in range(KT):
                        hf, at = divmod(m, 4)
                        last = mm(b[hf][:, P * at:P * at + P], y_parts[i % 2][:, D * k + P * m:D * k + P * m + P], ident,
                                  start=(k == 0 and at == 0), stop=(k == PE_ROWS), skip_group_check=True)
                        if k == PE_ROWS and at == 3:
                            last.then_inc(bank_full, 1)

            for l in range(DEPTH):
                mt, t0 = main_tiles(l), c0(l)
                nt = T - t0
                ru, au = ret_units(l), att_units(l)

                def step_vec():
                    pe.wait_ge(const_in, 16)
                    pe.wait_ge(vec_loaded, 16 * N_VEC_LOADS)
                    for i in range(DEPTH):
                        b = open_bank(pe, ("vec", i))
                        turn(b[:, 0:VEC_OF[i]], vec_rows[0:VEC_OF[i], i, :], VEC_OF[i]).then_inc(bank_full, 1)

                def step_x(t):
                    pe.wait_ge(x_loaded, 32)
                    for hf in range(2):
                        b = open_bank(pe, ("x", t, hf))
                        for k in range(4):
                            last = turn(b[:, P * k:P * k + P], x_in[:, t, P * (4 * hf + k):P * (4 * hf + k) + P])
                        last.then_inc(bank_full, 1)

                def step_adaw(la, q):
                    pe.wait_ge(silu_ready, 1)
                    b = open_bank(pe, ("adaw", la, q))
                    for i in range(2):
                        p = piece_at[(la, "ada", 2 * q + i)]
                        await_loaded(pe, p)
                        for k in range(KT):
                            g = 32 * (k % 4)
                            last = mm(b[g:g + 32, 256 * i:256 * i + 256], silu_c[:, k, :], piece_view(p, KT, 256)[:, k, :],
                                      start=(k < 4), stop=(k >= 4))
                    last.then_inc(bank_full, 1)

                def step_adat(la, q):
                    b = open_bank(pe, ("adat", la, q))
                    await_emptied(pe, ("adaw", la, q))
                    for m in range(4):
                        last = mm(b[:, 2 * m:2 * m + 2], ada_row[:, P * m:P * m + P], const_cols("sel"), start=True, stop=True)
                    last.then_inc(bank_full, 1)

                def step_ms1(s):
                    pe.wait_ge(ones_ready, 1)
                    mean_square(("ms1", l, s), range(KT))

                def step_c(j, t):
                    pe.wait_ge(h_ready, norm_at(("ms1", l, t // 2)) + 1)
                    p = piece_at[(l, ("cA", "cB", "cC")[j])]
                    await_loaded(pe, p)
                    n = 256 if j < 2 else CW - 512
                    token_job(("c", l, j, t), hT, t, piece_view(p, KT, n), n)

                def step_turn_c(t):
                    pe.wait_ge(c_normed, TT * l + t + 1)
                    if t in mt:
                        b = open_bank(pe, ("ct", l, t, 0))
                        for k in range(3):
                            last = turn(b[:, P * k:P * k + P], lat_c[:, t, P * k:P * k + P])
                        last.then_inc(bank_full, 1)
                    b = open_bank(pe, ("ct", l, t, 1))
                    for k in range(2):
                        last = turn(b[:, P * k:P * k + P], lat_c[:, t, QL + P * k:QL + P * k + P])
                    last.then_inc(bank_full, 1)

                def step_project(t):
                    pa, pb_, pk = piece_at[(l, "uqA")], piece_at[(l, "uqB")], piece_at[(l, "ukv")]
                    for p in (pa, pb_, pk):
                        await_loaded(pe, p)
                    wa, wb, wk = piece_view(pa, 2, 768), slot_of(pb_), piece_view(pk, 2, D)
                    if t in mt:
                        await_emptied(pe, ("ct", l, t, 0))
                        for hf in range(2):
                            b = open_bank(pe, ("qp", l, t, hf))
                            for k in range(3):
                                w = wa[:, k, 384 * hf:384 * hf + 384] if k < 2 else wb[:, 384 * hf:384 * hf + 384]
                                last = mm(b[:, 0:384], cqT[:, k, :], w, start=(k == 0), stop=(k == 2))
                            last.then_inc(bank_full, 1)
                    await_emptied(pe, ("ct", l, t, 1))
                    for hf in range(2):
                        b = open_bank(pe, ("kvp", l, t, hf))
                        for k in range(2):
                            last = mm(b[:, :], ckT[:, k, :], wk[:, k, 512 * hf:512 * hf + 512], start=(k == 0), stop=(k == 1))
                        last.then_inc(bank_full, 1)

                def step_turn_qk(t):
                    pe.wait_ge(qk_tok_ready, TT * l + t + 1)
                    for name, src in (("qt", q_tok), ("kt", k_tok)):
                        if name == "qt" and t not in mt:
                            continue
                        for hf in range(2):
                            b = open_bank(pe, (name, l, t, hf))
                            for i in range(4):
                                last = turn(b[0:QK, P * i:P * i + P], src[:, 4 * hf + i, :])
                            last.then_inc(bank_full, 1)

                def step_att(n):
                    if n < len(au):
                        t, h = au[n]
                        nk = T if t >= 2 else CTX
                        if n == 0:
                            await_emptied(pe, ("kt", l, TT - 1, 1))
                        b = open_bank(pe, ("S", l, n))
                        mm(b[:, 0:nk], qT[0:QK, h, P * t:P * t + P], kT[0:QK, h, 0:nk], start=True, stop=True).then_inc(bank_full, 1)
                    if 0 <= n - 1 < len(au):
                        t, h = au[n - 1]
                        nk = T if t >= 2 else CTX
                        b = open_bank(pe, ("PT", l, n - 1))
                        await_emptied(pe, ("S", l, n - 1))
                        for j in range(nk // P):
                            last = turn(b[:, P * j:P * j + P], probs[:, (n - 1) % 2, P * j:P * j + P])
                        last.then_inc(bank_full, 1)
                    if n >= 2:
                        t, h = au[n - 2]
                        nk = T if t >= 2 else CTX
                        b = open_bank(pe, ("pv", l, n - 2))
                        await_emptied(pe, ("PT", l, n - 2))
                        for j in range(nk // P):
                            last = mm(b[:, 0:VD], probsT[:, (n - 2) % 2, P * j:P * j + P], mv[:, j, VD * h:VD * h + VD],
                                      start=(j == 0), stop=(j == nk // P - 1))
                        last.then_inc(bank_full, 1)
                        if h == HEADS_M - 1:
                            b = open_bank(pe, ("omt", l, t))
                            await_emptied(pe, ("pv", l, n - 2))
                            for k in range(4):
                                last = turn(b[:, P * k:P * k + P], o_tok[:, P * k:P * k + P])
                            last.then_inc(bank_full, 1)

                def step_ws():
                    p = piece_at[(l, "ws")]
                    await_loaded(pe, p)
                    b = open_bank(pe, ("ws", l))
                    for g in range(4):
                        last = turn(b[:, P * g:P * g + P], piece_view(p, 4, P)[:, g, :])
                    last.then_inc(bank_full, 1)

                def step_gv(j, t):
                    p = piece_at[(l, "gv", j)]
                    await_loaded(pe, p)
                    token_job(("gv", l, j, t), hT, t, piece_view(p, KT, 256), 256)

                def step_sv(t):
                    b = open_bank(pe, ("sv", l, t))
                    await_emptied(pe, ("ws", l))
                    pe.wait_ge(gv_normed, before(l, lambda i: len(main_tiles(i))) + t - mt[0] + 1)
                    for g in range(4):
                        last = mm(b[:, P * g:P * g + P], gv[:, t, P * g:P * g + P], wsT[:, g, :], start=True, stop=True)
                    last.then_inc(bank_full, 1)

                def step_merge(m, br):
                    pg, pw = piece_at[(l, "gate", m // 2, br)], piece_at[(l, "br", m // 2, br)]
                    await_loaded(pe, pg)
                    i = P * (m % 2)
                    feature_job(("gate", l, m, br), piece_view(pg, KT, 256)[:, :, i:i + P], hT, t0, nt)
                    await_loaded(pe, pw)
                    if m == 0 and br == 2:
                        pe.wait_ge(y_gmlp_ready, before(l, lambda i: len(main_tiles(i))) + len(mt))
                    elif m == 0:
                        await_emptied(pe, ("omt", l, TT - 1) if br else ("ot", l, len(ru) - 1))
                    feature_job(("y", l, m, br), piece_view(pw, 4, 256)[:, :, i:i + P], (y_ret, y_mla, y_gmlp)[br], t0, nt)

                def step_v(j, t):
                    p = piece_at[(l, "rv", j)]
                    await_loaded(pe, p)
                    token_job(("v", l, j, t), hT, t, piece_view(p, KT, 256), 256)

                def projection(kind):
                    def step(m):
                        p = piece_at[(l, kind if kind == "u" else "r" + kind, m // 2)]
                        await_loaded(pe, p)
                        i = P * (m % 2)
                        feature_job((kind, l, m), piece_view(p, KT, 256)[:, :, i:i + P], hT, 0 if kind == "k" else t0, T if kind == "k" else nt)
                    return step

                def step_ret(n):
                    if n < len(ru):
                        h, s = ru[n]
                        if n == 0:
                            await_emptied(pe, ("q", l, 3))
                            await_emptied(pe, ("k", l, 3))
                        for pr in range(1 + s):
                            b = open_bank(pe, ("s", l, n, pr))
                            for i in range(2):
                                j = 2 * pr + i
                                last = mm(b[:, 256 * i:256 * i + 256], rkT[:, h, P * j:P * j + P],
                                          rqT[:, h, 256 * s:256 * s + 256], start=True, stop=True)
                            last.then_inc(bank_full, 1)
                    if 0 <= n - 1 < len(ru):
                        h, s = ru[n - 1]
                        b = open_bank(pe, ("o", l, n - 1))
                        await_emptied(pe, ("s", l, n - 1, s))
                        if n == 1:
                            await_emptied(pe, ("v", l, 1, TT - 1))
                        for i in range(2):
                            nj = 2 + 2 * s
                            for j in range(nj):
                                last = mm(b[:, P * i:P * i + P], att[:, (n - 1) % 2, j, P * i:P * i + P],
                                          rv[:, j, P * h:P * h + P], start=(j == 0), stop=(j == nj - 1))
                        last.then_inc(bank_full, 1)
                    if n >= 2:
                        b = open_bank(pe, ("ot", l, n - 2))
                        pe.wait_ge(on_ready, before(l, lambda i: len(ret_units(i))) + n - 1)
                        for i in range(2):
                            last = turn(b[:, P * i:P * i + P], on[:, (n - 2) % 2, P * i:P * i + P])
                        last.then_inc(bank_full, 1)

                def step_out(m):
                    p = piece_at[(l, "wo", m // 2)]
                    await_loaded(pe, p)
                    pe.wait_ge(merged_ready, 8 * (l + 1))
                    i = P * (m % 2)
                    feature_job(("out", l, m), piece_view(p, KT, 256)[:, :, i:i + P], merged, 0, nt)
                    if m:
                        mean_square(("ms2", l), [m - 1])

                def step_ms2():
                    mean_square(("ms2", l), [KT - 1])

                def step_rt():
                    pe.wait_ge(h_ready, norm_at(("ms2", l)) + 1)
                    p = piece_at[(l, "router")]
                    await_loaded(pe, p)
                    b = open_bank(pe, ("rt", l))
                    for i, t in enumerate(mt):
                        for k in range(KT):
                            last = mm(b[:, N_EXP * i:N_EXP * i + N_EXP], hT[:, k, P * t:P * t + P], piece_view(p, KT, N_EXP)[:, k, :],
                                      start=(k == 0), stop=(k == KT - 1))
                    last.then_inc(bank_full, 1)

                def step_h2(t):
                    for hf in range(2):
                        b = open_bank(pe, ("h2", l, t, hf))
                        for k in range(4):
                            last = turn(b[:, P * k:P * k + P], hT[:, 4 * hf + k, P * t:P * t + P])
                        last.then_inc(bank_full, 1)

                def shared(kind):
                    def step(m):
                        p = piece_at[(l, kind)]
                        await_loaded(pe, p)
                        feature_job((kind, l, m), piece_view(p, KT, FF)[:, :, P * m:P * m + P], hT, t0, nt)
                    return step

                def step_sd(m):
                    p = piece_at[(l, "sd")]
                    await_loaded(pe, p)
                    pe.wait_ge(sh_ready, 2 * (l + 1))
                    feature_job(("sd", l, m), piece_view(p, 2, D)[:, :, P * m:P * m + P], shT[:, :, t0:T], 0, nt)

                def step_pos():
                    pe.wait_ge(mask_ready, l + 1)
                    b = open_bank(pe, ("pos", l))
                    for i in range(len(mt)):
                        for j in range(i + 1):
                            last = mm(b[:, N_EXP * i:N_EXP * i + N_EXP], const_cols("tri") if j == i else ones[:, :], mask[:, j, :],
                                      start=(j == 0), stop=(j == i))
                    last.then_inc(bank_full, 1)

                def step_cnt():
                    b = open_bank(pe, ("cnt", l))
                    for j in range(len(mt)):
                        last = mm(b[:, 0:N_EXP], ones[:, :], mask[:, j, :], start=(j == 0), stop=(j == len(mt) - 1))
                    last.then_inc(bank_full, 1)

                def step_list(e):
                    b = open_bank(pe, ("list", l, e))
                    pe.wait_ge(pick_ready, l * PICKS + e + 1)
                    for i in range(len(mt)):
                        last = mm(b[0:CAP[l], 0:3], pick[:, e, P * i:P * i + CAP[l]], entry(i, e), start=(i == 0), stop=(i == len(mt) - 1))
                    last.then_inc(bank_full, 1)

                steps = {"vec": step_vec, "x": step_x, "adaw": step_adaw, "adat": step_adat, "ms1": step_ms1, "c": step_c,
                         "turn_c": step_turn_c, "project": step_project, "turn_qk": step_turn_qk, "att": step_att, "ws": step_ws,
                         "u": projection("u"), "gv": step_gv, "sv": step_sv, "merge": step_merge, "q": projection("q"),
                         "k": projection("k"), "g": projection("g"), "v": step_v, "ret": step_ret, "out": step_out, "ms2": step_ms2,
                         "rt": step_rt, "h2": step_h2, "sg": shared("sg"), "su": shared("su"), "sd": step_sd, "pos": step_pos,
                         "cnt": step_cnt, "list": step_list, "comb": step_comb}
                for kind, *a in layer_steps(l):
                    if kind in steps:
                        steps[kind](*a)
                await_emptied(pe, ("sd", l, 7))
                await_emptied(pe, ("sg", l, 1))
                pe.wait_ge(moe_ready, l + 1)

                cap, nm = CAP[l], len(mt)

                def make_list(e, j):
                    pe.wait_ge(pick_ready, l * PICKS + e + 1)
                    pe.wait_ge(list_read, l * LISTS + e)
                    for i in range(nm):
                        last = mm(bank[7][0:cap, 256:259], pick[:, j, P * i:P * i + cap], entry(i, e), start=(i == 0), stop=(i == nm - 1))
                    last.then_inc(list_full, 1)

                def turn_rows(e, j, i):
                    pe.wait_ge(rows_in[j], 16 * (l * lists_of[j] + 1) + 16 * i)
                    pe.wait_ge(turned_act, l * N_EXP + e)
                    pe.wait_ge(turned_dve, l * N_EXP + e)
                    pe.sem_inc(pe_passed, 1)
                    for k in range(KT):
                        last = turn(bank[k // 4][:, cap * (k % 4):cap * (k % 4) + cap], x_rows[0:cap, j, k::KT], cap)
                    last.then_inc(rows_turned, 1)

                def gate_up(e, j, i):
                    gp, up = moe_at[l] + 3 * j, moe_at[l] + 3 * j + 1
                    pe.wait_ge(turned_act, l * N_EXP + e + 1)
                    pe.wait_ge(turned_dve, l * N_EXP + e + 1)
                    pe.wait_ge(piece_loaded[gp % NS], 16 * (gp // NS + 1) + 16 * i)
                    pe.wait_ge(piece_loaded[up % NS], 16 * (up // NS + 1) + 16 * i)
                    wg, wu = piece_view(gp, KT, FF), piece_view(up, KT, FF)

                    def halves():
                        for k in range(KT):
                            x = x_rowsT[:, j, cap * k:cap * k + P // 2]
                            mm(bank[4 + j][0:P // 2, 0:FF], x, wg[:, k, :], start=(k == 0), stop=(k == KT - 1))
                            last = mm(bank[4 + j][P // 2:P, 0:FF], x, wu[:, k, :], start=(k == 0), stop=(k == KT - 1))
                        last.then_inc(gu_full, 1)

                    def whole():
                        for k in range(KT):
                            x = x_rowsT[:, j, cap * k:cap * k + cap]
                            mm(bank[4 + j][:, 0:FF], x, wg[:, k, :], start=(k == 0), stop=(k == KT - 1), skip_group_check=True)
                            last = mm(bank[4 + j][:, FF:2 * FF], x, wu[:, k, :], start=False, stop=(k == KT - 1), skip_group_check=True)
                        last.then_inc(gu_full, 1)

                    by_size(pe, pe_passed, l, e, halves, whole)

                def turn_hidden(e, j):
                    pe.wait_ge(hid_ready, l * N_EXP + e + 1)
                    pe.sem_inc(pe_passed, 1)
                    for k in range(2):
                        last = turn(bank[7][:, cap * k:cap * k + cap], hid[0:cap, j, k::2], cap)
                    last.then_inc(hidT_full, 1)

                def down(e, j, i):
                    dp = moe_at[l] + 3 * j + 2
                    pe.wait_ge(piece_loaded[dp % NS], 16 * (dp // NS + 1) + 16 * i)
                    pe.wait_ge(hidT_ready, l * N_EXP + e + 1)
                    pe.wait_ge(y_act, l * N_EXP + e)
                    pe.wait_ge(y_dve, l * N_EXP + e)
                    wd = piece_view(dp, 2, D)

                    def product(m, o):
                        for k in range(2):
                            for hf in range(2):
                                last = mm(bank[2 + hf][o * hf:o * hf + m, :], hidT[:, j, cap * k:cap * k + m], wd[:, k, 512 * hf:512 * hf + 512],
                                          start=(k == 0), stop=(k == 1))
                        last.then_inc(down_full, 1)

                    by_size(pe, pe_passed, l, e, lambda: product(P // 2, P // 2), lambda: product(P, 0))

                turn_rows(0, 0, 0)

                def three_experts(i):
                    for j in range(BODY):
                        e = i * BODY + j
                        make_list(e + 2, (j + 2) % 3)
                        turn_rows(e + 1, (j + 1) % 3, i + (j + 1) // 3)
                        if j or i is not FIRST:
                            pe.wait_ge(list_read, l * LISTS + e + 3)
                            turn_hidden(e - 1, (j + 2) % 3)
                        gate_up(e, j, i)
                        if j or i is not FIRST:
                            down(e - 1, (j + 2) % 3, i + (j + 2) // 3 - 1)

                three_experts(FIRST)
                with pe.Fori(1, N_EXP // BODY) as i:
                    three_experts(i)
                turn_hidden(experts - 1, 2)
                gate_up(experts, 0, N_EXP // BODY)
                down(experts - 1, 2, N_EXP // BODY - 1)
                turn_hidden(experts, 0)
                down(experts, 0, N_EXP // BODY)
                pe.wait_ge(y_act, (l + 1) * N_EXP)
                pe.wait_ge(y_dve, (l + 1) * N_EXP)

                most = pe.value_load(maxcnt[0:1, l:l + 1], min_val=0, max_val=T)
                for b in range(1, tokens(l) // cap):
                    with pe.If(most > b * cap):
                        with pe.Fori(0, N_EXP) as e:
                            q = (b - 1) * N_EXP + e
                            pe.wait_ge(late_dve[l], 6 * q + 1)
                            for i in range(nm):
                                last = mm(bank[7][0:cap, 256:259], pick[:, 0, P * i:P * i + cap], entry(i, e), start=(i == 0), stop=(i == nm - 1))
                            last.then_inc(late_pe[l], 1)
                            pe.wait_ge(late_in[l], 16 * q + 16)
                            pe.sem_inc(pe_passed, 1)
                            for k in range(KT):
                                last = turn(bank[k // 4][:, cap * (k % 4):cap * (k % 4) + cap], x_rows[0:cap, 0, k::KT], cap)
                            last.then_inc(late_pe[l], 1)
                            pe.wait_ge(late_dve[l], 6 * q + 3)
                            pe.wait_ge(late_loaded[l], 48 * q + 48)
                            for w in range(2):
                                for k in range(KT):
                                    last = mm(bank[4 + w][0:cap, 0:FF], x_rowsT[:, 0, cap * k:cap * k + cap],
                                              late_w[:, w, FF * k:FF * k + FF], start=(k == 0), stop=(k == KT - 1))
                            last.then_inc(late_pe[l], 1)
                            pe.wait_ge(late_dve[l], 6 * q + 4)
                            pe.sem_inc(pe_passed, 1)
                            for k in range(2):
                                last = turn(bank[6][:, cap * k:cap * k + cap], hid[0:cap, 0, k::2], cap)
                            last.then_inc(late_pe[l], 1)
                            pe.wait_ge(late_dve[l], 6 * q + 5)
                            for k in range(2):
                                for hf in range(2):
                                    last = mm(bank[2 + hf][0:cap, :], hidT[:, 0, cap * k:cap * k + cap],
                                              late_w[:, 2, D * k + 512 * hf:D * k + 512 * hf + 512], start=(k == 0), stop=(k == 1))
                            last.then_inc(late_pe[l], 1)
                            pe.wait_ge(late_dve[l], 6 * q + 6)
            for t in main_tiles(DEPTH - 1):
                step_comb(DEPTH - 1, t)
            await_emptied(pe, ("comb", DEPTH - 1, TT - 1, 1))
            for t in range(2):
                for hf in range(2):
                    b = open_bank(pe, ("fin", DEPTH, t, hf))
                    for k in range(4):
                        last = turn(b[:, P * k:P * k + P], xT[:, 4 * hf + k, CTX + P * t:CTX + P * t + P])
                    last.then_inc(bank_full, 1)

        @block.scalar
        def _(act):
            af = nc.scalar.activation
            steps = [0]

            for l in range(DEPTH):
                vecs = {"c": dram["c"].rearrange("o (k p) -> (o k) p", p=P), "cctx": dram["c_ctx"].rearrange("(k p) -> k p", p=P)} if l == 0 else {}
                for name, src in (("ada_b", "ada_b"), ("n1", "norm1_g"), ("n2", "norm2_g"), ("gng", "ret_gn_g"), ("gnb", "ret_gn_b"),
                                  ("qag", "mla_qa_g"), ("kvag", "mla_kva_g")):
                    vecs[name] = dram[src][l].rearrange("(k p) -> k p", p=P)
                for name, src in vecs.items():
                    act.dma_start(vec_rows[VEC_AT[name]:VEC_AT[name] + VEC_ROWS[name], l, :], src).then_inc(vec_loaded, 16)

            def link(ins):
                steps[0] += 1
                ins.then_inc(act_step, 1)
                act.wait_ge(act_step, steps[0])

            def copy_out(key, dst, src=None, func=ACT.Copy, **kw):
                b = await_full(act, key)
                return af(dst, b[:, :] if src is None else src(b), func, **kw).then_inc(emptied["act"], 1)

            taken = [0]

            def root(dst, src, scale=1.0, eps=0):
                taken[0] += 1
                act.wait_ge(root_asked, taken[0])
                af(dst, src, ACT.Sqrt, scale=scale, bias=eps_col[:, eps:eps + 1]).then_inc(roots, 1)

            def squares(key, ks):
                n = norm_at(key)
                lo, hi = norm_cols(key)
                for k in ks:
                    if k >= 2:
                        act.wait_ge(sq_used, 7 * n + k - 1)
                    elif n:
                        await_full(act, norm_before(key))
                    af((sq_2 if key[0] == "ms2" else sq_1)[:, k % 2, 0:hi - lo], xT[:, k, lo:hi], ACT.Square).then_inc(sq_ready, 1)

            def rms(key):
                lo, hi = norm_cols(key)
                copy_out(key, rstd[:, lo:hi], lambda b: b[:, 0:hi - lo], ACT.Sqrt, scale=1.0 / D, bias=eps_col[:, 0:1])

            def shifts(key):
                l = key[1]
                for k in range(KT):
                    act.wait_ge(gained, KT * norm_at(key) + k + 1)
                    for s in norm_streams(key):
                        last = af(hT[:, k, span(l, s)], hT[:, k, span(l, s)], ACT.Identity,
                                  bias=mod[:, l, 24 * (key[0] == "ms2") + k, s:s + 1])
                last.then_inc(h_ready, 1)

            for l in range(DEPTH):
                mt, t0 = main_tiles(l), c0(l)
                nt = T - t0
                au = att_units(l)
                merges = [a for kind, *a in layer_steps(l) if kind == "merge"]

                def step_vec():
                    await_emptied(act, ("vec", 0))
                    for s, name in enumerate(("cctx", "c")):
                        last = af(silu_c[:, :, s], vec[:, 0, VEC_AT[name]:VEC_AT[name] + KT], ACT.Silu)
                    last.then_inc(silu_ready, 1)

                def step_x(t):
                    copy_out(("x", t, 0), xT[:, 0:4, P * t:P * t + P], lambda b: b[:, :].rearrange("p (k n) -> p k n", k=4))

                def step_adaw(la, q):
                    if q or la:
                        await_full(act, ("adat", la, q - 1) if q else ("adat", la - 1, 11))
                    copy_out(("adaw", la, q), ada_row[:, :])

                def step_ms1(s):
                    if l:
                        await_emptied(act, ("comb", l - 1, 2 * s + 1, 1))
                    else:
                        await_emptied(act, ("x", 2 * s + 1, 0))
                        await_emptied(act, ("x", 2 * s + 1, 1))
                    squares(("ms1", l, s), range(KT))
                    rms(("ms1", l, s))

                def step_norm(n):
                    shifts(("ms2", l) if n == 2 else ("ms1", l, n))

                def step_cnorm(t):
                    await_emptied(act, ("c", l, 2, t))
                    parts = [(j, at, n) for j, (at, n) in enumerate(((0, QL), (QL, KVL), (QL + KVL, ROPE))) if j or t in mt]
                    for j, at, n in parts:
                        last = af(c_sq[l][:, 0:n], lat_c[:, t, at:at + n], ACT.Square, accum_out=stat[:, 4 * j + t:4 * j + t + 1])
                        link(last)
                    for j, at, n in parts:
                        last = af(stat[:, 12 + 4 * j + t:13 + 4 * j + t], stat[:, 4 * j + t:4 * j + t + 1], ACT.Sqrt, scale=1.0 / n, bias=eps_col[:, 0:1])
                    last.then_inc(c_squared, 1)

                def step_turn_c(t):
                    if t in mt:
                        b = await_full(act, ("ct", l, t, 0))
                        for k in range(3):
                            last = af(cqT[:, k, :], b[:, P * k:P * k + P], ACT.Identity, scale=vcol(l, "qag", k))
                        last.then_inc(emptied["act"], 1)
                    b = await_full(act, ("ct", l, t, 1))
                    for k in range(2):
                        last = af(ckT[:, k, :], b[:, P * k:P * k + P], ACT.Identity, scale=vcol(l, "kvag", k))
                    last.then_inc(emptied["act"], 1)

                def step_project(t):
                    if t in mt:
                        for hf in range(2):
                            b = await_full(act, ("qp", l, t, hf))
                            if t:
                                await_emptied(act, ("kvp", l, t - 1, hf))
                            af(sq_tok[:, hf, 0:384], b[:, 0:384], ACT.Square).then_inc(qk_squared, 1)
                        root(stat[:, 48:56], stat[:, 48:56], eps=1)
                    for hf in range(2):
                        b = await_full(act, ("kvp", l, t, hf))
                        kv4 = b[:, :].rearrange("p (h d) -> p h d", h=4)
                        if t in mt:
                            await_emptied(act, ("qp", l, t, hf))
                        elif t:
                            await_emptied(act, ("kvp", l, t - 1, hf))
                        af(sq_tok[:, hf, 0:256].rearrange("p (h d) -> p h d", h=4), kv4[:, :, 0:NOPE], ACT.Square)
                        af(mv[:, t, 256 * hf:256 * hf + 256].rearrange("p (h d) -> p h d", h=4), kv4[:, :, NOPE:P],
                           ACT.Copy).then_inc(qk_squared, 1)
                    root(stat[:, 64:72], stat[:, 64:72], eps=2)

                def step_turn_qk(t):
                    for name, dst in (("qt", qT), ("kt", kT)):
                        if name == "qt" and t not in mt:
                            continue
                        for hf in range(2):
                            b = await_full(act, (name, l, t, hf))
                            af(dst[0:QK, 4 * hf:4 * hf + 4, P * t:P * t + P],
                               b[0:QK, :].rearrange("p (h n) -> p h n", h=4), ACT.Copy).then_inc(emptied["act"], 1)

                def step_att(n):
                    if n < len(au):
                        t, h = au[n]
                        nk = T if t >= 2 else CTX
                        b = await_full(act, ("S", l, n))
                        act.wait_ge(neg_max, before(l, lambda i: len(att_units(i))) + n + 1)
                        if n >= 2:
                            await_full(act, ("PT", l, n - 2))
                        if n >= 4:
                            await_emptied(act, ("pv", l, n - 4))
                        af(probs[:, n % 2, 0:nk], b[:, 0:nk], ACT.Exp, bias=stat[:, 80 + n % 4:81 + n % 4], scale=QK ** -0.5,
                           accum_out=stat[:, 84 + n % 4:85 + n % 4]).then_inc(emptied["act"], 1)
                    if n >= 2 and au[n - 2][1] == HEADS_M - 1:
                        t = au[n - 2][0]
                        copy_out(("omt", l, t), y_mla[:, :, P * t:P * t + P], lambda b: b[:, :].rearrange("p (k n) -> p k n", k=4))

                def step_ws():
                    copy_out(("ws", l), wsT[:, :, :].rearrange("p g i -> p (g i)"))

                def step_u(g):
                    copy_out(("u", l, g), y_gmlp[:, g, t0:T], lambda b: b[:, 0:nt], ACT.Gelu_apprx_tanh)

                def step_gv(j, t):
                    copy_out(("gv", l, j, t), gv[:, t, 256 * j:256 * j + 256], lambda b: b[:, 0:256], ACT.Gelu_apprx_tanh)

                def step_gnorm():
                    root(stat[:, 112 + mt[0]:116], stat[:, 105 + 2 * mt[0]:112:2])

                def step_merge(m, br):
                    n = merges.index([m, br])
                    if n >= 2:
                        await_emptied(act, ("y", l, *merges[n - 2]))
                    copy_out(("gate", l, m, br), gate_t[:, n % 2, 0:nt], lambda b: b[:, 0:nt], ACT.Tanh, scale=0.5)

                def step_decay(part):
                    if part == 0:
                        act.wait_ge(lg_arg, l + 1)
                        af(lg[:, 8:16], lg[:, 0:8], ACT.Exp, scale=-1.0).then_inc(lg_exp, 1)
                        return
                    act.wait_ge(decay_arg, l + 1)
                    for h in range(HEADS_R):
                        af(decay[:, 0, h, :], decay[:, 0, h, :], ACT.Exp)
                        af(decay[:, 1, h, :], const_cols("diff"), ACT.Exp, scale=lg[:, 16 + h:17 + h], bias=lg[:, 24 + h:25 + h])
                        last = af(decay_b[:, h, :], const_cols("diff"), ACT.Exp, scale=lg[:, 36 + h:37 + h], bias=lg[:, 28 + h:29 + h])
                    last.then_inc(decay_ready, 1)

                def step_q(h):
                    copy_out(("q", l, h), rqT[:, h, t0:T], lambda b: b[:, 0:nt])

                def step_k(h):
                    copy_out(("k", l, h), rkT[:, h, :])

                def step_g(h):
                    copy_out(("g", l, h), y_ret[:, h, t0:T], lambda b: b[:, 0:nt], ACT.Silu)

                def step_ret(n):
                    if 0 <= n - 1 < len(ret_units(l)):
                        root(stat[:, 40:42], stat[:, 37:40:2])

                def step_out(m):
                    await_emptied(act, ("out", l, m))
                    squares(("ms2", l), [m])

                def step_ms2():
                    rms(("ms2", l))

                def step_rt():
                    copy_out(("rt", l), score[:, 0:len(mt), :].rearrange("p t e -> p (t e)"), lambda b: b[:, 0:N_EXP * len(mt)],
                             ACT.Tanh, scale=0.5)

                def step_h2(t):
                    i = t - mt[0]
                    if i >= 2:
                        act.wait_ge(h2_stored[i % 2], 16 * (h2_base(l, i % 2) + i // 2))
                    for hf in range(2):
                        copy_out(("h2", l, t, hf), h2_tok[:, i % 2, 512 * hf:512 * hf + 512])
                    await_emptied(act, ("h2", l, t, 1))
                    act.dma_start(h2_dram[P * i:P * i + P, :], h2_tok[:, i % 2, :]).then_inc(h2_stored[i % 2], 16)

                def step_sg(m):
                    copy_out(("sg", l, m), sil_s[:, m, t0:T], lambda b: b[:, 0:nt], ACT.Silu)

                steps_of = {"vec": step_vec, "x": step_x, "adaw": step_adaw, "ms1": step_ms1, "cnorm": step_cnorm,
                            "turn_c": step_turn_c, "project": step_project, "turn_qk": step_turn_qk, "att": step_att, "ws": step_ws,
                            "u": step_u, "gv": step_gv, "gnorm": step_gnorm, "merge": step_merge, "decay": step_decay, "q": step_q,
                            "k": step_k, "g": step_g, "ret": step_ret, "out": step_out, "ms2": step_ms2, "norm": step_norm, "rt": step_rt, "h2": step_h2,
                            "sg": step_sg}
                for kind, *a in layer_steps(l):
                    if kind in steps_of:
                        steps_of[kind](*a)

                cap = CAP[l]
                act.wait_ge(moe_ready, l + 1)

                def turned(e, j):
                    act.wait_ge(rows_turned, l * N_EXP + e + 1)
                    af(x_rowsT[:, j, 0:4 * cap], bank[0][:, 0:4 * cap], ACT.Copy).then_inc(turned_act, 1)

                def silu(e, j):
                    act.wait_ge(gu_full, l * N_EXP + e + 1)
                    af(act_g[0:cap, j, :], bank[4 + j][0:cap, 0:FF], ACT.Silu).then_inc(silu_done, 1)

                def rows_down(e, j):
                    act.wait_ge(down_full, l * N_EXP + e + 1)
                    af(y_rows[0:cap, j, 0:512], bank[2][0:cap, :], ACT.Copy).then_inc(y_act, 1)

                turned(0, 0)

                def three_experts(i):
                    for j in range(BODY):
                        e = i * BODY + j
                        turned(e + 1, (j + 1) % 3)
                        silu(e, j)
                        if j or i is not FIRST:
                            rows_down(e - 1, (j + 2) % 3)

                three_experts(FIRST)
                with act.Fori(1, N_EXP // BODY) as i:
                    three_experts(i)
                silu(experts, 0)
                rows_down(experts - 1, 2)
                rows_down(experts, 0)
                most = act.value_load(maxcnt[0:1, l:l + 1], min_val=0, max_val=T)
                for b in range(1, tokens(l) // cap):
                    with act.If(most > b * cap):
                        with act.Fori(0, N_EXP) as e:
                            q = (b - 1) * N_EXP + e
                            act.wait_ge(late_pe[l], 5 * q + 3)
                            af(act_g[0:cap, 0, :], bank[4][0:cap, 0:FF], ACT.Silu).then_inc(late_act[l], 1)
            for t in range(2):
                for hf in range(2):
                    copy_out(("fin", DEPTH, t, hf), fin[:, t, 512 * hf:512 * hf + 512])
            await_emptied(act, ("fin", DEPTH, 1, 1))
            act.dma_start(out.rearrange("o (t p) d -> p (o t) d", p=P), fin[:, :, :]).then_inc(stored, 16)
            act.wait_ge(stored, 16)

        @block.vector
        def _(dve):
            v = nc.vector
            steps = [0]

            def link(ins):
                steps[0] += 1
                ins.then_inc(dve_step, 1)
                dve.wait_ge(dve_step, steps[0])

            def copy_out(key, dst, src=None):
                b = await_full(dve, key)
                return v.tensor_copy(dst, b[:, :] if src is None else src(b)).then_inc(emptied["dve"], 1)

            def norm(key):
                l, lo, hi = key[1], *norm_cols(key)
                await_emptied(dve, key)
                link(v.reciprocal(rstd[:, lo:hi], rstd[:, lo:hi]))
                g = gain2 if key[0] == "ms2" else gain1
                for k in range(KT):
                    for s in norm_streams(key):
                        last = v.scalar_tensor_tensor(out=hT[:, k, span(l, s)], in0=xT[:, k, span(l, s)], scalar=g[:, l, k, s:s + 1],
                                                      in1=rstd[:, span(l, s)], op0=ALU.mult, op1=ALU.mult)
                    last.then_inc(gained, 1)

            def rope(x, t, heads):
                def table_of(name):
                    at = CONST_AT[name] + ROPE * (t - 2)
                    return const[:, at:at + ROPE]

                cos_b = table_of("cos").unsqueeze(1).to_broadcast([P, heads, ROPE])
                y, z = rope_t[:, 0:heads, :], rope_u[:, 0:heads, :]
                v.tensor_tensor(y, x, cos_b, ALU.mult)
                for hf in range(2):
                    for i in range(2):
                        a, b = 16 * hf + 8 * i, 16 * hf + 8 * (1 - i)
                        last = v.tensor_tensor(z[:, :, a:a + 8], x[:, :, b:b + 8],
                                               table_of("sin")[:, a:a + 8].unsqueeze(1).to_broadcast([P, heads, 8]), ALU.mult)
                link(last)
                return v.tensor_tensor(x, y, z, ALU.add)

            asked = [0]

            def ask_root():
                asked[0] += 1
                dve.nop().then_inc(root_asked, 1)
                dve.wait_ge(roots, asked[0])

            def step_comb(l, t):
                i = t - main_tiles(l)[0]
                y = y_parts[i % 2]
                for k in range(PE_ROWS, TOPK):
                    dve.wait_ge(y_in[i % 2][k], 16 * (h2_base(l, i % 2) + i // 2 + 1))
                    if k > PE_ROWS:
                        part = y[:, D * PE_ROWS:D * PE_ROWS + D]
                        link(v.tensor_tensor(part, part, y[:, D * k:D * k + D], ALU.add))
                dve.nop().then_inc(y_summed, 1)
                for hf in range(2):
                    b = await_full(dve, ("comb", l, t, hf))
                    s = 0 if t < 2 else 1
                    for k in range(4):
                        m = 4 * hf + k
                        xs = xT[:, m, P * t:P * t + P]
                        last = v.scalar_tensor_tensor(out=xs, in0=b[:, P * k:P * k + P], scalar=mod[:, l, 40 + m, s:s + 1], in1=xs,
                                                      op0=ALU.mult, op1=ALU.add)
                    last.then_inc(emptied["dve"], 1)

            v.memset(ones[:, :], 1.0)
            v.memset(silu_c[:, :, :], 0.0)
            for i, w in enumerate((1, QK, NOPE)):
                v.memset(eps_col[:, i:i + 1], w * EPS)
            link(v.memset(stat[:, :], 0.0))
            dve.nop().then_inc(ones_ready, 1)
            for l in range(DEPTH):
                mt, t0 = main_tiles(l), c0(l)
                nt = T - t0
                nm = len(mt)
                cap = CAP[l]
                ru, au = ret_units(l), att_units(l)
                merges = [a for kind, *a in layer_steps(l) if kind == "merge"]
                sq_n = [before(l, lambda i: 2 * TT + 2 * len(main_tiles(i)))]

                def step_vec():
                    for i in range(DEPTH):
                        copy_out(("vec", i), vec[:, i, 0:VEC_OF[i]], lambda b: b[:, 0:VEC_OF[i]])

                def step_x(t):
                    copy_out(("x", t, 1), xT[:, 4:8, P * t:P * t + P], lambda b: b[:, :].rearrange("p (k n) -> p k n", k=4))

                def step_adat(la, q):
                    if la == 0 and q == 0:
                        await_emptied(dve, ("vec", 1))
                    b = await_full(dve, ("adat", la, q))
                    at = VEC_AT["ada_b"] + 4 * q
                    link(v.tensor_tensor(mod[:, la, 4 * q:4 * q + 4, :], b[:, 0:8].rearrange("p (m s) -> p m s", s=2),
                                         vec[:, la, at:at + 4].unsqueeze(2).to_broadcast([P, 4, 2]), ALU.add))
                    dve.nop().then_inc(emptied["dve"], 1)
                    for g, name, first in ((gain1, "n1", 8), (gain2, "n2", 32)):
                        if 4 * q + 4 == first + KT:
                            n_g = vec[:, la, VEC_AT[name]:VEC_AT[name] + KT].unsqueeze(2).to_broadcast([P, KT, 2])
                            link(v.scalar_tensor_tensor(out=g[:, la, :, :], in0=mod[:, la, first:first + KT, :], scalar=1.0, in1=n_g,
                                                        op0=ALU.add, op1=ALU.mult))
                    if 4 * q + 4 == 24:
                        link(v.tensor_scalar(half_gate[:, la, :, :], mod[:, la, 16:24, :], 0.5, None, ALU.mult))

                def step_c(j, t):
                    n = 256 if j < 2 else CW - 512
                    copy_out(("c", l, j, t), lat_c[:, t, 256 * j:256 * j + n], lambda b: b[:, 0:n])

                def step_cnorm(t):
                    if t == 0:
                        dve.wait_ge(rows_loaded, 16 * N_ROW_LOADS * (l + 1))
                        v.tensor_scalar(rows("qn"), rows("qn"), QK ** 0.5, None, ALU.mult)
                        link(v.tensor_scalar(rows("kn"), rows("kn"), NOPE ** 0.5, None, ALU.mult))
                    dve.wait_ge(c_squared, TT * l + t + 1)
                    first = 12 if t in mt else 16
                    link(v.reciprocal(stat[:, first + t:24:4], stat[:, first + t:24:4]))
                    if t in mt:
                        v.tensor_scalar(lat_c[:, t, 0:QL], lat_c[:, t, 0:QL], stat[:, 12 + t:13 + t], None, ALU.mult)
                    v.tensor_scalar(lat_c[:, t, QL:QL + KVL], lat_c[:, t, QL:QL + KVL], stat[:, 16 + t:17 + t], None, ALU.mult)
                    kr = lat_c[:, t, QL + KVL:CW]
                    link(v.scalar_tensor_tensor(out=kr, in0=kr, scalar=stat[:, 20 + t:21 + t], in1=rows("kr"), op0=ALU.mult, op1=ALU.mult))
                    if t >= 2:
                        link(rope(lat_c[:, t:t + 1, QL + KVL:CW], t, 1))
                    dve.nop().then_inc(c_normed, 1)

                def step_project(t):
                    parts = [("qp", q_tok, 384, QK, 48)] * (t in mt) + [("kvp", k_tok, 256, NOPE, 64)]
                    for name, dst, width, w, at in parts:
                        for hf in range(2):
                            sq_n[0] += 1
                            dve.wait_ge(qk_squared, sq_n[0])
                            sq = sq_tok[:, hf, 0:width].rearrange("p (h d) -> p h d", h=4)
                            last = v.tensor_reduce(stat[:, at + 4 * hf:at + 4 * hf + 4], sq, AX_X, ALU.add)
                        link(last)
                        ask_root()
                        link(v.reciprocal(stat[:, at:at + 8], stat[:, at:at + 8]))
                        if t:
                            await_full(dve, ("kt", l, t - 1, 1))
                        for hf in range(2):
                            b = await_full(dve, (name, l, t, hf))
                            r = stat[:, at + 4 * hf:at + 4 * hf + 4]
                            src = b[:, 0:4 * (QK if name == "qp" else P)].rearrange("p (h d) -> p h d", h=4)[:, :, 0:w]
                            last = v.tensor_tensor(dst[:, 4 * hf:4 * hf + 4, 0:w], src, r.unsqueeze(2).to_broadcast([P, 4, w]), ALU.mult)
                            last.then_inc(emptied["dve"], 1)
                        await_emptied(dve, (name, l, t, 1))
                        g = rows("qn" if name == "qp" else "kn")
                        link(v.tensor_tensor(dst[:, :, 0:w], dst[:, :, 0:w], g.unsqueeze(1).to_broadcast([P, HEADS_M, w]), ALU.mult))
                        if name == "qp" and t >= 2:
                            link(rope(dst[:, :, NOPE:QK], t, HEADS_M))
                    link(v.tensor_copy(k_tok[:, :, NOPE:QK], lat_c[:, t:t + 1, QL + KVL:CW].to_broadcast([P, HEADS_M, ROPE])))
                    dve.nop().then_inc(qk_tok_ready, 1)

                def step_att(n):
                    if n < len(au):
                        t, h = au[n]
                        nk = T if t >= 2 else CTX
                        b = await_full(dve, ("S", l, n))
                        mx = stat[:, 80 + n % 4:81 + n % 4]
                        link(v.tensor_reduce(mx, b[:, 0:nk], AX_X, ALU.max))
                        link(v.tensor_scalar(mx, mx, -QK ** -0.5, None, ALU.mult))
                        dve.nop().then_inc(neg_max, 1)
                    if 0 <= n - 1 < len(au):
                        t, h = au[n - 1]
                        nk = T if t >= 2 else CTX
                        if n >= 3:
                            await_full(dve, ("pv", l, n - 3))
                        copy_out(("PT", l, n - 1), probsT[:, (n - 1) % 2, 0:nk], lambda b: b[:, 0:nk])
                    if n >= 2:
                        t, h = au[n - 2]
                        rec = stat[:, 88 + n % 4:89 + n % 4]
                        await_emptied(dve, ("S", l, n - 2))
                        link(v.reciprocal(rec, stat[:, 84 + (n - 2) % 4:85 + (n - 2) % 4]))
                        b = await_full(dve, ("pv", l, n - 2))
                        if h == 0 and t > mt[0]:
                            await_full(dve, ("omt", l, t - 1))
                        v.tensor_scalar(o_tok[:, VD * h:VD * h + VD], b[:, 0:VD], rec, None, ALU.mult).then_inc(emptied["dve"], 1)

                def step_gnorm():
                    for t in mt:
                        await_emptied(dve, ("gv", l, 1, t))
                        link(v.bn_stats(stat[:, 96:102], gv[:, t, :]))
                        link(v.bn_aggr(stat[:, 104 + 2 * t:106 + 2 * t], stat[:, 96:102]))
                    ask_root()
                    link(v.reciprocal(stat[:, 112 + mt[0]:116], stat[:, 112 + mt[0]:116]))
                    for t in mt:
                        link(v.tensor_scalar(gv[:, t, :], gv[:, t, :], stat[:, 104 + 2 * t:105 + 2 * t], stat[:, 112 + t:113 + t], ALU.subtract, ALU.mult))
                        link(v.tensor_tensor(gv[:, t, :], gv[:, t, :], rows("lng"), ALU.mult))
                        v.tensor_tensor(gv[:, t, :], gv[:, t, :], rows("lnb"), ALU.add).then_inc(gv_normed, 1)

                def step_sv(t):
                    b = await_full(dve, ("sv", l, t))
                    link(v.tensor_tensor(sv_tmp, b[:, :], rows("bs"), ALU.add))
                    dve.nop().then_inc(emptied["dve"], 1)
                    yg = y_gmlp[:, :, P * t:P * t + P]
                    link(v.tensor_tensor(yg, yg, sv_tmp.rearrange("p (g n) -> p g n", g=4), ALU.mult))
                    dve.nop().then_inc(y_gmlp_ready, 1)

                def step_merge(m, br):
                    n = merges.index([m, br])
                    b = await_full(dve, ("y", l, m, br))
                    await_emptied(dve, ("gate", l, m, br))
                    first = br == 2
                    dst = merged[:, m, 0:nt] if first else prod_t[:, 0:nt]
                    v.scalar_tensor_tensor(out=dst, in0=gate_t[:, n % 2, 0:nt], scalar=1.0, in1=b[:, 0:nt], op0=ALU.add,
                                           op1=ALU.mult).then_inc(emptied["dve"], 1)
                    if not first:
                        await_emptied(dve, ("y", l, m, br))
                        link(v.tensor_tensor(merged[:, m, 0:nt], merged[:, m, 0:nt], prod_t[:, 0:nt], ALU.add))
                    if br == 0:
                        dve.nop().then_inc(merged_ready, 1)

                def step_decay(part):
                    if part:
                        return
                    dec = rows("dec")
                    link(v.scalar_tensor_tensor(out=lg[:, 0:8], in0=dec, scalar=-1.0, in1=dec, op0=ALU.mult, op1=ALU.max))
                    dve.nop().then_inc(lg_arg, 1)
                    dve.wait_ge(lg_exp, l + 1)
                    e_, s_, s2, q_ = lg[:, 8:16], lg[:, 40:48], lg[:, 48:56], lg[:, 56:64]
                    link(v.tensor_scalar(s_, e_, 2.0, None, ALU.add))
                    link(v.reciprocal(s2, s_))
                    link(v.tensor_tensor(s_, s2, e_, ALU.mult))
                    link(v.tensor_tensor(s2, s_, s_, ALU.mult))
                    link(v.tensor_scalar(q_, s2, 1.0 / 19, None, ALU.mult))
                    for odd in (17, 15, 13, 11, 9, 7, 5, 3):
                        link(v.scalar_tensor_tensor(out=q_, in0=q_, scalar=1.0 / odd, in1=s2, op0=ALU.add, op1=ALU.mult))
                    link(v.scalar_tensor_tensor(out=q_, in0=q_, scalar=1.0, in1=s_, op0=ALU.add, op1=ALU.mult))
                    link(v.tensor_scalar(s2, dec, 0.0, None, ALU.min))
                    link(v.scalar_tensor_tensor(out=lg[:, 16:24], in0=q_, scalar=-2.0, in1=s2, op0=ALU.mult, op1=ALU.add))
                    link(v.tensor_scalar(lg[:, 24:32], lg[:, 16:24], float(CTX), None, ALU.mult))
                    link(v.tensor_scalar(lg[:, 32:40], lg[:, 16:24], -1.0, None, ALU.mult))
                    diff = const_cols("diff")
                    for h in range(HEADS_R):
                        v.tensor_scalar(decay[:, 0, h, :], diff, 0.0, lg[:, 16 + h:17 + h], ALU.max, ALU.mult)
                        last = v.tensor_scalar(decay_b[:, h, :], diff, 0.0, lg[:, 36 + h:37 + h], ALU.min, ALU.mult)
                    link(last)
                    link(v.tensor_tensor(decay[:, 0, :, :], decay[:, 0, :, :], decay_b[:, :, :], ALU.add))
                    dve.nop().then_inc(decay_arg, 1)

                def step_v(j, t):
                    copy_out(("v", l, j, t), rv[:, t, 256 * j:256 * j + 256], lambda b: b[:, 0:256])

                def step_ret(n):
                    if n == 0:
                        dve.wait_ge(decay_ready, l + 1)
                        link(v.tensor_tensor(decay[:, 1, :, :], decay[:, 1, :, :], decay_b[:, :, :], ALU.add))
                        await_emptied(dve, ("g", l, 3))
                    if n < len(ru):
                        h, s = ru[n]
                        if n >= 2:
                            await_full(dve, ("o", l, n - 2))
                        for pr in range(1 + s):
                            b = await_full(dve, ("s", l, n, pr))
                            for i in range(2):
                                cross = s == 1 and pr == 0
                                w = decay[:, int(cross), h, P - P * i:P - P * i + 256]
                                last = v.scalar_tensor_tensor(out=att[:, n % 2, 2 * pr + i, :], in0=b[:, 256 * i:256 * i + 256],
                                                              scalar=P ** -0.5, in1=w, op0=ALU.mult, op1=ALU.mult)
                            last.then_inc(emptied["dve"], 1)
                    if 0 <= n - 1 < len(ru):
                        u = n - 1
                        if u >= 2:
                            await_full(dve, ("ot", l, u - 2))
                        b = await_full(dve, ("o", l, u))
                        for i in range(2):
                            last = v.bn_stats(stat[:, 24 + 6 * i:30 + 6 * i], b[:, P * i:P * i + P])
                        link(last)
                        for i in range(2):
                            last = v.bn_aggr(stat[:, 36 + 2 * i:38 + 2 * i], stat[:, 24 + 6 * i:30 + 6 * i])
                        link(last)
                        ask_root()
                        link(v.reciprocal(stat[:, 40:42], stat[:, 40:42]))
                        for i in range(2):
                            last = v.tensor_scalar(on[:, u % 2, P * i:P * i + P], b[:, P * i:P * i + P], stat[:, 36 + 2 * i:37 + 2 * i],
                                                   stat[:, 40 + i:41 + i], ALU.subtract, ALU.mult)
                        link(last)
                        dve.nop().then_inc(on_ready, 1)
                        dve.nop().then_inc(emptied["dve"], 1)
                    if n >= 2:
                        h, s = ru[n - 2]
                        b = await_full(dve, ("ot", l, n - 2))
                        link(v.tensor_scalar(tmp_ret[:, n % 2, :], b[:, 0:256], vcol(l, "gng", h), vcol(l, "gnb", h), ALU.mult, ALU.add))
                        v.tensor_tensor(y_ret[:, h, span(l, s)], y_ret[:, h, span(l, s)], tmp_ret[:, n % 2, :],
                                        ALU.mult).then_inc(emptied["dve"], 1)

                def residual(key, gate, m):
                    b = await_full(dve, key)
                    for s in streams(l):
                        last = v.scalar_tensor_tensor(out=xT[:, m, span(l, s)], in0=b[:, span(l, s, t0)], scalar=gate[:, s:s + 1],
                                                      in1=xT[:, m, span(l, s)], op0=ALU.mult, op1=ALU.add)
                    last.then_inc(emptied["dve"], 1)

                def step_out(m):
                    residual(("out", l, m), half_gate[:, l, m, :], m)

                def step_rt():
                    await_emptied(dve, ("rt", l))
                    sc, se, ma, eqm, cu = (x[:, 0:nm, :] for x in (score, sel, mask, eq, cum))
                    link(v.tensor_scalar(sc, sc, 0.5, 0.5, ALU.mult, ALU.add))
                    link(v.tensor_tensor(se, sc, rows("bias").unsqueeze(1).to_broadcast([P, nm, N_EXP]), ALU.add))
                    for i in range(nm):
                        last = v.max(top8[:, i, :], sel[:, i, :])
                    link(last)
                    sixth = top8[:, 0:nm, TOPK - 1:TOPK].to_broadcast([P, nm, N_EXP])
                    v.tensor_tensor(ma, se, sixth, ALU.is_gt)
                    link(v.tensor_tensor(eqm, se, sixth, ALU.is_equal))
                    v.memset(one64[:, :], 1.0)
                    link(v.tensor_reduce(need[:, 0:nm], ma, AX_X, ALU.add))
                    link(v.tensor_scalar(need[:, 0:nm], need[:, 0:nm], -1.0, float(TOPK), ALU.mult, ALU.add))
                    for i in range(nm):
                        last = v.tensor_tensor_scan(cum[:, i, :], one64[:, :], eq[:, i, :], 0.0, ALU.mult, ALU.add)
                    link(last)
                    link(v.tensor_tensor(cu, cu, need[:, 0:nm].unsqueeze(2).to_broadcast([P, nm, N_EXP]), ALU.is_le))
                    link(v.tensor_tensor(eqm, eqm, cu, ALU.mult))
                    link(v.tensor_tensor(ma, ma, eqm, ALU.add))
                    dve.nop().then_inc(mask_ready, 1)
                    link(v.memset(table[:, :, :, :], 0.0))
                    for i in range(nm):
                        last = v.tensor_tensor_scan(cum[:, i, :], one64[:, :], mask[:, i, :], 0.0, ALU.mult, ALU.add)
                    link(last)
                    link(v.tensor_tensor(kslot[:, 0:nm, :], cu, ma, ALU.subtract))
                    tok = const[:, CONST_AT["tok"] + 4 * l + mt[0]:CONST_AT["tok"] + 4 * l + TT].unsqueeze(2).to_broadcast([P, nm, N_EXP])
                    v.scalar_tensor_tensor(out=table[:, 0:nm, 0:N_EXP, 1], in0=kslot[:, 0:nm, :], scalar=float(tokens(l)), in1=tok,
                                           op0=ALU.mult, op1=ALU.add)
                    v.tensor_copy(table[:, 0:nm, 0:N_EXP, 0], tok)
                    link(v.tensor_tensor(se, sc, ma, ALU.mult))
                    link(v.tensor_reduce(wsum[:, 0:nm], se, AX_X, ALU.add))
                    link(v.reciprocal(wsum[:, 0:nm], wsum[:, 0:nm]))
                    link(v.scalar_tensor_tensor(out=table[:, 0:nm, 0:N_EXP, 2], in0=se, scalar=ROUTED_SCALE,
                                                in1=wsum[:, 0:nm].unsqueeze(2).to_broadcast([P, nm, N_EXP]), op0=ALU.mult, op1=ALU.mult))
                    v.memset(pos1[:, :, :], 0.0)
                    link(v.memset(x_rows[:, :, :], 0.0))
                    dve.nop().then_inc(small_used, 1)

                def picks(e, j, iota):
                    for i in range(nm):
                        pp = pos1[:, i, e:e + 1] if isinstance(e, int) else pos1[:, i, bass.ds(e, 1)]
                        last = v.tensor_scalar(pick[:, j, P * i:P * i + cap], iota, pp, None, ALU.is_equal)
                    return last

                def read_list(j, b=bank[7][:, 256:259]):
                    v.tensor_scalar(idx[0:cap, j, 0:2], b[0:cap, 0:2], BIG, None, ALU.add)
                    return v.tensor_copy(wrow[0:cap, j:j + 1], b[0:cap, 2:3])

                def step_pos():
                    b = await_full(dve, ("pos", l))
                    link(v.scalar_tensor_tensor(out=pos1[:, 0:nm, 0:N_EXP], in0=b[:, 0:nm * N_EXP].rearrange("p (t e) -> p t e", t=nm),
                                                scalar=1.0, in1=mask[:, 0:nm, :], op0=ALU.add, op1=ALU.mult))
                    dve.nop().then_inc(emptied["dve"], 1)
                    for e in range(3):
                        picks(e, e, const_cols("iota1")[:, 0:cap]).then_inc(pick_ready, 1)

                def step_cnt():
                    b = await_full(dve, ("cnt", l))
                    v.memset(counts[:, N_EXP:N_EXP + 2], 0)
                    v.tensor_copy(counts[:, 0:N_EXP], b[:, 0:N_EXP])
                    link(v.tensor_reduce(need[:, 0:1], b[:, 0:N_EXP], AX_X, ALU.max))
                    dve.nop().then_inc(emptied["dve"], 1)
                    link(v.tensor_copy(maxcnt[:, l:l + 1], need[:, 0:1]))
                    dve.nop().then_inc(moe_ready, 1)

                def step_su(m):
                    b = await_full(dve, ("su", l, m))
                    await_emptied(dve, ("sg", l, m))
                    link(v.tensor_tensor(shT[:, m, t0:T], sil_s[:, m, t0:T], b[:, 0:nt], ALU.mult))
                    dve.nop().then_inc(emptied["dve"], 1)
                    dve.nop().then_inc(sh_ready, 1)

                def step_list(e):
                    b = await_full(dve, ("list", l, e))
                    link(read_list(e, b[:, 0:3]))
                    dve.nop().then_inc(list_read, 1)
                    dve.nop().then_inc(emptied["dve"], 1)

                def step_sd(m):
                    residual(("sd", l, m), mod[:, l, 40 + m, :], m)

                steps_of = {"vec": step_vec, "x": step_x, "adat": step_adat, "norm": lambda n: norm(("ms2", l) if n == 2 else ("ms1", l, n)), "c": step_c,
                            "cnorm": step_cnorm, "project": step_project, "att": step_att, "gnorm": step_gnorm, "sv": step_sv,
                            "merge": step_merge, "decay": step_decay, "v": step_v, "ret": step_ret, "out": step_out,
                            "rt": step_rt, "pos": step_pos, "cnt": step_cnt, "su": step_su,
                            "list": step_list, "sd": step_sd, "comb": step_comb}
                for kind, *a in layer_steps(l):
                    if kind in steps_of:
                        steps_of[kind](*a)

                def pick_for(e, j):
                    dve.wait_ge(list_read, l * LISTS + e - 2)
                    picks(e, j, const_cols("iota1")[:, 0:cap]).then_inc(pick_ready, 1)

                def list_of(e, j):
                    dve.wait_ge(list_full, l * (LISTS - 2) + e - 1)
                    if not isinstance(e, int) or e >= 3:
                        dve.wait_ge(hid_ready, l * N_EXP + e - 2)
                    read_list(j).then_inc(list_read, 1)

                def turned(e, j):
                    dve.wait_ge(rows_turned, l * N_EXP + e + 1)
                    v.tensor_copy(x_rowsT[:, j, 4 * cap:8 * cap], bank[1][:, 0:4 * cap]).then_inc(turned_dve, 1)

                def hidden(e, j, i):
                    dve.wait_ge(list_read, l * LISTS + e + 1)
                    dve.wait_ge(rows_out[j], 16 * l * experts_of[j] + 16 * i)
                    v.tensor_copy(idx[0:cap, j, 2:3], idx[0:cap, j, 1:2])
                    dve.wait_ge(silu_done, l * N_EXP + e + 1)

                    def gated(m, up):
                        v.scalar_tensor_tensor(out=hid[0:m, j, :], in0=act_g[0:m, j, :], scalar=wrow[0:m, j:j + 1], in1=up,
                                               op0=ALU.mult, op1=ALU.mult).then_inc(hid_ready, 1)

                    by_size(dve, dve_passed, l, e, lambda: gated(P // 2, bank[4 + j][P // 2:P, 0:FF]), lambda: gated(P, bank[4 + j][:, FF:2 * FF]))

                def hidden_turned(e, j):
                    dve.wait_ge(hidT_full, l * N_EXP + e + 1)
                    v.tensor_copy(hidT[:, j, 0:2 * cap], bank[7][:, 0:2 * cap]).then_inc(hidT_ready, 1)

                def rows_down(e, j):
                    dve.wait_ge(down_full, l * N_EXP + e + 1)

                    def half(m, o):
                        v.tensor_copy(y_rows[0:m, j, 512:1024], bank[3][o:o + m, :]).then_inc(y_dve, 1)

                    by_size(dve, dve_passed, l, e, lambda: half(P // 2, P // 2), lambda: half(P, 0))

                turned(0, 0)

                def three_experts(i):
                    for j in range(BODY):
                        e = i * BODY + j
                        list_of(e + 2, (j + 2) % 3)
                        turned(e + 1, (j + 1) % 3)
                        if j or i is not FIRST:
                            hidden_turned(e - 1, (j + 2) % 3)
                        pick_for(e + 3, j)
                        hidden(e, j, i)
                        if j or i is not FIRST:
                            rows_down(e - 1, (j + 2) % 3)

                three_experts(FIRST)
                with dve.Fori(1, N_EXP // BODY) as i:
                    three_experts(i)
                hidden_turned(experts - 1, 2)
                hidden(experts, 0, N_EXP // BODY)
                rows_down(experts - 1, 2)
                hidden_turned(experts, 0)
                rows_down(experts, 0)

                most = dve.value_load(maxcnt[0:1, l:l + 1], min_val=0, max_val=T)
                with dve.If(most > cap):
                    for j in range(3):
                        dve.wait_ge(rows_out[j], 16 * (l + 1) * experts_of[j])
                for b in range(1, tokens(l) // cap):
                    with dve.If(most > b * cap):
                        v.tensor_scalar(hid[:, 1, 0:cap], const_cols("iota1")[:, 0:cap], float(b * cap), None, ALU.add).then_inc(late_iota[l], 1)
                        dve.wait_ge(late_iota[l], b)
                        with dve.Fori(0, N_EXP) as e:
                            q = (b - 1) * N_EXP + e
                            picks(e, 0, hid[:, 1, 0:cap]).then_inc(late_dve[l], 1)
                            dve.wait_ge(late_pe[l], 5 * q + 1)
                            read_list(0).then_inc(late_dve[l], 1)
                            dve.wait_ge(late_dve[l], 6 * q + 2)
                            v.tensor_copy(idx[0:cap, 0, 2:3], idx[0:cap, 0, 1:2])
                            dve.wait_ge(late_pe[l], 5 * q + 2)
                            v.tensor_copy(x_rowsT[:, 0, 0:4 * cap], bank[0][:, 0:4 * cap])
                            v.tensor_copy(x_rowsT[:, 0, 4 * cap:8 * cap], bank[1][:, 0:4 * cap]).then_inc(late_dve[l], 1)
                            dve.wait_ge(late_act[l], q + 1)
                            dve.wait_ge(late_dve[l], 6 * q + 2)
                            v.scalar_tensor_tensor(out=hid[0:cap, 0, :], in0=act_g[0:cap, 0, :], scalar=wrow[0:cap, 0:1],
                                                   in1=bank[5][0:cap, 0:FF], op0=ALU.mult, op1=ALU.mult).then_inc(late_dve[l], 1)
                            dve.wait_ge(late_pe[l], 5 * q + 4)
                            v.tensor_copy(hidT[:, 0, 0:2 * cap], bank[6][:, 0:2 * cap]).then_inc(late_dve[l], 1)
                            dve.wait_ge(late_pe[l], 5 * q + 5)
                            v.tensor_copy(y_rows[0:cap, 0, 0:512], bank[2][0:cap, :])
                            v.tensor_copy(y_rows[0:cap, 0, 512:1024], bank[3][0:cap, :]).then_inc(late_dve[l], 1)
                            dve.wait_ge(late_out[l], 16 * q + 16)

            for t in main_tiles(DEPTH - 1):
                step_comb(DEPTH - 1, t)

        @block.gpsimd
        def _(pool):
            pool.dma_start(const[:, :], dram["const"]).then_inc(const_in, 16)
            pool.wait_ge(vec_loaded, 16 * N_VEC_LOADS)
            for s, name in enumerate(("ctx", "x")):
                pool.dma_start(x_in[:, 2 * s:2 * s + 2, :], dram[name].rearrange("o (t p) d -> p (o t) d", p=P)).then_inc(x_loaded, 16)
            for l in range(DEPTH):
                if l:
                    pool.wait_ge(small_used, l)
                for name, src in (("qn", "mla_qn_g"), ("kn", "mla_kn_g"), ("kr", "mla_kr_g"), ("lng", "gmlp_ln_g"), ("lnb", "gmlp_ln_b"),
                                  ("bias", "moe_bias")):
                    pool.dma_start(rows(name), dram[src][l].partition_broadcast(P)).then_inc(rows_loaded, 16)
                pool.dma_start(rows("bs"), dram["gmlp_bs"][l].rearrange("g i -> (g i)").partition_broadcast(P)).then_inc(rows_loaded, 16)
                pool.dma_start(rows("dec")[:, 0:4], dram["ret_decay_fwd"][l].partition_broadcast(P)).then_inc(rows_loaded, 16)
                pool.dma_start(rows("dec")[:, 4:8], dram["ret_decay_bwd"][l].partition_broadcast(P)).then_inc(rows_loaded, 16)

                cap = CAP[l]

                def gather(m, j, done):
                    pool.sem_inc(pool_passed, 1)
                    pool.indirect_dma_start(out=x_rows[0:m, j, :], out_offset=None, in_=h2_dram[0:tokens(l), :],
                                            in_offset=bass.IndirectOffsetOnAxis(ap=idx[0:m, j, 0:1], axis=0),
                                            bounds_check=tokens(l) - 1, oob_is_err=False).then_inc(done, 16)

                def scatter(m, j, done):
                    pool.sem_inc(pool_passed, 1)
                    pool.indirect_dma_start(out=y_dram[0:TOPK * tokens(l), :],
                                            out_offset=bass.IndirectOffsetOnAxis(ap=idx[0:m, j, 2:3], axis=0),
                                            in_=y_rows[0:m, j, :], in_offset=None,
                                            bounds_check=TOPK * tokens(l) - 1, oob_is_err=False).then_inc(done, 16)

                def fitted(e, move, j, done):
                    with pool.If(few(pool, e, cap)):
                        move(cap // 2, j, done)
                    with pool.Else():
                        move(cap, j, done)

                pool.wait_ge(moe_ready, l + 1)
                for j in range(2):
                    pool.wait_ge(h2_stored[j], 16 * h2_base(l + 1, j))
                for e in range(2):
                    pool.wait_ge(list_read, l * LISTS + e + 1)
                    gather(cap, e, rows_in[e])

                def three_experts(i):
                    for j in range(BODY):
                        e = i * BODY + j
                        j2 = (j + 2) % 3
                        pool.wait_ge(list_read, l * LISTS + e + 3)
                        fitted(e + 2, gather, j2, rows_in[j2])
                        if j or i is not FIRST:
                            pool.wait_ge(y_act, l * N_EXP + e)
                            pool.wait_ge(y_dve, l * N_EXP + e)
                            fitted(e - 1, scatter, j2, rows_out[j2])

                three_experts(FIRST)
                with pool.Fori(1, N_EXP // BODY) as i:
                    three_experts(i)
                for e in (experts - 1, experts):
                    pool.wait_ge(y_act, l * N_EXP + e + 1)
                    pool.wait_ge(y_dve, l * N_EXP + e + 1)
                    fitted(e, scatter, e % 3, rows_out[e % 3])
                for j in range(3):
                    pool.wait_ge(rows_out[j], 16 * (l + 1) * experts_of[j])
                    pool.wait_ge(rows_in[j], 16 * (l + 1) * lists_of[j])

                most = pool.value_load(maxcnt[0:1, l:l + 1], min_val=0, max_val=T)
                for b in range(1, tokens(l) // cap):
                    with pool.If(most > b * cap):
                        with pool.Fori(0, N_EXP) as e:
                            q = (b - 1) * N_EXP + e
                            pool.wait_ge(late_dve[l], 6 * q + 2)
                            gather(cap, 0, late_in[l])
                            pool.wait_ge(late_dve[l], 6 * q + 6)
                            scatter(cap, 0, late_out[l])
                            pool.wait_ge(late_out[l], 16 * q + 16)

                for i, t in enumerate(main_tiles(l)):
                    if i >= 2:
                        await_full(pool, ("comb", l, main_tiles(l)[i - 2], 1))
                    for k in range(TOPK):
                        at = k * tokens(l) + P * i
                        pool.dma_start(y_parts[i % 2][:, D * k:D * k + D], y_dram[at:at + P, :]).then_inc(y_in[i % 2][k], 16)


_INS = ["x", "c", "ctx", "c_ctx", "ada_w", "ada_b", "norm1_g", "norm2_g", "w_in", "ret_decay_fwd", "ret_decay_bwd",
        "ret_gn_g", "ret_gn_b", "w_br_ret", "mla_qa_g", "mla_w_uq", "mla_kva_g", "mla_w_ukv", "mla_qn_g", "mla_kn_g",
        "mla_kr_g", "w_br_mla", "gmlp_ln_g", "gmlp_ln_b", "gmlp_ws", "gmlp_bs", "w_br_gmlp", "w_out", "moe_router",
        "moe_bias", "moe_w_gate", "moe_w_up", "moe_w_down", "sh_w_gate", "sh_w_up", "sh_w_down"]


def kernel(**inputs):
    import concourse.bacc as _bacc
    from concourse.bass_utils import run_bass_kernel_spmd as _run

    nc = _bacc.Bacc("TRN2", target_bir_lowering=False, num_devices=1)
    arrays, dram = {}, {}
    for name in _INS + ["const"]:
        a = np.ascontiguousarray(shape_constants() if name == "const" else inputs[name])
        arrays[f"in_{name}"] = a
        dram[name] = nc.dram_tensor(f"in_{name}", a.shape, mybir.dt.from_np(a.dtype), kind="ExternalInput").ap()
    out = nc.dram_tensor("out_x", (1, SEQ, D), F32, kind="ExternalOutput").ap()
    backbone(nc, dram, out)
    r = _run(nc, [arrays], core_ids=[0])
    return r.results[0]["out_x"]
```
